# Optimizing a Trainium2 kernel written in Bass

```python
import math
import jax
import jax.numpy as jnp
from jax import lax
import numpy as np

D_MODEL = 1024
BATCH = 1
SEQ = 128
DEPTH = 2
DEC_BATCH = 1
DEC_SEQ = 128
PAST_LEN = 128

GRID_W = 64
ROPE_THETA = 10000.0
NORM_EPS = 1e-6
Q_BLOCK = 128

RET_HEADS = 4
RET_QK_DIM = 64
RET_V_DIM = 64
RET_CHUNK = 128
DIFF_HEADS = 4
DIFF_QK_DIM = 32
DIFF_V_DIM = 2 * DIFF_QK_DIM
MLA_HEADS = 8
MLA_Q_LORA = 256
MLA_KV_LORA = 128
MLA_NOPE_DIM = 64
MLA_ROPE_DIM = 32
MLA_V_DIM = 64

RET_QK_W = RET_HEADS * RET_QK_DIM
RET_V_W = RET_HEADS * RET_V_DIM
DIFF_QK_W = DIFF_HEADS * 2 * DIFF_QK_DIM
DIFF_V_W = DIFF_HEADS * DIFF_V_DIM
MLA_V_W = MLA_HEADS * MLA_V_DIM
MIX_W = RET_V_W + DIFF_V_W + MLA_V_W
IN_SPLITS = (RET_QK_W, RET_QK_W, RET_V_W, RET_V_W, DIFF_QK_W, DIFF_QK_W, DIFF_V_W, MLA_Q_LORA, MLA_KV_LORA, MLA_ROPE_DIM)
IN_W = sum(IN_SPLITS)

N_EXPERTS = 64
TOP_K = 6
N_GROUPS = 8
TOPK_GROUPS = 4
EXPERT_FF = 256
SHARED_FF = 256
ROUTED_SCALE = 2.5
EXPERT_BLOCK = 128

kernel_name = 'hybrid_ret_diff_mla_moe_dit_step'

def rmsnorm(x, gain=None):
    xf = x.astype(jnp.float32)
    y = xf * lax.rsqrt(jnp.mean(xf * xf, axis=-1, keepdims=True) + NORM_EPS)
    if gain is not None:
        y = y * gain.astype(jnp.float32)
    return y.astype(x.dtype)

def swiglu(x, w_gate, w_up, w_down):
    return (jax.nn.silu(x @ w_gate) * (x @ w_up)) @ w_down

def axial_rope_tables(n_tok, dim):
    n_rows = n_tok // GRID_W
    row = jnp.repeat(jnp.arange(n_rows, dtype=jnp.float32), GRID_W)
    col = jnp.tile(jnp.arange(GRID_W, dtype=jnp.float32), n_rows)
    half = dim // 2
    freqs = ROPE_THETA ** (-jnp.arange(0, half, 2, dtype=jnp.float32) / half)
    ar = row[:, None] * freqs[None, :]
    ac = col[:, None] * freqs[None, :]
    ang = jnp.concatenate([ar, ar, ac, ac], axis=-1)
    return jnp.cos(ang), jnp.sin(ang)

def apply_rope(x, cos, sin):
    a, b, c, d = jnp.split(x, 4, axis=-1)
    rot = jnp.concatenate([-b, a, -d, c], axis=-1)
    return x * cos.astype(x.dtype) + rot * sin.astype(x.dtype)

def sweep_queries(fn, qs):
    B, H, L, _ = qs[0].shape
    nb = L // Q_BLOCK
    blocks = tuple(jnp.moveaxis(q.reshape(B, H, nb, Q_BLOCK, q.shape[-1]), 2, 0) for q in qs)
    out = lax.map(lambda t: fn(*t), blocks)
    return jnp.moveaxis(out, 0, 2).reshape(B, H, L, out.shape[-1])

def retention_dir(q, k, v, log_gamma, s0, strict):
    B, H, L, dk = q.shape
    dv = v.shape[-1]
    C = RET_CHUNK
    nc = L // C
    dt = q.dtype
    idx = jnp.arange(C, dtype=jnp.float32)
    dist = idx[:, None] - idx[None, :]
    mask = (dist > 0) if strict else (dist >= 0)
    dmat = jnp.where(mask[None], jnp.exp(dist[None] * log_gamma[:, None, None]), 0.0).astype(dt)
    q_dec = jnp.exp((idx + 1.0)[None, :] * log_gamma[:, None]).astype(dt)
    k_dec = jnp.exp((C - 1.0 - idx)[None, :] * log_gamma[:, None]).astype(dt)
    c_dec = jnp.exp(C * log_gamma).astype(dt)
    qc = q.reshape(B, H, nc, C, dk)
    kc = k.reshape(B, H, nc, C, dk)
    vc = v.reshape(B, H, nc, C, dv)
    scores = jnp.einsum('bhnid,bhnjd->bhnij', qc, kc) * dmat[None, :, None]
    o_inner = jnp.einsum('bhnij,bhnje->bhnie', scores, vc)
    kv = jnp.einsum('bhnjd,bhnje->nbhde', kc * k_dec[None, :, None, :, None], vc)

    def step(s, kv_n):
        return s * c_dec[None, :, None, None] + kv_n, s

    s_fin, s_prev = lax.scan(step, s0.astype(dt), kv)
    o_cross = jnp.einsum('bhnid,nbhde->bhnie', qc * q_dec[None, :, None, :, None], s_prev)
    return (o_inner + o_cross).reshape(B, H, L, dv), s_fin

def retention(q, k, v, log_dec_f, log_dec_b, s0f, s0b):
    lgf = -jnp.exp(log_dec_f.astype(jnp.float32))
    lgb = -jnp.exp(log_dec_b.astype(jnp.float32))
    o_f, s_f = retention_dir(q, k, v, lgf, s0f, False)
    flip = lambda t: jnp.flip(t, axis=2)
    o_b, s_b = retention_dir(flip(q), flip(k), flip(v), lgb, s0b, True)
    return o_f + flip(o_b), s_f, s_b

def diff_attention(q1, q2, k1, k2, v, lam):
    scale = DIFF_QK_DIM ** -0.5

    def block(q1b, q2b):
        s1 = jnp.einsum('bhqd,bhkd->bhqk', q1b, k1).astype(jnp.float32) * scale
        s2 = jnp.einsum('bhqd,bhkd->bhqk', q2b, k2).astype(jnp.float32) * scale
        a = jax.nn.softmax(s1, axis=-1) - lam * jax.nn.softmax(s2, axis=-1)
        return jnp.einsum('bhqk,bhkd->bhqd', a.astype(v.dtype), v)

    return sweep_queries(block, (q1, q2))

def mla_attention(q_nope, q_rope, k_nope, k_rope, v):
    scale = (MLA_NOPE_DIM + MLA_ROPE_DIM) ** -0.5

    def block(qn, qr):
        s = jnp.einsum('bhqd,bhkd->bhqk', qn, k_nope) + jnp.einsum('bhqd,bkd->bhqk', qr, k_rope)
        p = jax.nn.softmax(s.astype(jnp.float32) * scale, axis=-1)
        return jnp.einsum('bhqk,bhkd->bhqd', p.astype(v.dtype), v)

    return sweep_queries(block, (q_nope, q_rope))

def token_mixers(h, lw, lam_init, ropes, ctx):
    B, L, _ = h.shape
    offsets = np.cumsum(IN_SPLITS)[:-1].tolist()
    rq, rk, rv, rg, dq, dk, dv, cq, ckv, kpe = jnp.split(h @ lw['w_in'], offsets, axis=-1)

    def heads(t, n):
        return t.reshape(B, L, n, -1).transpose(0, 2, 1, 3)

    rq = heads(rq, RET_HEADS)
    rk = heads(rk, RET_HEADS) * (RET_QK_DIM ** -0.5)
    rv = heads(rv, RET_HEADS)
    if ctx is None:
        s0f = jnp.zeros((B, RET_HEADS, RET_QK_DIM, RET_V_DIM), h.dtype)
        s0b = s0f
    else:
        s0f, s0b = ctx[4], ctx[5]
    o_r, s_f, s_b = retention(rq, rk, rv, lw['ret_decay_fwd'], lw['ret_decay_bwd'], s0f, s0b)
    ret_out = rmsnorm(o_r).transpose(0, 2, 1, 3).reshape(B, L, RET_V_W) * jax.nn.silu(rg)

    dq = dq.reshape(B, L, DIFF_HEADS, 2, DIFF_QK_DIM).transpose(0, 2, 1, 3, 4)
    dk = dk.reshape(B, L, DIFF_HEADS, 2, DIFF_QK_DIM).transpose(0, 2, 1, 3, 4)
    dv = heads(dv, DIFF_HEADS)
    q1, q2, k1, k2 = dq[..., 0, :], dq[..., 1, :], dk[..., 0, :], dk[..., 1, :]
    if ropes is not None:
        cos_d, sin_d = ropes[0]
        q1, q2, k1, k2 = (apply_rope(t, cos_d, sin_d) for t in (q1, q2, k1, k2))
    diff_k = jnp.concatenate([k1, k2], axis=-1)
    if ctx is None:
        diff_k_all, diff_v_all = diff_k, dv
    else:
        diff_k_all = jnp.concatenate([ctx[0], diff_k], axis=2)
        diff_v_all = jnp.concatenate([ctx[1], dv], axis=2)
    lq1, lk1, lq2, lk2 = lw['diff_lambda'].astype(jnp.float32)
    lam = jnp.exp(jnp.sum(lq1 * lk1)) - jnp.exp(jnp.sum(lq2 * lk2)) + lam_init
    o_d = diff_attention(q1, q2, diff_k_all[..., :DIFF_QK_DIM], diff_k_all[..., DIFF_QK_DIM:], diff_v_all, lam)
    diff_out = (rmsnorm(o_d, lw['diff_subln']) * (1.0 - lam_init)).transpose(0, 2, 1, 3).reshape(B, L, DIFF_V_W)

    qm = heads(rmsnorm(cq, lw['mla_q_norm']) @ lw['mla_w_uq'], MLA_HEADS)
    q_nope, q_rope = qm[..., :MLA_NOPE_DIM], qm[..., MLA_NOPE_DIM:]
    ckv = rmsnorm(ckv, lw['mla_kv_norm'])
    if ropes is not None:
        cos_m, sin_m = ropes[1]
        q_rope = apply_rope(q_rope, cos_m, sin_m)
        kpe = apply_rope(kpe, cos_m, sin_m)
    if ctx is None:
        ckv_all, kpe_all = ckv, kpe
    else:
        ckv_all = jnp.concatenate([ctx[2], ckv], axis=1)
        kpe_all = jnp.concatenate([ctx[3], kpe], axis=1)
    S = ckv_all.shape[1]
    kv = (ckv_all @ lw['mla_w_ukv']).reshape(B, S, MLA_HEADS, MLA_NOPE_DIM + MLA_V_DIM).transpose(0, 2, 1, 3)
    k_nope, v_m = kv[..., :MLA_NOPE_DIM], kv[..., MLA_NOPE_DIM:]
    o_m = mla_attention(q_nope, q_rope, k_nope, kpe_all, v_m)
    mla_out = o_m.transpose(0, 2, 1, 3).reshape(B, L, MLA_V_W)

    mix = jnp.concatenate([ret_out, diff_out, mla_out], axis=-1)
    new_ctx = (diff_k, dv, ckv, kpe, s_f, s_b) if ctx is None else None
    return mix, new_ctx

def moe_dispatch(x, eidx, gates, w_gate, w_up, w_down):
    T, D = x.shape
    TK = T * TOP_K
    flat_e = eidx.reshape(-1)
    flat_tok = jnp.repeat(jnp.arange(T, dtype=jnp.int32), TOP_K)
    flat_g = gates.reshape(-1)
    order = jnp.argsort(flat_e)
    se, stok, sg = flat_e[order], flat_tok[order], flat_g[order]
    counts = jnp.zeros((N_EXPERTS,), jnp.int32).at[flat_e].add(1)
    padded = (counts + EXPERT_BLOCK - 1) // EXPERT_BLOCK * EXPERT_BLOCK
    start = jnp.cumsum(counts) - counts
    pend = jnp.cumsum(padded)
    pstart = pend - padded
    dest = pstart[se] + jnp.arange(TK, dtype=jnp.int32) - start[se]
    P = TK + N_EXPERTS * EXPERT_BLOCK
    nblk = P // EXPERT_BLOCK
    buf_tok = jnp.full((P,), T, jnp.int32).at[dest].set(stok)
    buf_g = jnp.zeros((P,), x.dtype).at[dest].set(sg.astype(x.dtype))
    blk_e = jnp.minimum(jnp.searchsorted(pend, jnp.arange(nblk, dtype=jnp.int32) * EXPERT_BLOCK, side='right'), N_EXPERTS - 1)
    xb = jnp.concatenate([x, jnp.zeros((1, D), x.dtype)], axis=0)[buf_tok].reshape(nblk, EXPERT_BLOCK, D)

    def run(args):
        xe, e = args
        return swiglu(xe, w_gate[e], w_up[e], w_down[e])

    yb = lax.map(run, (xb, blk_e)).reshape(P, D)
    return jax.ops.segment_sum(yb * buf_g[:, None], buf_tok, num_segments=T + 1)[:T]

def moe_ffn(h, lw):
    B, L, D = h.shape
    T = B * L
    x = h.reshape(T, D)
    scores = jax.nn.sigmoid((x @ lw['router_w']).astype(jnp.float32))
    sel = scores + lw['router_bias'].astype(jnp.float32)
    grp_score = lax.top_k(sel.reshape(T, N_GROUPS, N_EXPERTS // N_GROUPS), 2)[0].sum(-1)
    _, gidx = lax.top_k(grp_score, TOPK_GROUPS)
    gmask = jnp.any(jnp.arange(N_GROUPS)[None, None, :] == gidx[:, :, None], axis=1)
    sel = jnp.where(jnp.repeat(gmask, N_EXPERTS // N_GROUPS, axis=1), sel, -jnp.inf)
    _, eidx = lax.top_k(sel, TOP_K)
    gates = jnp.take_along_axis(scores, eidx, axis=-1)
    gates = gates / jnp.sum(gates, axis=-1, keepdims=True) * ROUTED_SCALE
    routed = moe_dispatch(x, eidx, gates, lw['exp_w_gate'], lw['exp_w_up'], lw['exp_w_down'])
    shared = swiglu(x, lw['sh_w_gate'], lw['sh_w_up'], lw['sh_w_down'])
    return (routed + shared).reshape(B, L, D)

def trunk_layer(x, cond, lw, lam_init, ropes, ctx):
    mod = (jax.nn.silu(cond) @ lw['w_ada'] + lw['b_ada'])[:, None, :]
    shift1, scale1, gate1, shift2, scale2, gate2 = jnp.split(mod, 6, axis=-1)
    h = rmsnorm(x, lw['norm_mix']) * (1 + scale1) + shift1
    mix, new_ctx = token_mixers(h, lw, lam_init, ropes, ctx)
    x = x + gate1 * (mix @ lw['w_out'])
    h = rmsnorm(x, lw['norm_ffn']) * (1 + scale2) + shift2
    x = x + gate2 * moe_ffn(h, lw)
    return x, new_ctx

def setup_inputs(seed: int = 0) -> dict:
    key = jax.random.key(seed)
    keys = iter(jax.random.split(key, 40))

    def nrm(shape, s):
        return jax.random.normal(next(keys), shape, jnp.float32) * s

    D = D_MODEL
    ret_base = -(5.0 + jnp.arange(RET_HEADS, dtype=jnp.float32)) * math.log(2.0)
    return {
        'x_prompt': nrm((BATCH, SEQ, D), 1.0),
        'x_sample': nrm((DEC_BATCH, DEC_SEQ, D), 1.0),
        'cache_diff_k': nrm((DEC_BATCH, DEPTH, DIFF_HEADS, PAST_LEN, 2 * DIFF_QK_DIM), 1.0),
        'cache_diff_v': nrm((DEC_BATCH, DEPTH, DIFF_HEADS, PAST_LEN, DIFF_V_DIM), 1.0),
        'cache_mla_ckv': nrm((DEC_BATCH, DEPTH, PAST_LEN, MLA_KV_LORA), 1.0),
        'cache_mla_kpe': nrm((DEC_BATCH, DEPTH, PAST_LEN, MLA_ROPE_DIM), 1.0),
        'state_ret_fwd': nrm((DEC_BATCH, DEPTH, RET_HEADS, RET_QK_DIM, RET_V_DIM), 1.0),
        'state_ret_bwd': nrm((DEC_BATCH, DEPTH, RET_HEADS, RET_QK_DIM, RET_V_DIM), 1.0),
        'c': nrm((DEC_BATCH, D), 1.0),
        'c_ctx': nrm((D,), 1.0),
        'w_ada': nrm((DEPTH, D, 6 * D), 0.5 * D ** -0.5),
        'b_ada': nrm((DEPTH, 6 * D), 0.01),
        'norm_mix': 1.0 + nrm((DEPTH, D), 0.02),
        'norm_ffn': 1.0 + nrm((DEPTH, D), 0.02),
        'norm_final': 1.0 + nrm((D,), 0.02),
        'w_in': nrm((DEPTH, D, IN_W), D ** -0.5),
        'ret_decay_fwd': ret_base[None, :] + nrm((DEPTH, RET_HEADS), 0.1),
        'ret_decay_bwd': ret_base[None, :] + nrm((DEPTH, RET_HEADS), 0.1),
        'diff_lambda': nrm((DEPTH, 4, DIFF_QK_DIM), 0.1),
        'diff_subln': 1.0 + nrm((DEPTH, DIFF_V_DIM), 0.02),
        'mla_q_norm': 1.0 + nrm((DEPTH, MLA_Q_LORA), 0.02),
        'mla_w_uq': nrm((DEPTH, MLA_Q_LORA, MLA_HEADS * (MLA_NOPE_DIM + MLA_ROPE_DIM)), MLA_Q_LORA ** -0.5),
        'mla_kv_norm': 1.0 + nrm((DEPTH, MLA_KV_LORA), 0.02),
        'mla_w_ukv': nrm((DEPTH, MLA_KV_LORA, MLA_HEADS * (MLA_NOPE_DIM + MLA_V_DIM)), MLA_KV_LORA ** -0.5),
        'w_out': nrm((DEPTH, MIX_W, D), MIX_W ** -0.5),
        'router_w': nrm((DEPTH, D, N_EXPERTS), D ** -0.5),
        'router_bias': nrm((DEPTH, N_EXPERTS), 0.01),
        'exp_w_gate': nrm((DEPTH, N_EXPERTS, D, EXPERT_FF), D ** -0.5),
        'exp_w_up': nrm((DEPTH, N_EXPERTS, D, EXPERT_FF), D ** -0.5),
        'exp_w_down': nrm((DEPTH, N_EXPERTS, EXPERT_FF, D), EXPERT_FF ** -0.5),
        'sh_w_gate': nrm((DEPTH, D, SHARED_FF), D ** -0.5),
        'sh_w_up': nrm((DEPTH, D, SHARED_FF), D ** -0.5),
        'sh_w_down': nrm((DEPTH, SHARED_FF, D), SHARED_FF ** -0.5),
    }

def reference(x_prompt, x_sample, cache_diff_k, cache_diff_v, cache_mla_ckv, cache_mla_kpe, state_ret_fwd, state_ret_bwd, c, c_ctx, w_ada, b_ada, norm_mix, norm_ffn, norm_final, w_in, ret_decay_fwd, ret_decay_bwd, diff_lambda, diff_subln, mla_q_norm, mla_w_uq, mla_kv_norm, mla_w_ukv, w_out, router_w, router_bias, exp_w_gate, exp_w_up, exp_w_down, sh_w_gate, sh_w_up, sh_w_down):
    n_lat = x_sample.shape[1]
    rope_d = axial_rope_tables(n_lat, DIFF_QK_DIM)
    rope_m = axial_rope_tables(n_lat, MLA_ROPE_DIM)
    xp, xs = x_prompt, x_sample
    ctx_states = []
    for l in range(DEPTH):
        lw = {
            'w_ada': w_ada[l], 'b_ada': b_ada[l], 'norm_mix': norm_mix[l], 'norm_ffn': norm_ffn[l],
            'w_in': w_in[l], 'ret_decay_fwd': ret_decay_fwd[l], 'ret_decay_bwd': ret_decay_bwd[l],
            'diff_lambda': diff_lambda[l], 'diff_subln': diff_subln[l],
            'mla_q_norm': mla_q_norm[l], 'mla_w_uq': mla_w_uq[l], 'mla_kv_norm': mla_kv_norm[l], 'mla_w_ukv': mla_w_ukv[l],
            'w_out': w_out[l], 'router_w': router_w[l], 'router_bias': router_bias[l],
            'exp_w_gate': exp_w_gate[l], 'exp_w_up': exp_w_up[l], 'exp_w_down': exp_w_down[l],
            'sh_w_gate': sh_w_gate[l], 'sh_w_up': sh_w_up[l], 'sh_w_down': sh_w_down[l],
        }
        lam_init = 0.8 - 0.6 * math.exp(-0.3 * l)
        xp, st = trunk_layer(xp, c_ctx[None, :], lw, lam_init, None, None)
        ctx_states.append(st)
        cache_l = (cache_diff_k[:, l], cache_diff_v[:, l], cache_mla_ckv[:, l], cache_mla_kpe[:, l], state_ret_fwd[:, l], state_ret_bwd[:, l])
        xs, _ = trunk_layer(xs, c, lw, lam_init, (rope_d, rope_m), cache_l)
    y_prompt = rmsnorm(xp, norm_final)
    y_sample = rmsnorm(xs, norm_final)
    new_diff_k = jnp.stack([s[0] for s in ctx_states], axis=1)
    new_diff_v = jnp.stack([s[1] for s in ctx_states], axis=1)
    new_mla_ckv = jnp.stack([s[2] for s in ctx_states], axis=1)
    new_mla_kpe = jnp.stack([s[3] for s in ctx_states], axis=1)
    new_ret_fwd = jnp.stack([s[4] for s in ctx_states], axis=1)
    new_ret_bwd = jnp.stack([s[5] for s in ctx_states], axis=1)
    return (y_prompt, y_sample, new_diff_k, new_diff_v, new_mla_ckv, new_mla_kpe, new_ret_fwd, new_ret_bwd)


_drawn_inputs = setup_inputs


def setup_inputs(seed=0):
    import zlib

    import numpy as np

    out = dict(_drawn_inputs(seed))
    spreads = {}
    factors = {'norm_final': 2.858, 'mla_q_norm': 5.228, 'mla_kv_norm': 2.952}
    for name, (base, spread) in spreads.items():
        noise = np.random.default_rng([zlib.crc32(name.encode()), seed]).standard_normal(out[name].shape)
        drawn = base * np.exp(spread * noise) if base else spread * noise
        out[name] = jnp.asarray(drawn.astype(out[name].dtype))
    for name, factor in factors.items():
        out[name] = (out[name] * factor).astype(out[name].dtype)
    return out
```

```python
import math
from contextlib import ExitStack

import numpy as np

import concourse.bass as bass
from concourse import mybir

F32 = mybir.dt.float32
BF16 = mybir.dt.bfloat16
I32 = mybir.dt.int32
U32 = mybir.dt.uint32
ALU = mybir.AluOpType
ACT = mybir.ActivationFunctionType
AX = mybir.AxisListType

P = 128
D = 1024
NC_ = D // P
G = 2
T = G * P
DEPTH = 2
EPS = 1e-6
GRID_W = 64
ROPE_THETA = 10000.0

RET_H, RET_D = 4, 64
DIF_H, DIF_D, DIF_V = 4, 32, 64
MLA_H, MLA_N, MLA_R, MLA_V = 8, 64, 32, 64
MLA_QK = MLA_N + MLA_R
Q_LORA, KV_LORA = 256, 128
IN_W = 2208

E = 64
GROUPS = 8
TOP_G, TOP_K = 4, 6
FF = 256
ROUTED_SCALE = 2.5
CAP = 64
PAIRS = E // 2

CONSTS = ["ident", "ones", "rot_d", "rot_m", "cos_d", "sin_d", "cos_m", "sin_m", "fwd", "bwd", "before", "iota", "cols"]
CO = {n: P * i for i, n in enumerate(CONSTS)}
COL = {"i+1": 0, "C-i": 1, "C-1-i": 2, "i": 3, "eps": 4, "sel": 5}


def shape_constants():
    a = np.zeros((P, len(CONSTS), P), np.float32)
    i = np.arange(P)
    a[:, 0] = np.eye(P)
    a[:, 1] = 1.0

    def tables(n_heads, lead, dim):
        freqs = ROPE_THETA ** (-np.arange(0, dim // 2, 2, dtype=np.float32) / (dim // 2))
        ar = (i // GRID_W)[:, None] * freqs[None, :].astype(np.float32)
        ac = (i % GRID_W)[:, None] * freqs[None, :].astype(np.float32)
        ang = np.concatenate([ar, ar, ac, ac], axis=-1).astype(np.float32)
        rot = np.zeros((P, P), np.float32)
        cos, sin = np.zeros((P, P), np.float32), np.zeros((P, P), np.float32)
        cos[:lead], q = 1.0, dim // 4
        for h in range(n_heads):
            o = lead + h * dim
            cos[o:o + dim], sin[o:o + dim] = np.cos(ang).T, np.sin(ang).T
            for k in range(q):
                rot[o + q + k, o + k] = -1.0
                rot[o + k, o + q + k] = 1.0
                rot[o + 3 * q + k, o + 2 * q + k] = -1.0
                rot[o + 2 * q + k, o + 3 * q + k] = 1.0
        return rot, cos, sin

    a[:, 2], a[:, 4], a[:, 5] = tables(P // DIF_D, 0, DIF_D)
    a[:, 3], a[:, 6], a[:, 7] = tables(1, MLA_N, MLA_R)
    a[:, 8] = np.maximum(i[None, :] - i[:, None], 0)
    a[:, 9] = np.maximum(i[:, None] - i[None, :], 0)
    a[:, 10] = i[:, None] < i[None, :]
    a[:, 11] = i[None, :]
    a[:, 12, 0], a[:, 12, 1], a[:, 12, 2], a[:, 12, 3], a[:, 12, 4] = i + 1, P - i, P - 1 - i, i, EPS
    a[:, 12, 5], a[:, 12, 6] = i % 32 == 0, i % 32 == 1
    return a.reshape(P, len(CONSTS) * P)


def stream_items():
    out = []
    for l in range(DEPTH):
        if l == 0:
            out += [("ada", 0, n) for n in range(4)]
        rest = [("ada", 0, n) for n in range(4, 12)] + [("ada", 1, n) for n in range(12)] if l == 0 else []
        for k in range(5):
            out.append(("w_in", l, k))
            out += rest[:2]
            rest = rest[2:]
        out += [("mla", l, 0)] + rest
        out += [("w_out", l, 0), ("w_out", l, 1), ("router", l, 0), ("shared", l, 0)]
        out += [("expert", l, e) for e in range(E)]
    return out


def trunk(nc, t, out):
    ctx = ExitStack()
    with ctx:
        def sb(name, shape, dt=F32):
            return ctx.enter_context(nc.sbuf_tensor(name, shape, dt))

        def sem(name):
            return ctx.enter_context(nc.semaphore(name))

        RING = 4
        gu = sb("gu", [P, RING, 2 * NC_ * FF])
        dn = sb("dn", [P, RING, 2, D])
        cst = sb("cst", [P, len(CONSTS) * P])
        xT = sb("xT", [P, NC_, T])
        hT = sb("hT", [P, NC_, T])
        xn = sb("xn", [P, NC_, T])
        rows = sb("rows", [P, DEPTH, 64 + 64 + KV_LORA + Q_LORA + 128 + 8])
        gains = sb("gains", [P, 4, NC_])
        b_ada = sb("b_ada", [P, DEPTH, 6, NC_])
        cond = sb("cond", [P, G, NC_])
        condw = sb("condw", [P, NC_, 32])
        mod = sb("mod", [P, DEPTH, 6, NC_, G])
        amp = sb("amp", [P, 2, NC_, G])
        rada = sb("rada", [P, 512])
        s0 = sb("s0", [P, DEPTH, 2, 2, RET_D])
        ck = sb("ck", [P, DEPTH, DIF_H, 2 * DIF_D])
        cv = sb("cv", [P, DEPTH, DIF_H, DIF_V])
        cl = sb("cl", [P, DEPTH, KV_LORA])
        cr = sb("cr", [P, DEPTH, MLA_QK])
        ckT = sb("ckT", [P, DEPTH, 2, P])
        clT = sb("clT", [P, DEPTH, P])
        crT = sb("crT", [MLA_QK, DEPTH, P])
        dec = sb("dec", [P, DEPTH, 8])
        decv = sb("decv", [P, 4, 4])
        nlam = sb("nlam", [P, DEPTH])
        small = sb("small", [P, 512])
        arena = sb("arena", [P, 14656])
        flag_i = sb("flag_i", [1, DEPTH], I32)

        at = [0]

        def carve(n, name=None):
            at[0] += n
            assert at[0] <= 14656, at[0]
            return arena[:, at[0] - n:at[0]]

        def split(ap, *sizes):
            o, parts = 0, []
            for n in sizes:
                parts.append(ap[:, o:o + n])
                o += n
            return parts

        keys = carve(MLA_H * 3 * P)
        kmT = keys.rearrange("p (h k t) -> p h k t", h=MLA_H, k=3)
        a_q, a_k, a_s, a_cqn, a_cqT = split(keys, 2 * T, 2 * T, 8 * P, G * Q_LORA, 2 * T)
        qT = a_q.rearrange("p (c t) -> p c t", c=2)
        kT = a_k.rearrange("p (c t) -> p c t", c=2)
        sT = a_s.rearrange("p (b g m t) -> p b g m t", b=2, g=G, m=2)
        cqn = a_cqn.rearrange("p (g n) -> p g n", g=G)
        cqT = a_cqT.rearrange("p (c t) -> p c t", c=2)
        values = carve(3 * 512)
        vm = values.rearrange("p (k n) -> p k n", k=3)
        a_v, a_x, a_kd = split(values, G * 256, 4 * P, 2 * 256)
        v_tok = a_v.rearrange("p (g n) -> p g n", g=G)
        cross = a_x.rearrange("p (h d e) -> p h d e", h=4, d=2)
        kdec = a_kd.rearrange("p (d n) -> p d n", d=2)
        rgate = carve(G * 256).rearrange("p (g n) -> p g n", g=G)
        dqT = carve(2 * T).rearrange("p (c t) -> p c t", c=2)
        dkT = carve(2 * 3 * P).rearrange("p (c k t) -> p c k t", c=2, k=3)
        dv_tok = carve(G * 256).rearrange("p (g n) -> p g n", g=G)
        ckvn = carve(G * KV_LORA).rearrange("p (g n) -> p g n", g=G)
        kpe = carve(G * MLA_QK).rearrange("p (g n) -> p g n", g=G)
        ckvT = carve(3 * P).rearrange("p (k t) -> p k t", k=3)
        kpeT = carve(3 * P).rearrange("p (k t) -> p k t", k=3)
        qmT = carve(MLA_H * T).rearrange("p (h t) -> p h t", h=MLA_H)
        kv_out = carve(2 * 4 * RET_D).rearrange("p (d h e) -> p d h e", d=2, h=4)
        dk_tok = carve(256)
        mix = carve(G * D).rearrange("p (g n) -> p g n", g=G)
        work = carve(512)
        rtmp = carve(2 * 512).rearrange("p (a n) -> p a n", a=2)
        dmat = rtmp[:, 1].rearrange("p (b m t) -> p b m t", b=2, m=2)
        prob = xn[:, :, :].rearrange("p c t -> p (c t)").rearrange("p (m k) -> p m k", m=8)
        probT = hT[:, :, :].rearrange("p c t -> p (c t)").rearrange("p (m k t) -> p m k t", m=8, k=2)
        mixT = xn
        at[0] = 0
        h3 = carve(G * 3 * D // 2).bitcast(BF16).rearrange("p (g s c t) -> p g s c t", g=G, s=3, c=NC_)
        rem = carve(2 * D).rearrange("p (a n) -> p a n", a=2)
        xg = carve(NC_ * P).rearrange("p (c t) -> p c t", c=NC_)
        sact = carve(256)
        hh = carve(256)
        hs = carve(512)
        yy = carve(D)
        shs = carve(2 * T).rearrange("p (j t) -> p j t", j=2)
        shh = carve(2 * T).rearrange("p (j t) -> p j t", j=2)
        score = carve(G * E).rearrange("p (g e) -> p g e", g=G)
        selv = carve(G * E).rearrange("p (g e) -> p g e", g=G)
        gtop = carve(G * 64).rearrange("p (g a b) -> p g a b", g=G, a=GROUPS)
        gsc = carve(G * 8).rearrange("p (g a) -> p g a", g=G)
        top8 = carve(G * 8).rearrange("p (g a) -> p g a", g=G)
        idx8 = carve(G * 8).bitcast(U32).rearrange("p (g a) -> p g a", g=G)
        idxf = carve(G * 8).rearrange("p (g a) -> p g a", g=G)
        hit = carve(G * E * 8)
        gmask = carve(G * 8).rearrange("p (g a) -> p g a", g=G)
        mask = carve(G * E).rearrange("p (g e) -> p g e", g=G)
        gsum = carve(8)
        pos = carve(G * (E + 4)).rearrange("p (e g) -> p e g", g=G)
        wgt = carve(G * (E + 4)).rearrange("p (e g) -> p e g", g=G)
        onehot = carve(G * P // 2).bitcast(BF16).rearrange("p (g s) -> p g s", g=G)
        gated = carve(G * P).rearrange("p (g s) -> p g s", g=G)
        fl = carve(8)

        PS = ctx.enter_context(nc.psum_tensor("PS", [P, 8, 512], F32))

        def C(name, w=P, parts=P):
            return cst[0:parts, CO[name]:CO[name] + w]

        def col(name, w=1):
            o = CO["cols"] + COL[name]
            return cst[:, o:o + w]

        ident = C("ident")

        def r_bias(l):
            return rows[:, l, 0:64]

        def r_subln(l):
            return rows[:, l, 64:128]

        def r_kvn(l):
            return rows[:, l, 128:128 + KV_LORA]

        def r_qn(l):
            return rows[:, l, 256:256 + Q_LORA]

        def r_lam(l):
            return rows[:, l, 512:640]

        def r_dec(l):
            return rows[:, l, 640:648]

        def bc(ap, axis, n):
            u = ap.unsqueeze(axis)
            s = list(u.shape)
            s[axis] = n
            return u.to_broadcast(s)

        names = """const_in x_in mod_in small_in gain_in weights_used down_free store_done
            cond_ready turned_x xT_a xT_d setup_evict_a setup_evict_d caches_placed
            ada_r ada_sel ada_mod
            sq_ready ss_ready std_ready xn_ready h_a h_d amp_ready
            proj q_ready k_ready rg_exp rv_ready dq_ready dk_ready cq_sq cqn_ready ckv_sq ckvn_ready
            decay_rate decay_args decays_ready lam_arg lam_exp
            t_cq t_ckv t_kpe cqT_ready ckvT_ready kpeT_ready
            ret_s sT_ready ret_x cross_ready t_k ktok_ready d_rot d_roped uq qm_ready
            ret_o ret_sum ret_std kv_p kv_ready kpe_rot kpe_roped q_rot q_roped
            ukv_k km_a km_d ukv_v vm_ready
            s_ready nb_ready exp_done pt_turned pt_even pt_odd pv_done o_done dif_sum dif_std
            t_mix mixT_a mixT_d wo_done x_bank
            sig_exp routed rank_done pos_ready flag_ready t_h part_a part_d sh_silu sh_h
            zeroed sel_ready gated_ready gathered xg_a xg_b silu_ready hid_ready turned hs_ready down_a y_a y_b combined
            turned_y y_sq y_ms y_std y_done act_own dve_own""".split()
        S = {n: sem(n) for n in names}
        gu_loaded = [sem(f"gu_loaded{j}") for j in range(RING)]
        dn_loaded = [sem(f"dn_loaded{j}") for j in range(RING)]
        ov = [{n: sem(f"over{l}_{n}") for n in
               "w sel gath xg up silu hid turn hs down y comb step".split()} for l in range(DEPTH)]

        items = stream_items()
        number = {it: n for n, it in enumerate(items)}
        first_expert = [number[("expert", l, 0)] for l in range(DEPTH)]

        def gu_slot(l, e4):
            return (first_expert[l] + e4) % RING
        loaded_at, cum, dcum, dloaded = {}, [0] * RING, [0] * RING, {}
        for n, it in enumerate(items):
            cum[n % RING] += 32 if it[0] in ("shared", "expert", "mla") else 16
            loaded_at[it] = cum[n % RING]
            if it[0] == "shared":
                dcum[RING - 1] += 16
                dloaded[it] = dcum[RING - 1]
            if it[0] == "expert":
                dcum[it[2] % RING] += 16
                dloaded[it] = dcum[it[2] % RING]
        UQ, UKV = 2 * MLA_H * MLA_QK, MLA_H * (MLA_N + MLA_V)
        DN_PER = E + 1
        DN0 = 3

        def w_ada_view(it):
            _, l, q = it
            return t["w_ada"][l].rearrange("(p c) n -> p c n", c=NC_)[:, :, q * 512:(q + 1) * 512]

        items_ada = [it for it in items if it[0] == "ada"]
        stores_in_layer = 6
        small_total = 16 * (4 + 4 * DEPTH + DEPTH * 7)
        mod_total = 16 * 3 * DEPTH

        def ada_at(l, k):
            if l > 0:
                return []
            return [[4, 5], [6, 7], [8, 9], [10, 11], [12, 13], [14, 15], [16, 17, 18], [19, 20], [21, 22, 23], []][k]

        def ada_here(step, l, k):
            for n in ada_at(l, k):
                step(n)

        def projected(eng, l, k, part):
            if part == 0:
                eng.wait_ge(S["proj"], 4 * l + k + 1)
            else:
                eng.wait_ge(S["weights_used"], number[("w_in", l, k)] + 1)

        def x_banks(k):
            return 4 * k

        def k_bank(h):
            return (3, 4, 5, 0, 1, 2, 3, 4)[h]

        def wo_bank(c):
            return (4, 5, 0, 1)[c // 2]

        def pt_before(U):
            return 12 * (U // 4) + (0, 2, 6, 8)[U % 4]

        def half_before(U):
            return pt_before(U) // 2

        def pt_view(b, nk):
            if nk == 2:
                return probT[:, 2 * b:2 * b + 2].rearrange("p m k t -> p (m k) t")
            return probT[:, 4 * b:4 * b + 4, 0, :]

        def pt_tile(m, k, nk):
            return probT[:, m, k, :]

        def chain(eng, own):
            count = [0]

            def link(ins):
                count[0] += 1
                ins.then_inc(own, 1)
                eng.wait_ge(own, count[0])

            told = {}

            def settle(name):
                told[name] = told.get(name, 0) + 1
                eng.wait_ge(S[name], told[name])
            return link, settle

        def over_flag(eng, l):
            eng.wait_ge(S["flag_ready"], l + 1)
            return eng.value_load(flag_i[0:1, l:l + 1], min_val=0, max_val=1)

        BEFORE = 1
        OW = 2

        def over_loads(sp, l):
            o = ov[l]
            with sp.If(over_flag(sp, l) > 0):
                sp.wait_ge(S["weights_used"], first_expert[l] + E)
                sp.wait_ge(S["down_free"], DN0 + DN_PER * (l + 1))
                with sp.Fori(0, E) as e:
                    sp.wait_ge(o["comb"], e * OW + BEFORE)
                    for half, name in enumerate(("gate", "up")):
                        sp.dma_start(gu[:, 0, half * NC_ * FF:(half + 1) * NC_ * FF],
                                     t[f"exp_w_{name}"][l, bass.ds(e, 1)].rearrange("e (p c) n -> (e p) (c n)", c=NC_)
                                     ).then_inc(o["w"], 16)
                    sp.dma_start(dn[:, 0].rearrange("p j n -> p (j n)"),
                                 t["exp_w_down"][l, bass.ds(e, 1)].rearrange("e (p j) n -> (e p) (j n)", j=2)
                                 ).then_inc(o["w"], 16)
                sp.wait_ge(o["comb"], E * OW + BEFORE)

        block = ctx.enter_context(nc.Block())

        @block.sync
        def _(sp):
            def load_expert_gu(slot, l, e, shared=False):
                for half, name in enumerate(("gate", "up")):
                    if shared:
                        src = t[f"sh_w_{name}"][l].rearrange("(p c) n -> p (c n)", c=NC_)
                    else:
                        src = t[f"exp_w_{name}"][l, e].rearrange("e (p c) n -> (e p) (c n)", c=NC_)
                    dst = gu[:, slot, half * NC_ * FF:(half + 1) * NC_ * FF]
                    sp.dma_start(dst, src).then_inc(gu_loaded[slot], 16)

            def load_expert_dn(slot, l, e, shared=False):
                if shared:
                    src = t["sh_w_down"][l].rearrange("(p j) n -> p (j n)", j=2)
                else:
                    src = t["exp_w_down"][l, e].rearrange("e (p j) n -> (e p) (j n)", j=2)
                sp.dma_start(dn[:, slot].rearrange("p j n -> p (j n)"), src).then_inc(dn_loaded[slot], 16)

            x_tok = arena[:, 0:G * D].rearrange("p (g n) -> p g n", g=G)
            sp.dma_start(x_tok[:, 0], t["x_prompt"][0]).then_inc(S["const_in"], 16)
            sp.dma_start(x_tok[:, 1], t["x_sample"][0]).then_inc(S["const_in"], 16)
            sp.dma_start(cst[:, :], t["shape_consts"]).then_inc(S["const_in"], 16)
            for l in range(DEPTH):
                for it in items:
                    n = number[it]
                    if it[1] != l and it[0] != "ada" or it[0] == "expert" or (l > 0 and it[0] == "ada"):
                        continue
                    if n >= RING:
                        sp.wait_ge(S["weights_used"], n - RING + 1)
                    slot = n % RING
                    if it[0] == "ada":
                        src = w_ada_view(it)
                        dst = gu[:, slot, :].rearrange("p (c n) -> p c n", c=NC_)
                        sp.dma_start(dst, src).then_inc(gu_loaded[slot], 16)
                    elif it[0] == "w_in":
                        w = min(512, IN_W - 512 * it[2])
                        src = t["w_in"][l].rearrange("(p c) n -> p c n", c=NC_)[:, :, 512 * it[2]:512 * it[2] + w]
                        dst = gu[:, slot, 0:NC_ * w].rearrange("p (c n) -> p c n", c=NC_)
                        sp.dma_start(dst, src).then_inc(gu_loaded[slot], 16)
                    elif it[0] == "w_out":
                        src = t["w_out"][l, 512 * it[2]:512 * it[2] + 512].rearrange("(k p) n -> p k n", p=P)
                        dst = gu[:, slot, :].rearrange("p (k n) -> p k n", k=4)
                        sp.dma_start(dst, src).then_inc(gu_loaded[slot], 16)
                    elif it[0] == "mla":
                        sp.dma_start(gu[:, slot, 0:UQ].rearrange("p (k n) -> p k n", k=2),
                                     t["mla_w_uq"][l].rearrange("(k p) n -> p k n", p=P)).then_inc(gu_loaded[slot], 16)
                        sp.dma_start(gu[:, slot, UQ:UQ + UKV], t["mla_w_ukv"][l]).then_inc(gu_loaded[slot], 16)
                    elif it[0] == "router":
                        sp.dma_start(gu[:, slot, 0:NC_ * E], t["router_w"][l].rearrange("(p c) n -> p (c n)", c=NC_)
                                     ).then_inc(gu_loaded[slot], 16)
                    else:
                        load_expert_gu(slot, l, 0, shared=True)
                        if l > 0:
                            sp.wait_ge(S["down_free"], DN0 + DN_PER * l)
                        load_expert_dn(RING - 1, l, 0, shared=True)
                with sp.Fori(0, E // RING) as m:
                    for q in range(2):
                        for h in range(2):
                            e4 = 2 * q + h
                            sp.wait_ge(S["weights_used"], m * RING + (first_expert[l] + e4 - RING + 1))
                            load_expert_gu(gu_slot(l, e4), l, bass.ds(m * RING + e4, 1))
                        for h in range(2):
                            e4 = 2 * q + h
                            sp.wait_ge(S["down_free"], m * RING + (DN_PER * l + 1 + e4))
                            load_expert_dn(e4, l, bass.ds(m * RING + e4, 1))
                over_loads(sp, l)

        @block.gpsimd
        def _(pool):
            pool.memset(condw[:, :, :], 0.0)
            pool.memset(cr[:, :, :], 0.0).then_inc(S["zeroed"], 1)
            pool.sem_inc(S["down_free"], DN0)
            for free in [S[n] for n in ("hid_ready", "y_a", "y_b")] + [o[n] for o in ov for n in ("comb", "xg", "hid", "y")]:
                pool.sem_inc(free, BEFORE)
            pool.wait_ge(S["const_in"], 48)
            for l in range(DEPTH):
                if l > 0:
                    pool.wait_ge(S["x_bank"], x_banks(2 * l))
                pool.memset(kpe[:, :, 0:MLA_N], 0.0)
                pool.wait_ge(S["setup_evict_d"], 1)
                pool.wait_ge(S["setup_evict_a"], 1)
                pool.tensor_copy(dkT[:, :, 1, :], ckT[:, l])
                pool.tensor_copy(ckvT[:, 1, :], clT[:, l])
                pool.tensor_copy(kpeT[0:MLA_QK, 1, :], crT[:, l]).then_inc(S["caches_placed"], 1)
                pool.wait_ge(S["x_bank"], x_banks(2 * l + 1))
                pool.memset(yy, 0.0)
                pool.memset(hs, 0.0)
                pool.memset(wgt[:, E:E + 4, :], 0.0)
                pool.memset(pos[:, E:E + 4, :], -1.0).then_inc(S["zeroed"], 1)

        @block.scalar
        def _(act):
            link, settle = chain(act, S["act_own"])
            A = nc.scalar.activation
            n_small = [0]

            def load(dst, src, s="small_in"):
                act.dma_start(dst, src).then_inc(S[s], 16)
                if s == "small_in":
                    n_small[0] += 1
            for g, name in enumerate(("c_ctx", "c")):
                src = t[name] if name == "c_ctx" else t[name].rearrange("a d -> (a d)")
                load(cond[:, g], src.rearrange("(p c) -> p c", c=NC_), "x_in")
            for l in range(DEPTH):
                load(b_ada[:, l], t["b_ada"][l].rearrange("(s p c) -> p s c", p=P, c=NC_), "mod_in")
                load(gains[:, l], t["norm_mix"][l].rearrange("(p c) -> p c", c=NC_), "mod_in")
                load(gains[:, 2 + l], t["norm_ffn"][l].rearrange("(p c) -> p c", c=NC_), "mod_in")
            load(ck[:, :, :, :], t["cache_diff_k"][0].rearrange("l h t d -> t l h d"))
            load(cv[:, :, :, :], t["cache_diff_v"][0].rearrange("l h t d -> t l h d"))
            load(cl[:, :, :], t["cache_mla_ckv"][0].rearrange("l t d -> t l d"))
            act.wait_ge(S["zeroed"], 1)
            load(cr[:, :, MLA_N:], t["cache_mla_kpe"][0].rearrange("l t d -> t l d"))
            for d, name in enumerate(("state_ret_fwd", "state_ret_bwd")):
                for b in range(2):
                    for l in range(DEPTH):
                        load(s0[64 * b:64 * b + 64, l, :, d, :],
                             t[name][0, l].rearrange("(m b) d e -> b d m e", b=2)[b])
            for l in range(DEPTH):
                for dst, src in ((r_bias(l), t["router_bias"][l]), (r_subln(l), t["diff_subln"][l]),
                                 (r_kvn(l), t["mla_kv_norm"][l]), (r_qn(l), t["mla_q_norm"][l]),
                                 (r_lam(l), t["diff_lambda"][l].rearrange("a b -> (a b)")),
                                 (r_dec(l)[:, 0:4], t["ret_decay_fwd"][l]), (r_dec(l)[:, 4:8], t["ret_decay_bwd"][l])):
                    load(dst, src.partition_broadcast(P))
            assert 16 * n_small[0] == small_total

            act.wait_ge(S["x_in"], 32)
            act.wait_ge(S["zeroed"], 1)
            A(condw[:, :, 0:G], cond[:, :, :].rearrange("p g c -> p c g"), ACT.Silu).then_inc(S["cond_ready"], 1)
            settle("cond_ready")
            act.wait_ge(S["turned_x"], 1)
            A(xT[:, :, 0:P], PS[:, 0:2, :].rearrange("p b (c t) -> p (b c) t", c=4), ACT.Copy).then_inc(S["xT_a"], 1)
            settle("xT_a")

            def ada(n):
                act.wait_ge(S["weights_used"], number[items_ada[n]] + 1)
                if n >= 1:
                    act.wait_ge(S["ada_sel"], n)
                A(rada[:, :], PS[:, 7, :], ACT.Copy).then_inc(S["ada_r"], 1)
                settle("ada_r")

            def norm(k):
                for b in range(4):
                    if k == 0:
                        act.wait_ge(S["xT_d"], 1)
                    else:
                        act.wait_ge(S["x_bank"], x_banks(k - 1) + b + 1)
                    A(hT[:, 2 * b:2 * b + 2, :], xT[:, 2 * b:2 * b + 2, :], ACT.Square).then_inc(S["sq_ready"], 1)
                act.wait_ge(S["ss_ready"], k + 1)
                A(small[:, 0:T], PS[:, 6, 0:T], ACT.Sqrt, bias=col("eps"), scale=1.0 / D).then_inc(S["std_ready"], 1)
                if k == 0:
                    for n in range(4):
                        ada(n)
                l, w = divmod(k, 2)
                act.wait_ge(S["amp_ready"], k + 1)
                for c in range(NC_):
                    act.wait_ge(S["xn_ready"], NC_ * k + c + 1)
                    A(hT[:, c, 0:P], xn[:, c, 0:P], ACT.Identity, scale=amp[:, w, c, 0:1],
                      bias=mod[:, l, 3 * w, c, 0:1]).then_inc(S["h_a"], 1)

            def prepare(l):
                A(small[:, 260:268], r_dec(l), ACT.Exp).then_inc(S["decay_rate"], 1)
                settle("decay_rate")
                act.wait_ge(S["lam_arg"], l + 1)
                A(small[:, 300:302], small[:, 298:300], ACT.Exp).then_inc(S["lam_exp"], 1)
                settle("lam_exp")
                act.wait_ge(S["decay_args"], l + 1)
                A(decv[:, :, :], decv[:, :, :], ACT.Exp)
                A(dmat, dmat, ACT.Exp).then_inc(S["decays_ready"], 1)
                settle("decays_ready")

            act.wait_ge(S["const_in"], 48)
            for l in range(DEPTH):
                if l > 0:
                    prepare(l)
                norm(2 * l)
                if l == 0:
                    act.wait_ge(S["small_in"], small_total)
                    prepare(l)
                projected(act, l, 0, 0)
                A(qT, PS[:, 0, :].rearrange("p (c t) -> p c t", c=2), ACT.Copy).then_inc(S["q_ready"], 1)
                settle("q_ready")
                projected(act, l, 0, 1)
                A(kT, PS[:, 1, :].rearrange("p (c t) -> p c t", c=2), ACT.Copy,
                  scale=RET_D ** -0.5).then_inc(S["k_ready"], 1)
                settle("k_ready")
                if l == 0:
                    act.wait_ge(S["turned_x"], 4)
                    A(clT[:, :, :], PS[:, 5, 0:2 * P].rearrange("p (l t) -> p l t", l=2), ACT.Copy)
                    A(crT[:, :, :], PS[0:MLA_QK, 5, 2 * P:4 * P].rearrange("p (l t) -> p l t", l=2),
                      ACT.Copy).then_inc(S["setup_evict_a"], 1)
                ada_here(ada, l, 0)
                for g in range(G):
                    projected(act, l, 1, g)
                    A(rgate[:, g], PS[:, 2 + g, 256:512], ACT.Exp, scale=-1.0).then_inc(S["rg_exp"], 1)
                    settle("rg_exp")
                ada_here(ada, l, 1)
                projected(act, l, 2, 0)
                A(dqT, PS[:, 4, :].rearrange("p (c t) -> p c t", c=2), ACT.Copy).then_inc(S["dq_ready"], 1)
                settle("dq_ready")
                ada_here(ada, l, 2)
                for g in range(G):
                    projected(act, l, 3, g)
                    link(A(work[:, 0:256], PS[:, g, 256:512], ACT.Square, accum_out=small[:, 304 + g:305 + g]))
                    A(dv_tok[:, g], PS[:, g, 0:256], ACT.Copy)
                    A(small[:, 306 + g:307 + g], small[:, 304 + g:305 + g], ACT.Sqrt, bias=col("eps"),
                      scale=1.0 / Q_LORA).then_inc(S["cq_sq"], 1)
                    settle("cq_sq")
                ada_here(ada, l, 3)
                act.wait_ge(S["weights_used"], number[("w_in", l, 4)] + 1)
                for g in range(G):
                    link(A(work[:, 0:128], PS[:, 2, 256 * g:256 * g + 128], ACT.Square,
                           accum_out=small[:, 310 + g:311 + g]))
                A(small[:, 312:314], small[:, 310:312], ACT.Sqrt, bias=col("eps"),
                  scale=1.0 / KV_LORA).then_inc(S["ckv_sq"], 1)
                settle("ckv_sq")
                ada_here(ada, l, 4)
                act.wait_ge(S["t_cq"], l + 1)
                A(cqT, PS[:, 3, :].rearrange("p (c t) -> p c t", c=2), ACT.Copy).then_inc(S["cqT_ready"], 1)
                settle("cqT_ready")
                act.wait_ge(S["t_ckv"], l + 1)
                A(ckvT[:, 0:3:2, :], PS[:, 4, 0:2 * P].rearrange("p (k t) -> p k t", k=2),
                  ACT.Copy).then_inc(S["ckvT_ready"], 1)
                settle("ckvT_ready")
                for b in range(4):
                    act.wait_ge(S["uq"], 4 * l + b + 1)
                    A(qmT[0:MLA_QK, 2 * b:2 * b + 2, :], PS[0:MLA_QK, b, :].rearrange("p (h t) -> p h t", h=2),
                      ACT.Copy).then_inc(S["qm_ready"], 1)
                    settle("qm_ready")
                act.wait_ge(S["ret_sum"], l + 1)
                A(small[:, 328:336], small[:, 320:328], ACT.Sqrt, bias=col("eps"),
                  scale=1.0 / RET_D).then_inc(S["ret_std"], 1)
                settle("ret_std")
                act.wait_ge(S["kv_p"], l + 1)
                A(kv_out[0:64], PS[0:64, 5, :].rearrange("p (d h e) -> p d h e", d=2, h=4),
                  ACT.Copy).then_inc(S["kv_ready"], 1)
                settle("kv_ready")
                act.wait_ge(S["kv_ready"], l + 1)
                store_count = [0]

                def store(dst, src):
                    act.dma_start(dst, src).then_inc(S["store_done"], 16)
                    store_count[0] += 1
                for d, name in enumerate(("ret_fwd", "ret_bwd")):
                    store(out[name][0, l].rearrange("h d e -> d h e"), kv_out[0:64, d])
                for h in range(0, MLA_H, 2):
                    act.wait_ge(S["ukv_k"], MLA_H * l + h + 1)
                    A(kmT[0:64, h], PS[0:64, k_bank(h), 0:3 * P].rearrange("p (k t) -> p k t", k=3),
                      ACT.Copy).then_inc(S["km_a"], 1)
                    settle("km_a")
                act.wait_ge(S["ktok_ready"], l + 1)
                act.wait_ge(S["ckvn_ready"], l + 1)
                act.wait_ge(S["cq_sq"], 2 * l + 2)
                store(out["diff_k"][0, l].rearrange("h t d -> t h d"), dk_tok.rearrange("p (h d) -> p h d", h=DIF_H))
                store(out["diff_v"][0, l].rearrange("h t d -> t h d"),
                      dv_tok[:, 0].rearrange("p (h d) -> p h d", h=DIF_H))
                store(out["mla_ckv"][0, l], ckvn[:, 0])
                store(out["mla_kpe"][0, l], kpe[:, 0, MLA_N:])
                assert store_count[0] == stores_in_layer
                for k in range(3):
                    if k < 2:
                        act.wait_ge(S["ukv_v"], 2 * l + k + 1)
                    else:
                        act.wait_ge(S["weights_used"], number[("mla", l, 0)] + 1)
                    A(vm[:, k], PS[:, (5, 0, 1)[k], :], ACT.Copy).then_inc(S["vm_ready"], 1)
                    settle("vm_ready")
                for u in range(4):
                    U = 4 * l + u
                    nk = 1 + u % 2
                    scale = (DIF_D if u < 2 else MLA_QK) ** -0.5
                    act.wait_ge(S["nb_ready"], U + 1)
                    act.wait_ge(S["pt_turned"], pt_before(U))
                    for m in range(8):
                        A(prob[:, m, 0:nk * P], PS[:, m // 2, (m % 2) * 256:(m % 2) * 256 + nk * P], ACT.Exp,
                          bias=small[:, 340 + m:341 + m], scale=scale,
                          accum_out=small[:, 350 + m:351 + m]).then_inc(S["exp_done"], 1)
                        settle("exp_done")
                    ada_here(ada, l, 5 + u)
                    for b in range(1, 2 * nk, 2):
                        act.wait_ge(S["pt_turned"], pt_before(U) + b + 1)
                        A(pt_view(b, nk), PS[:, 5, :].rearrange("p (m t) -> p m t", m=4),
                          ACT.Copy).then_inc(S["pt_odd"], 1)
                        settle("pt_odd")
                    if u in (1, 2):
                        act.wait_ge(S["dif_sum"], 2 * l + u)
                        A(small[:, 472 + 4 * (u - 1):472 + 4 * u], small[:, 464 + 4 * (u - 1):464 + 4 * u], ACT.Sqrt,
                          bias=col("eps"), scale=1.0 / DIF_V).then_inc(S["dif_std"], 1)
                for b in (0, 2):
                    act.wait_ge(S["t_mix"], 4 * l + b + 1)
                    A(mixT[:, 2 * b:2 * b + 2, :], PS[:, b, :].rearrange("p (k t) -> p k t", k=2),
                      ACT.Copy).then_inc(S["mixT_a"], 1)
                    settle("mixT_a")
                norm(2 * l + 1)
                act.wait_ge(S["weights_used"], number[("router", l, 0)] + 1)
                A(score, PS[:, 4, 0:G * E].rearrange("p (g e) -> p g e", g=G), ACT.Sigmoid).then_inc(S["sig_exp"], 1)
                settle("sig_exp")
                for g in range(G):
                    act.wait_ge(S["t_h"], 2 * l + g + 1)
                    for s in range(3):
                        src = PS[:, 2 * g:2 * g + 2, :].rearrange("p b (c t) -> p (b c) t", c=4) if s == 0 \
                            else rem[:, s - 1].rearrange("p (c t) -> p c t", c=NC_)
                        if s > 0:
                            act.wait_ge(S["part_d"], 4 * l + 2 * g + s)
                        A(h3[:, g, s], src, ACT.Copy).then_inc(S["part_a"], 1)
                        settle("part_a")
                if l == DEPTH - 1:
                    act.wait_ge(S["part_d"], 4 * l + 4)
                    act.dma_start(rem[:, 0], t["norm_final"].partition_broadcast(P)).then_inc(S["gain_in"], 16)
                act.wait_ge(S["weights_used"], number[("shared", l, 0)] + 1)
                A(shs, PS[:, 5, :].rearrange("p (j t) -> p j t", j=2), ACT.Silu).then_inc(S["sh_silu"], 1)
                settle("sh_silu")
                g0 = (PAIRS + 1) * l
                act.wait_ge(S["gathered"], 2 * g0 + 1)
                A(xg[:, 0:4], PS[:, 4, :].rearrange("p (c t) -> p c t", c=4), ACT.Copy).then_inc(S["xg_a"], 1)
                with act.Fori(0, PAIRS // 2) as m:
                    for q in range(2):
                        act.wait_ge(S["weights_used"], m * 4 + (first_expert[l] + 2 * q + 2))
                        A(sact, PS[:, 5, 0:FF], ACT.Silu).then_inc(S["silu_ready"], 1)
                        act.wait_ge(S["gathered"], m * 4 + (2 * (g0 + q + 1) + 1))
                        A(xg[:, 0:4], PS[:, 4, :].rearrange("p (c t) -> p c t", c=4), ACT.Copy).then_inc(S["xg_a"], 1)
                        act.wait_ge(S["down_a"], m * 2 + (PAIRS * l + q + 1))
                        A(yy[:, 0:512], PS[:, 7, :], ACT.Copy).then_inc(S["y_a"], 1)
                o = ov[l]
                with act.If(over_flag(act, l) > 0):
                    with act.Fori(0, E) as e:
                        for w in range(OW):
                            act.wait_ge(o["gath"], e * (2 * OW) + (2 * w + 1))
                            A(xg[:, 0:4], PS[:, 4, :].rearrange("p (c t) -> p c t", c=4), ACT.Copy).then_inc(o["xg"], 1)
                            act.wait_ge(o["up"], e * OW + (w + 1))
                            A(sact, PS[:, 5, 0:FF], ACT.Silu).then_inc(o["silu"], 1)
                            act.wait_ge(o["down"], e * (2 * OW) + (2 * w + 1))
                            A(yy[:, 0:512], PS[:, 7, :], ACT.Copy).then_inc(o["y"], 1)
            for b in range(4):
                g, half = divmod(b, 2)
                act.wait_ge(S["turned_y"], b + 1)
                A(hT[:, 2 * b:2 * b + 2, :].rearrange("p c t -> p (c t)"), PS[:, 4 + b, :], ACT.Square,
                  accum_out=small[:, 2 * g + half:2 * g + half + 1]).then_inc(S["y_sq"], 1)
            act.wait_ge(S["y_ms"], 1)
            A(small[:, 6:8], small[:, 4:6], ACT.Sqrt, bias=col("eps"), scale=1.0 / D).then_inc(S["y_std"], 1)
            y_tok = arena[:, 0:G * D].rearrange("p (g n) -> p g n", g=G)
            for g, name in enumerate(("y_prompt", "y_sample")):
                act.wait_ge(S["y_done"], g + 1)
                act.dma_start(out[name][0], y_tok[:, g]).then_inc(S["store_done"], 16)
            act.wait_ge(S["store_done"], 16 * (stores_in_layer * DEPTH + 2))

        @block.vector
        def _(v):
            link, settle = chain(v, S["dve_own"])
            tt, ts, stt = v.tensor_tensor, v.tensor_scalar, v.scalar_tensor_tensor
            v.wait_ge(S["turned_x"], 2)
            v.tensor_copy(xT[:, :, P:T], PS[:, 2:4, :].rearrange("p b (c t) -> p (b c) t", c=4)).then_inc(S["xT_d"], 1)
            settle("xT_d")
            v.wait_ge(S["xT_a"], 1)
            v.wait_ge(S["const_in"], 48)

            def ada(n):
                la, q = divmod(n, 12)
                half = q % 2
                hp = slice(64 * half, 64 * half + 64)
                v.wait_ge(S["ada_sel"], n + 1)
                tt(mod[hp, la, q // 2], PS[hp, 6, 0:16].rearrange("p (c g) -> p c g", g=G),
                   bc(b_ada[hp, la, q // 2], 2, G), ALU.add).then_inc(S["ada_mod"], 1)
                settle("ada_mod")

            def ada_lag(l, k):
                for n in ada_at(l, k):
                    if n > 4:
                        ada(n - 1)
                if l == 0 and k == 9:
                    ada(23)

            def amplify(k):
                l, w = divmod(k, 2)
                v.wait_ge(S["ada_mod"], 4 if k == 0 else 24)
                if k >= 2:
                    v.wait_ge(S["h_a"], NC_ * (k - 1))
                stt(amp[:, w], mod[:, l, 3 * w + 1], 1.0, bc(gains[:, 2 * w + l], 2, G), ALU.add,
                    ALU.mult).then_inc(S["amp_ready"], 1)
                settle("amp_ready")

            def norm(k):
                v.wait_ge(S["std_ready"], k + 1)
                link(v.reciprocal(small[:, 0:T], small[:, 0:T]))
                l, w = divmod(k, 2)

                def normed(c):
                    tt(xn[:, c], xT[:, c], small[:, 0:T], ALU.mult).then_inc(S["xn_ready"], 1)

                def modulated(c):
                    v.wait_ge(S["xn_ready"], NC_ * k + c + 1)
                    ts(hT[:, c, P:T], xn[:, c, P:T], amp[:, w, c, 1:2], mod[:, l, 3 * w, c, 1:2], ALU.mult,
                       ALU.add).then_inc(S["h_d"], 1)
                if k == 0:
                    for c in range(NC_):
                        normed(c)
                    v.wait_ge(S["mod_in"], mod_total)
                    for n in range(4):
                        ada(n)
                    amplify(0)
                else:
                    normed(0)
                for c in range(NC_):
                    if k > 0 and c + 1 < NC_:
                        normed(c + 1)
                    modulated(c)

            def lam_init_of(l):
                return 0.8 - 0.6 * math.exp(-0.3 * l)

            def prepare(l):
                lam_r = r_lam(l).rearrange("p (a b d) -> p a b d", a=2, b=2)
                prod = small[:, 400:464].rearrange("p (a d) -> p a d", a=2)
                link(tt(prod, lam_r[:, :, 0], lam_r[:, :, 1], ALU.mult))
                v.tensor_reduce(small[:, 298:300], prod, AX.X, ALU.add).then_inc(S["lam_arg"], 1)
                settle("lam_arg")
                v.wait_ge(S["decay_rate"], l + 1)
                link(ts(dec[:, l], small[:, 260:268], -1.0, None, ALU.mult))
                for k, (c, o) in enumerate((("i+1", 0), ("C-i", 4), ("C-1-i", 0), ("i", 4))):
                    link(ts(decv[:, k], dec[:, l, o:o + 4], col(c), None, ALU.mult))
                if l > 0:
                    v.wait_ge(S["x_bank"], x_banks(2 * l))
                for h in range(RET_H):
                    dst = dmat[:, h % 2, h // 2]
                    link(ts(dst, C("fwd"), dec[:, l, h:h + 1], None, ALU.mult))
                    ins = stt(dst, C("bwd"), dec[:, l, 4 + h:5 + h], dst, ALU.mult, ALU.add)
                    if h < RET_H - 1:
                        link(ins)
                    else:
                        ins.then_inc(S["decay_args"], 1)
                        settle("decay_args")
                v.wait_ge(S["lam_exp"], l + 1)
                link(tt(nlam[:, l:l + 1], small[:, 301:302], small[:, 300:301], ALU.subtract))
                link(ts(nlam[:, l:l + 1], nlam[:, l:l + 1], -lam_init_of(l), None, ALU.add))

            for l in range(DEPTH):
                lam_init = lam_init_of(l)
                if l > 0:
                    prepare(l)
                    amplify(2 * l)
                norm(2 * l)
                if l == 0:
                    v.wait_ge(S["small_in"], small_total)
                    prepare(l)
                    v.wait_ge(S["turned_x"], 3)
                    v.tensor_copy(ckT[:, :, :, :], PS[:, 4, :].rearrange("p (l c t) -> p l c t", l=2, c=2)
                                  ).then_inc(S["setup_evict_d"], 1)
                    settle("setup_evict_d")
                ada_lag(l, 0)
                for g in range(G):
                    v.wait_ge(S["rg_exp"], 2 * l + g + 1)
                    link(v.tensor_copy(v_tok[:, g], PS[:, 2 + g, 0:256]))
                    link(ts(rgate[:, g], rgate[:, g], 1.0, None, ALU.add))
                    link(v.reciprocal(rgate[:, g], rgate[:, g]))
                    tt(rgate[:, g], rgate[:, g], PS[:, 2 + g, 256:512], ALU.mult).then_inc(S["rv_ready"], 1)
                    settle("rv_ready")
                ada_lag(l, 1)
                projected(v, l, 2, 1)
                v.tensor_copy(dkT[:, :, 0:3:2, :], PS[:, 5, :].rearrange("p (c k t) -> p c k t", c=2, k=2)
                              ).then_inc(S["dk_ready"], 1)
                settle("dk_ready")
                ada_lag(l, 2)
                for g in range(G):
                    v.wait_ge(S["cq_sq"], 2 * l + g + 1)
                    link(v.reciprocal(small[:, 314:315], small[:, 306 + g:307 + g]))
                    stt(cqn[:, g], PS[:, g, 256:512], small[:, 314:315], r_qn(l), ALU.mult,
                        ALU.mult).then_inc(S["cqn_ready"], 1)
                    settle("cqn_ready")
                ada_lag(l, 3)
                v.wait_ge(S["ckv_sq"], l + 1)
                link(v.reciprocal(small[:, 316:318], small[:, 312:314]))
                for g in range(G):
                    link(stt(ckvn[:, g], PS[:, 2, 256 * g:256 * g + 128], small[:, 316 + g:317 + g], r_kvn(l),
                             ALU.mult, ALU.mult))
                v.wait_ge(S["caches_placed"], l + 1)
                v.tensor_copy(kpe[:, :, MLA_N:], PS[:, 2, :].rearrange("p (g n) -> p g n", g=G)[:, :, 128:160]
                              ).then_inc(S["ckvn_ready"], 1)
                settle("ckvn_ready")
                ada_lag(l, 4)
                v.wait_ge(S["t_kpe"], l + 1)
                v.tensor_copy(kpeT[0:MLA_QK, 0:3:2, :],
                              PS[0:MLA_QK, 5, 0:2 * P].rearrange("p (k t) -> p k t", k=2)).then_inc(S["kpeT_ready"], 1)
                settle("kpeT_ready")
                v.wait_ge(S["ret_s"], l + 1)
                v.wait_ge(S["decays_ready"], l + 1)
                for b in range(2):
                    ins = tt(sT[:, b], PS[:, b, :].rearrange("p (g m t) -> p g m t", g=G, m=2), bc(dmat[:, b], 1, G),
                             ALU.mult)
                    if b == 0:
                        link(ins)
                    else:
                        ins.then_inc(S["sT_ready"], 1)
                        settle("sT_ready")
                v.wait_ge(S["ret_x"], l + 1)
                for b in range(2):
                    ins = v.tensor_copy(cross.rearrange("p (m b) d e -> p b m (d e)", b=2)[:, b],
                                        PS[:, 2 + b, 0:256].rearrange("p (m n) -> p m n", m=2))
                    if b == 0:
                        link(ins)
                    else:
                        ins.then_inc(S["cross_ready"], 1)
                        settle("cross_ready")
                v.wait_ge(S["t_k"], l + 1)
                for d in range(2):
                    link(tt(kdec[:, d].rearrange("p (h e) -> p h e", h=4),
                            PS[:, 4, 0:256].rearrange("p (h e) -> p h e", h=4), bc(decv[:, 2 + d], 2, RET_D), ALU.mult))
                v.tensor_copy(dk_tok, PS[:, 4, 256:512]).then_inc(S["ktok_ready"], 1)
                settle("ktok_ready")

                def rope(dst_views, src, cos, sin, tmp, done):
                    link(tt(tmp, src, sin, ALU.mult))
                    link(tt(dst_views, dst_views, cos, ALU.mult))
                    tt(dst_views, dst_views, tmp, ALU.add).then_inc(done, 1)
                v.wait_ge(S["d_rot"], l + 1)
                rot = PS[:, 5, :].rearrange("p (a c t) -> p a c t", a=2, c=2)
                tmp = rtmp[:, 0].rearrange("p (c t) -> p c t", c=4)
                link(tt(tmp, PS[:, 5, :].rearrange("p (c t) -> p c t", c=4), bc(C("sin_d"), 1, 4), ALU.mult))
                link(tt(dqT[:, :, P:T], dqT[:, :, P:T], bc(C("cos_d"), 1, 2), ALU.mult))
                link(tt(dqT[:, :, P:T], dqT[:, :, P:T], tmp[:, 0:2], ALU.add))
                link(tt(dkT[:, :, 2], dkT[:, :, 2], bc(C("cos_d"), 1, 2), ALU.mult))
                tt(dkT[:, :, 2], dkT[:, :, 2], tmp[:, 2:4], ALU.add).then_inc(S["d_roped"], 1)
                settle("d_roped")
                v.wait_ge(S["ret_o"], l + 1)
                ro = work.rearrange("p (g h e) -> p g h e", g=G, h=4)
                link(v.tensor_copy(ro, PS[:, 4, :].rearrange("p (g h e) -> p g h e", g=G, h=4)))
                for d in range(2):
                    tv = rtmp[:, 1, 0:256].rearrange("p (h e) -> p h e", h=4)
                    link(tt(tv, cross[:, :, d], bc(decv[:, d], 2, RET_D), ALU.mult))
                    link(tt(ro[:, 1], ro[:, 1], tv, ALU.add))
                link(tt(rtmp[:, 0], work, work, ALU.mult))
                v.tensor_reduce(small[:, 320:328], rtmp[:, 0].rearrange("p (a e) -> p a e", e=RET_D), AX.X,
                                ALU.add).then_inc(S["ret_sum"], 1)
                settle("ret_sum")
                v.wait_ge(S["kpe_rot"], l + 1)
                rp = slice(0, MLA_QK)
                tmpk = rtmp[rp, 1, 0:P]
                rope(kpeT[rp, 2], PS[rp, 0, 0:P], C("cos_m", parts=MLA_QK), C("sin_m", parts=MLA_QK), tmpk,
                     S["kpe_roped"])
                for b in range(2):
                    v.wait_ge(S["q_rot"], 2 * l + b + 1)
                    if b == 0:
                        v.wait_ge(S["kpe_roped"], l + 1)
                    else:
                        v.wait_ge(S["q_roped"], 2 * l + 1)
                    rope(qmT[rp, 4 * b:4 * b + 4, P:T], PS[rp, 1 + b, :].rearrange("p (h t) -> p h t", h=4),
                         bc(C("cos_m", parts=MLA_QK), 1, 4), bc(C("sin_m", parts=MLA_QK), 1, 4),
                         rtmp[rp, 1].rearrange("p (h t) -> p h t", h=4), S["q_roped"])
                v.wait_ge(S["ret_std"], l + 1)
                link(v.reciprocal(small[:, 328:336], small[:, 328:336]))
                link(tt(work.rearrange("p (a e) -> p a e", e=RET_D), work.rearrange("p (a e) -> p a e", e=RET_D),
                        bc(small[:, 328:336], 2, RET_D), ALU.mult))
                link(tt(mix[:, :, 0:256], work.rearrange("p (g n) -> p g n", g=G), rgate, ALU.mult))
                for h in range(1, MLA_H, 2):
                    v.wait_ge(S["ukv_k"], MLA_H * l + h + 1)
                    v.tensor_copy(kmT[0:64, h], PS[0:64, k_bank(h), 0:3 * P].rearrange("p (k t) -> p k t", k=3)
                                  ).then_inc(S["km_d"], 1)
                    settle("km_d")
                v.tensor_copy(kmT[64:96], bc(kpeT[64:96], 1, MLA_H)).then_inc(S["km_d"], 1)
                settle("km_d")
                def negated_max(u):
                    nk = 1 + u % 2
                    scale = (DIF_D if u < 2 else MLA_QK) ** -0.5
                    v.wait_ge(S["s_ready"], 4 * l + u + 1)
                    sv = PS[:, 0:4, :].rearrange("p b (c k) -> p b c k", c=2)[:, :, :, 0:nk * P]
                    link(v.tensor_reduce(small[:, 370:378].rearrange("p (b c) -> p b c", c=2), sv, AX.X, ALU.max))
                    ts(small[:, 340:348], small[:, 370:378], -scale, None, ALU.mult).then_inc(S["nb_ready"], 1)
                    settle("nb_ready")

                def dif_heads(u):
                    return rtmp[:, u, 0:256]

                def dif_normed(u):
                    v.wait_ge(S["dif_std"], 2 * l + u + 1)
                    std = small[:, 472 + 4 * u:476 + 4 * u]
                    link(v.reciprocal(std, std))
                    o3 = dif_heads(u).rearrange("p (h e) -> p h e", h=4)
                    link(tt(o3, o3, bc(std, 2, DIF_V), ALU.mult))
                    link(stt(mix[:, u, 256:512].rearrange("p (h e) -> p h e", h=4), o3, 1.0 - lam_init,
                             bc(r_subln(l), 1, 4), ALU.mult, ALU.mult))

                negated_max(0)
                for u in range(4):
                    U = 4 * l + u
                    g, nk = u % 2, 1 + u % 2
                    ada_lag(l, 5 + u)
                    v.wait_ge(S["exp_done"], 8 * (U + 1))
                    link(v.reciprocal(small[:, 380:388], small[:, 350:358]))
                    for b in range(0, 2 * nk, 2):
                        v.wait_ge(S["pt_turned"], pt_before(U) + b + 1)
                        v.tensor_copy(pt_view(b, nk), PS[:, 4, :].rearrange("p (m t) -> p m t", m=4)
                                      ).then_inc(S["pt_even"], 1)
                        settle("pt_even")
                    if u < 3:
                        negated_max(u + 1)
                    v.wait_ge(S["pv_done"], U + 1)
                    rs = small[:, 380:388].rearrange("p (r c) -> p r c", c=2)
                    o4 = PS[:, 4, :].rearrange("p (r c e) -> p r c e", r=4, c=2)
                    if u < 2:
                        osc = work.rearrange("p (r c e) -> p r c e", r=4, c=2)
                        tt(osc, o4, bc(rs, 3, DIF_V), ALU.mult).then_inc(S["o_done"], 1)
                        settle("o_done")
                        od = dif_heads(u).rearrange("p (c r e) -> p c r e", c=2, r=2)
                        for r1 in range(2):
                            link(stt(od[:, :, r1], osc[:, 2 * r1 + 1], nlam[:, l:l + 1], osc[:, 2 * r1], ALU.mult,
                                     ALU.add))
                        link(tt(rtmp[:, u, 256:512], dif_heads(u), dif_heads(u), ALU.mult))
                        v.tensor_reduce(small[:, 464 + 4 * u:468 + 4 * u],
                                        rtmp[:, u, 256:512].rearrange("p (h e) -> p h e", h=4),
                                        AX.X, ALU.add).then_inc(S["dif_sum"], 1)
                        settle("dif_sum")
                    if u in (1, 2):
                        dif_normed(u - 1)
                    if u >= 2:
                        tt(mix[:, g, 512:1024].rearrange("p (c r e) -> p r c e", c=2, r=4), o4, bc(rs, 3, MLA_V),
                           ALU.mult).then_inc(S["o_done"], 1)
                        settle("o_done")
                for b in (1, 3):
                    v.wait_ge(S["t_mix"], 4 * l + b + 1)
                    v.tensor_copy(mixT[:, 2 * b:2 * b + 2, :], PS[:, b, :].rearrange("p (k t) -> p k t", k=2)
                                  ).then_inc(S["mixT_d"], 1)
                    settle("mixT_d")
                ada_lag(l, 9)
                v.wait_ge(S["store_done"], 16 * stores_in_layer * (l + 1))
                v.wait_ge(S["ada_mod"], 24)
                for b in range(4):
                    if b < 3:
                        v.wait_ge(S["wo_done"], 3 * l + b + 1)
                    else:
                        v.wait_ge(S["weights_used"], number[("w_out", l, 1)] + 1)
                    for c in (2 * b, 2 * b + 1):
                        for g in range(G):
                            tk = slice(g * P, g * P + P)
                            ins = stt(xT[:, c, tk], PS[:, wo_bank(c), (c % 2) * T + g * P:(c % 2) * T + g * P + P],
                                      mod[:, l, 2, c, g:g + 1], xT[:, c, tk], ALU.mult, ALU.add)
                    ins.then_inc(S["x_bank"], 1)
                    settle("x_bank")
                amplify(2 * l + 1)
                norm(2 * l + 1)
                v.wait_ge(S["sig_exp"], l + 1)
                link(tt(selv, score, bc(r_bias(l), 1, G), ALU.add))
                for g in range(G):
                    for a in range(GROUPS):
                        last = v.max(gtop[:, g, a], selv[:, g, 8 * a:8 * a + 8])
                link(last)
                link(tt(gsc, gtop[:, :, :, 0], gtop[:, :, :, 1], ALU.add))

                def topk(src, k, n, dst):
                    for g in range(G):
                        last = v.max(top8[:, g], src[:, g])
                    link(last)
                    for g in range(G):
                        last = v.max_index(idx8[:, g], top8[:, g], src[:, g])
                    link(last)
                    link(v.tensor_copy(idxf, idx8))
                    for g in range(G):
                        hv = hit[:, 0:n * k].rearrange("p (e k) -> p e k", k=k)
                        link(tt(hv, bc(cst[:, CO["iota"]:CO["iota"] + n], 2, k), bc(idxf[:, g, 0:k], 1, n),
                                ALU.is_equal))
                        link(v.tensor_reduce(dst[:, g], hv, AX.X, ALU.max))
                topk(gsc, TOP_G, GROUPS, gmask)
                link(ts(gmask, gmask, 1.0, 1e30, ALU.subtract, ALU.mult))
                link(tt(selv.rearrange("p g (a b) -> p g a b", a=GROUPS), selv.rearrange("p g (a b) -> p g a b", a=GROUPS),
                        bc(gmask, 3, GROUPS), ALU.add))
                topk(selv, TOP_K, E, mask)
                link(tt(score, score, mask, ALU.mult))
                v.tensor_reduce(gsum[:, 0:2], score, AX.X, ALU.add).then_inc(S["routed"], 1)
                settle("routed")
                v.wait_ge(S["routed"], l + 1)
                link(v.reciprocal(gsum[:, 2:4], gsum[:, 0:2]))
                link(ts(gsum[:, 2:4], gsum[:, 2:4], ROUTED_SCALE, None, ALU.mult))
                link(tt(wgt[:, 0:E, :].rearrange("p e g -> p g e"), score, bc(gsum[:, 2:4], 2, E), ALU.mult))
                for g in range(G):
                    for s in range(2):
                        v.wait_ge(S["part_a"], 6 * l + 3 * g + s + 1)
                        src = PS[:, 2 * g:2 * g + 2, :].rearrange("p b (c t) -> p (b c) t", c=4) if s == 0 \
                            else rem[:, 0].rearrange("p (c t) -> p c t", c=NC_)
                        tt(rem[:, s].rearrange("p (c t) -> p c t", c=NC_), src, h3[:, g, s],
                           ALU.subtract).then_inc(S["part_d"], 1)
                        settle("part_d")
                        if s == 0:
                            v.wait_ge(S["part_d"], 4 * l + 2 * g + 1)
                v.wait_ge(S["rank_done"], l + 1)
                link(v.tensor_reduce(fl[:, 0:1], PS[:, 4, G * E:G * E + E], AX.X, ALU.max))
                link(ts(fl[:, 1:2], fl[:, 0:1], float(CAP), None, ALU.is_gt))
                v.tensor_copy(flag_i[0:1, l:l + 1], fl[0:1, 1:2]).then_inc(S["flag_ready"], 1)
                settle("flag_ready")
                posv = pos[:, 0:E, :].rearrange("p e g -> p g e")
                link(stt(hit[:, 0:G * E].rearrange("p (g e) -> p g e", g=G),
                         PS[:, 4, 0:G * E].rearrange("p (g e) -> p g e", g=G), 1.0, mask, ALU.add, ALU.mult))
                ts(posv, hit[:, 0:G * E].rearrange("p (g e) -> p g e", g=G), -1.0, None, ALU.add
                   ).then_inc(S["pos_ready"], 1)
                settle("pos_ready")
                v.wait_ge(S["sh_silu"], l + 1)
                tt(shh, shs, PS[:, 6, :].rearrange("p (j t) -> p j t", j=2), ALU.mult).then_inc(S["sh_h"], 1)
                settle("sh_h")
                g0, s0_ = (PAIRS + 1) * l, (PAIRS + 2) * l
                iota2 = bc(bc(cst[:, CO["iota"]:CO["iota"] + CAP], 1, 2), 1, G)

                def pair_of(x, at):
                    return bc(x.rearrange("p e g -> p (e g)")[:, at].rearrange("p (e g) -> p g e", g=G), 3, CAP)

                def one_hot(at):
                    return tt(onehot.rearrange("p g (e s) -> p g e s", e=2), iota2, pair_of(pos, at), ALU.is_equal)

                def gate_it(at):
                    return tt(gated.rearrange("p g (e s) -> p g e s", e=2),
                              onehot.rearrange("p g (e s) -> p g e s", e=2), pair_of(wgt, at), ALU.mult)
                v.wait_ge(S["pos_ready"], l + 1)
                v.wait_ge(S["zeroed"], l + 2)
                one_hot(slice(0, 4)).then_inc(S["sel_ready"], 1)
                v.wait_ge(S["sel_ready"], s0_ + 1)
                gate_it(slice(0, 4)).then_inc(S["gated_ready"], 1)
                v.wait_ge(S["gathered"], 2 * g0 + 2)
                v.wait_ge(S["gated_ready"], g0 + 1)
                one_hot(slice(4, 8)).then_inc(S["sel_ready"], 1)
                v.tensor_copy(xg[:, 4:8], PS[:, 4, :].rearrange("p (c t) -> p c t", c=4)).then_inc(S["xg_b"], 1)
                with v.Fori(0, PAIRS // 2) as m:
                    for q in range(2):
                        v.wait_ge(S["silu_ready"], m * 2 + (PAIRS * l + q + 1))
                        tt(hh, sact, PS[:, 5, FF:2 * FF], ALU.mult).then_inc(S["hid_ready"], 1)
                        v.wait_ge(S["turned"], m * 2 + (PAIRS * l + q + 1))
                        v.tensor_copy(hs, PS[:, 6, :]).then_inc(S["hs_ready"], 1)
                        v.wait_ge(S["sel_ready"], m * 2 + (s0_ + q + 2))
                        gate_it(bass.ds(m * 8 + 4 * (q + 1), 4)).then_inc(S["gated_ready"], 1)
                        v.wait_ge(S["gathered"], m * 4 + (2 * (g0 + q + 1) + 2))
                        v.tensor_copy(xg[:, 4:8], PS[:, 4, :].rearrange("p (c t) -> p c t", c=4)).then_inc(S["xg_b"], 1)
                        v.wait_ge(S["gated_ready"], m * 2 + (g0 + q + 2))
                        one_hot(bass.ds(m * 8 + 4 * (q + 2), 4)).then_inc(S["sel_ready"], 1)
                        v.wait_ge(S["down_free"], m * 4 + (DN0 + DN_PER * l + 1 + 2 * q + 2))
                        v.tensor_copy(yy[:, 512:1024], PS[:, 6, :]).then_inc(S["y_b"], 1)
                o = ov[l]
                with v.If(over_flag(v, l) > 0):
                    with v.Fori(0, E) as e:
                        for w in range(OW):
                            v.wait_ge(o["comb"], e * OW + (w + BEFORE))
                            p_ap = pos.rearrange("p e g -> p (e g)")[:, bass.ds(e * 2, 2)]
                            w_ap = wgt.rearrange("p e g -> p (e g)")[:, bass.ds(e * 2, 2)]
                            ts(fl[:, 0:2], p_ap, float(-(CAP + P * w)), None, ALU.add).then_inc(o["step"], 1)
                            v.wait_ge(o["step"], e * (2 * OW) + (2 * w + 1))
                            tt(onehot, bc(C("iota"), 1, G), bc(fl[:, 0:2], 2, P), ALU.is_equal).then_inc(o["step"], 1)
                            v.wait_ge(o["step"], e * (2 * OW) + (2 * w + 2))
                            tt(gated, onehot, bc(w_ap, 2, P), ALU.mult).then_inc(o["sel"], 1)
                            v.wait_ge(o["gath"], e * (2 * OW) + (2 * w + 2))
                            v.tensor_copy(xg[:, 4:8], PS[:, 4, :].rearrange("p (c t) -> p c t", c=4)).then_inc(o["xg"], 1)
                            v.wait_ge(o["silu"], e * OW + (w + 1))
                            tt(hh, sact, PS[:, 5, FF:2 * FF], ALU.mult).then_inc(o["hid"], 1)
                            v.wait_ge(o["turn"], e * OW + (w + 1))
                            v.tensor_copy(hs, PS[:, 6, :]).then_inc(o["hs"], 1)
                            v.wait_ge(o["down"], e * (2 * OW) + (2 * w + 2))
                            v.tensor_copy(yy[:, 512:1024], PS[:, 6, :]).then_inc(o["y"], 1)
                v.wait_ge(S["combined"], l + 1)
                for c in range(NC_):
                    for g in range(G):
                        tk = slice(g * P, g * P + P)
                        ins = stt(xT[:, c, tk], PS[:, c // 2, (c % 2) * T + g * P:(c % 2) * T + g * P + P],
                                  mod[:, l, 5, c, g:g + 1], xT[:, c, tk], ALU.mult, ALU.add)
                    if c % 2:
                        ins.then_inc(S["x_bank"], 1)
                        settle("x_bank")
            v.wait_ge(S["y_sq"], 4)
            tt(small[:, 4:6], small[:, 0:4:2], small[:, 1:4:2], ALU.add).then_inc(S["y_ms"], 1)
            v.wait_ge(S["y_std"], 1)
            link(v.reciprocal(small[:, 6:8], small[:, 6:8]))
            v.wait_ge(S["gain_in"], 16)
            y_tok = arena[:, 0:G * D].rearrange("p (g n) -> p g n", g=G)
            for g in range(G):
                stt(y_tok[:, g].rearrange("p (t c) -> p c t", c=NC_),
                    PS[:, 4 + 2 * g:6 + 2 * g, :].rearrange("p b (c t) -> p (b c) t", c=4), small[:, 6 + g:7 + g],
                    rem[:, 0].rearrange("p (t c) -> p c t", c=NC_), ALU.mult, ALU.mult).then_inc(S["y_done"], 1)

        @block.tensor
        def _(pe):
            mmul = pe.matmul

            def turn(dst, src, parts=P):
                return pe.transpose(dst, src, ident[0:parts, 0:parts])

            pe.wait_ge(S["const_in"], 48)
            x_tok = arena[:, 0:G * D].rearrange("p (g n) -> p g n", g=G)
            for g in range(G):
                for c in range(NC_):
                    ins = turn(PS[:, 2 * g + c // 4, (c % 4) * P:(c % 4) * P + P],
                               x_tok[:, g].rearrange("p (t c) -> p c t", c=NC_)[:, c])
                ins.then_inc(S["turned_x"], 1)

            def turn_caches():
                pe.wait_ge(S["small_in"], small_total)
                for l in range(DEPTH):
                    for c in range(2):
                        ins = turn(PS[:, 4, (2 * l + c) * P:(2 * l + c + 1) * P],
                                   ck[:, l, 2 * c:2 * c + 2].rearrange("p h d -> p (h d)"))
                ins.then_inc(S["turned_x"], 1)
                for l in range(DEPTH):
                    turn(PS[:, 5, l * P:l * P + P], cl[:, l])
                for l in range(DEPTH):
                    ins = turn(PS[0:MLA_QK, 5, (2 + l) * P:(3 + l) * P], cr[:, l])
                ins.then_inc(S["turned_x"], 1)

            def piece(it):
                n = number[it]
                pe.wait_ge(gu_loaded[n % RING], loaded_at[it])
                return gu[:, n % RING, :]

            def ada_select(n):
                half = (n % 12) % 2
                pe.wait_ge(S["ada_r"], n + 1)
                if n >= 1:
                    pe.wait_ge(S["ada_mod"], n)
                for c in range(NC_):
                    ins = mmul(PS[64 * half:64 * half + 64, 6, 2 * c:2 * c + 2],
                               rada[:, :].rearrange("p (t c) -> p c t", c=NC_)[:, c], col("sel", 2), start=True, stop=True)
                ins.then_inc(S["ada_sel"], 1)

            def ada(n, flush=False):
                w = piece(items_ada[n])
                if n >= 1:
                    pe.wait_ge(S["ada_r"], n)
                wv = w.rearrange("p (c n) -> p c n", c=NC_)
                for kk in range(2):
                    for j in range(4):
                        k = 2 * j + kk
                        ins = mmul(PS[32 * j:32 * j + 32, 7, :], condw[:, k, :], wv[:, k], start=(kk == 0), stop=(kk == 1))
                ins.then_inc(S["weights_used"], 1)
                if n not in (0, 4):
                    ada_select(n - 1)
                if flush:
                    ada_select(n)

            def norm(k):
                for c in range(NC_):
                    if c % 2 == 0:
                        pe.wait_ge(S["sq_ready"], 4 * k + c // 2 + 1)
                    ins = mmul(PS[:, 6, 0:T], C("ones"), hT[:, c], start=(c == 0), stop=(c == NC_ - 1))
                ins.then_inc(S["ss_ready"], 1)

            def project(bank, o, lhs, rhs, fresh=None):
                for k in range(NC_):
                    if fresh is not None:
                        pe.wait_ge(S["h_a"], NC_ * fresh + k + 1)
                        pe.wait_ge(S["h_d"], NC_ * fresh + k + 1)
                    ins = mmul(PS[0:lhs(k).shape[-1], bank, o:o + rhs(k).shape[-1]], lhs(k), rhs(k), start=(k == 0),
                               stop=(k == NC_ - 1))
                return ins

            for l in range(DEPTH):
                norm(2 * l)
                if l == 0:
                    pe.wait_ge(S["cond_ready"], 1)
                    pe.wait_ge(S["std_ready"], 1)
                    for n in range(4):
                        ada(n, flush=(n == 3))

                def tok(g):
                    return lambda k: hT[:, k, g * P:g * P + P]

                def wcol(w, a, n, width=512):
                    wv = w[:, 0:NC_ * width].rearrange("p (c n) -> p c n", c=NC_)
                    return lambda k: wv[:, k, a:a + n]

                def all_tok(k):
                    return hT[:, k, :]
                w = piece(("w_in", l, 0))
                for b in range(2):
                    for c in range(2):
                        ins = project(b, c * T, wcol(w, 256 * b + 128 * c, 128), all_tok,
                                      fresh=2 * l if b + c == 0 else None)
                    if b == 0:
                        ins.then_inc(S["proj"], 1)
                    else:
                        ins.then_inc(S["weights_used"], 1)
                if l == 0:
                    turn_caches()
                ada_here(ada, l, 0)
                w = piece(("w_in", l, 1))
                for g in range(G):
                    ins = project(2 + g, 0, tok(g), wcol(w, 0, 512))
                    if g == 0:
                        ins.then_inc(S["proj"], 1)
                    else:
                        ins.then_inc(S["weights_used"], 1)
                ada_here(ada, l, 1)
                w = piece(("w_in", l, 2))
                if l == 0:
                    pe.wait_ge(S["setup_evict_a"], 1)
                    pe.wait_ge(S["setup_evict_d"], 1)
                for b in range(2):
                    for c in range(2):
                        ins = project(4 + b, c * T, wcol(w, 256 * b + 128 * c, 128), all_tok)
                    if b == 0:
                        ins.then_inc(S["proj"], 1)
                    else:
                        ins.then_inc(S["weights_used"], 1)
                ada_here(ada, l, 2)
                w = piece(("w_in", l, 3))
                pe.wait_ge(S["q_ready"], l + 1)
                pe.wait_ge(S["k_ready"], l + 1)
                for g in range(G):
                    ins = project(g, 0, tok(g), wcol(w, 0, 512))
                    if g == 0:
                        ins.then_inc(S["proj"], 1)
                    else:
                        ins.then_inc(S["weights_used"], 1)
                ada_here(ada, l, 3)
                w = piece(("w_in", l, 4))
                pe.wait_ge(S["rv_ready"], 2 * l + 1)
                for g in range(G):
                    ins = project(2, 256 * g, tok(g), wcol(w, 0, 160, 160))
                ins.then_inc(S["weights_used"], 1)
                ada_here(ada, l, 4)
                pe.wait_ge(S["cqn_ready"], 2 * l + 2)
                pe.wait_ge(S["rv_ready"], 2 * l + 2)
                for k in range(2):
                    for g in range(G):
                        ins = turn(PS[:, 3, (2 * k + g) * P:(2 * k + g + 1) * P], cqn[:, g, k * P:k * P + P])
                ins.then_inc(S["t_cq"], 1)
                pe.wait_ge(S["ckvn_ready"], l + 1)
                pe.wait_ge(S["dq_ready"], l + 1)
                for g in range(G):
                    ins = turn(PS[:, 4, g * P:g * P + P], ckvn[:, g])
                ins.then_inc(S["t_ckv"], 1)
                pe.wait_ge(S["dk_ready"], l + 1)
                for g in range(G):
                    ins = turn(PS[0:MLA_QK, 5, g * P:g * P + P], kpe[:, g])
                ins.then_inc(S["t_kpe"], 1)
                for g in range(G):
                    for m in range(2):
                        for b in range(2):
                            hp = slice(64 * b, 64 * b + 64)
                            ins = mmul(PS[:, b, (2 * g + m) * P:(2 * g + m + 1) * P], kT[hp, m, g * P:g * P + P],
                                       qT[hp, m, g * P:g * P + P], start=True, stop=True)
                ins.then_inc(S["ret_s"], 1)
                pe.wait_ge(S["cqT_ready"], l + 1)
                for m in range(2):
                    for b in range(2):
                        hp = slice(64 * b, 64 * b + 64)
                        ins = mmul(PS[:, 2 + b, m * P:m * P + P], qT[hp, m, P:T],
                                   s0[hp, l, m].rearrange("p d e -> p (d e)"), start=True, stop=True)
                ins.then_inc(S["ret_x"], 1)
                pe.wait_ge(S["ckvT_ready"], l + 1)
                for c in range(2):
                    turn(PS[:, 4, c * P:c * P + P], kT[:, c, 0:P])
                for c in range(2):
                    ins = turn(PS[:, 4, (2 + c) * P:(3 + c) * P], dkT[:, c, 0])
                ins.then_inc(S["t_k"], 1)
                pe.wait_ge(S["kpeT_ready"], l + 1)
                mmul(PS[:, 5, 0:256], C("rot_d"), dqT[:, :, P:T], start=True, stop=True)
                mmul(PS[:, 5, 256:512], C("rot_d"), dkT[:, :, 2], start=True, stop=True).then_inc(S["d_rot"], 1)
                w = piece(("mla", l, 0))
                w_uq = w[:, 0:UQ].rearrange("p (k n) -> p k n", k=2)
                w_ukv = w[:, UQ:UQ + UKV]
                for h in range(MLA_H):
                    if h == 0:
                        pe.wait_ge(S["sT_ready"], l + 1)
                    if h == 4:
                        pe.wait_ge(S["cross_ready"], l + 1)
                    for k in range(2):
                        ins = mmul(PS[0:MLA_QK, h // 2, (h % 2) * T:(h % 2) * T + T],
                                   w_uq[:, k, MLA_QK * h:MLA_QK * h + MLA_QK], cqT[:, k], start=(k == 0), stop=(k == 1))
                    if h % 2:
                        ins.then_inc(S["uq"], 1)
                pe.wait_ge(S["ktok_ready"], l + 1)
                for g in range(G):
                    for h in range(RET_H):
                        ins = mmul(PS[:, 4, (4 * g + h) * 64:(4 * g + h + 1) * 64], sT[:, h % 2, g, h // 2],
                                   v_tok[:, g, 64 * h:64 * h + 64], start=True, stop=True)
                ins.then_inc(S["ret_o"], 1)
                pe.wait_ge(S["d_roped"], l + 1)
                for d in range(2):
                    for h in range(RET_H):
                        ins = mmul(PS[0:64, 5, (4 * d + h) * 64:(4 * d + h + 1) * 64], kdec[:, d, 64 * h:64 * h + 64],
                                   v_tok[:, 0, 64 * h:64 * h + 64], start=True, stop=True)
                ins.then_inc(S["kv_p"], 1)
                pe.wait_ge(S["qm_ready"], 4 * l + 4)
                rm = cst[0:MLA_QK, CO["rot_m"]:CO["rot_m"] + MLA_QK]
                mmul(PS[0:MLA_QK, 0, 0:P], rm, kpeT[0:MLA_QK, 2], start=True, stop=True).then_inc(S["kpe_rot"], 1)
                for b in range(2):
                    mmul(PS[0:MLA_QK, 1 + b, :], rm, qmT[0:MLA_QK, 4 * b:4 * b + 4, P:T], start=True,
                         stop=True).then_inc(S["q_rot"], 1)
                for h in range(MLA_H):
                    if h == 1:
                        pe.wait_ge(S["ret_sum"], l + 1)
                    if h == 2:
                        pe.wait_ge(S["kv_ready"], l + 1)
                    if h == 3:
                        pe.wait_ge(S["kpe_roped"], l + 1)
                    if h in (4, 5):
                        pe.wait_ge(S["q_roped"], 2 * l + h - 3)
                    if h == 6:
                        pe.wait_ge(S["km_a"], 4 * l + 1)
                    if h == 7:
                        pe.wait_ge(S["km_d"], 5 * l + 1)
                    mmul(PS[0:64, k_bank(h), 0:3 * P], w_ukv[:, 128 * h:128 * h + 64],
                         ckvT.rearrange("p k t -> p (k t)"), start=True, stop=True).then_inc(S["ukv_k"], 1)
                wv = w_ukv.rearrange("p (h n) -> p h n", h=MLA_H)[:, :, MLA_N:]
                for k in range(3):
                    if k == 0:
                        pe.wait_ge(S["km_a"], 4 * l + 2)
                    if k == 1:
                        pe.wait_ge(S["km_d"], 5 * l + 2)
                    if k == 2:
                        pe.wait_ge(S["km_a"], 4 * l + 3)
                    mmul(PS[:, (5, 0, 1)[k], :], ckvT[:, k], wv, start=True, stop=True
                         ).then_inc(S["weights_used"] if k == 2 else S["ukv_v"], 1)
                pe.wait_ge(S["vm_ready"], 3 * l + 3)
                pe.wait_ge(S["km_a"], 4 * l + 4)
                pe.wait_ge(S["km_d"], 5 * l + 5)
                def scores(u):
                    U = 4 * l + u
                    g, nk = u % 2, 1 + u % 2
                    ks = slice(0, 1) if g == 0 else slice(1, 3)
                    if u > 0:
                        pe.wait_ge(S["exp_done"], 8 * U)
                    for c in range(2):
                        for r in range(4):
                            dst = PS[:, r, c * 256:c * 256 + nk * P]
                            if u < 2:
                                rp = slice(32 * r, 32 * r + 32)
                                ins = mmul(dst, dqT[rp, c, g * P:g * P + P],
                                           dkT[rp, c, ks].rearrange("p k t -> p (k t)"), start=True, stop=True)
                            else:
                                h = 4 * c + r
                                ins = mmul(dst, qmT[0:MLA_QK, h, g * P:g * P + P],
                                           kmT[0:MLA_QK, h, ks].rearrange("p k t -> p (k t)"), start=True, stop=True)
                    ins.then_inc(S["s_ready"], 1)

                scores(0)
                for u in range(4):
                    U = 4 * l + u
                    g, nk = u % 2, 1 + u % 2
                    ada_here(ada, l, 5 + u)
                    if u > 0:
                        pe.wait_ge(S["o_done"], U)
                    for b in range(2 * nk):
                        if b >= 2:
                            pe.wait_ge(S["pt_even" if b % 2 == 0 else "pt_odd"], half_before(U) + b // 2)
                        for j in range(4):
                            m, k = divmod(4 * b + j, nk)
                            if j == 0:
                                pe.wait_ge(S["exp_done"], 8 * U + (4 * b + 3) // nk + 1)
                            ins = turn(PS[:, 4 + b % 2, j * P:j * P + P], prob[:, m, k * P:k * P + P])
                        ins.then_inc(S["pt_turned"], 1)
                    if u < 3:
                        scores(u + 1)
                    pe.wait_ge(S["pt_even"], half_before(U) + nk)
                    pe.wait_ge(S["pt_odd"], half_before(U) + nk)
                    for m in range(8):
                        r, c = divmod(m, 2)
                        for k in range(nk):
                            if u < 2:
                                h = 2 * c + r // 2
                                vv = (dv_tok[:, 0, 64 * h:64 * h + 64] if g == 0 else
                                      cv[:, l, h] if k == 0 else dv_tok[:, 1, 64 * h:64 * h + 64])
                            else:
                                h = 4 * c + r
                                vv = vm[:, k + g, 64 * h:64 * h + 64]
                            ins = mmul(PS[:, 4, m * 64:m * 64 + 64], pt_tile(m, k, nk), vv, start=(k == 0), stop=(k == nk - 1))
                    ins.then_inc(S["pv_done"], 1)
                pe.wait_ge(S["o_done"], 4 * l + 4)
                for k in range(NC_):
                    for g in range(G):
                        ins = turn(PS[:, k // 2, ((k % 2) * 2 + g) * P:((k % 2) * 2 + g + 1) * P],
                                   mix[:, g, k * P:k * P + P])
                    if k % 2:
                        ins.then_inc(S["t_mix"], 1)
                if l == 0:
                    ada_select(23)
                pe.wait_ge(S["mixT_a"], 2 * l + 2)
                pe.wait_ge(S["mixT_d"], 2 * l + 2)
                wo = [piece(("w_out", l, i)).rearrange("p (k t c) -> p k c t", k=4, c=NC_) for i in range(2)]
                for c in range(NC_):
                    for k in range(NC_):
                        ins = mmul(PS[:, wo_bank(c), (c % 2) * T:(c % 2) * T + T], wo[k // 4][:, k % 4, c], mixT[:, k],
                                   start=(k == 0), stop=(k == NC_ - 1))
                        if c == NC_ - 1 and k == 3:
                            ins.then_inc(S["weights_used"], 1)
                    if c == NC_ - 1:
                        ins.then_inc(S["weights_used"], 1)
                    elif c % 2:
                        ins.then_inc(S["wo_done"], 1)
                norm(2 * l + 1)
                w_rt = piece(("router", l, 0))
                for g in range(G):
                    ins = project(4, g * E, tok(g), lambda k: w_rt[:, k * E:k * E + E],
                                  fresh=2 * l + 1 if g == 0 else None)
                ins.then_inc(S["weights_used"], 1)
                for g in range(G):
                    for c in range(NC_):
                        ins = turn(PS[:, 2 * g + c // 4, (c % 4) * P:(c % 4) * P + P], hT[:, c, g * P:g * P + P])
                    ins.then_inc(S["t_h"], 1)
                w = piece(("shared", l, 0)).rearrange("p (u k t j) -> p u k j t", u=2, k=NC_, j=2)
                pe.wait_ge(S["std_ready"], 2 * l + 2)
                for u in range(2):
                    for j in range(2):
                        ins = project(5 + u, j * T, lambda k: w[:, u, k, j], all_tok)
                ins.then_inc(S["weights_used"], 1)
                pe.wait_ge(S["routed"], l + 1)
                mmul(PS[:, 4, 0:E], C("before"), mask[:, 0], start=True, stop=True)
                mmul(PS[:, 4, E:2 * E], C("ones"), mask[:, 0], start=True, stop=False)
                mmul(PS[:, 4, E:2 * E], C("before"), mask[:, 1], start=False, stop=True)
                mmul(PS[:, 4, 2 * E:3 * E], C("ones"), mask[:, 0], start=True, stop=False)
                mmul(PS[:, 4, 2 * E:3 * E], C("ones"), mask[:, 1], start=False, stop=True).then_inc(S["rank_done"], 1)
                pe.wait_ge(dn_loaded[RING - 1], dloaded[("shared", l, 0)])
                pe.wait_ge(S["sh_h"], l + 1)
                pe.wait_ge(S["part_a"], 6 * l + 6)
                wd = dn[:, RING - 1].rearrange("p j (t c) -> p j c t", c=NC_)
                for c in range(NC_):
                    for j in range(2):
                        ins = mmul(PS[:, c // 2, (c % 2) * T:(c % 2) * T + T], wd[:, j, c], shh[:, j],
                                   start=(j == 0 and c % 2 == 0), stop=False, skip_group_check=True)
                ins.then_inc(S["down_free"], 1)

                g0 = (PAIRS + 1) * l

                def gather(half):
                    for c in range(4 * half, 4 * half + 4):
                        for g in range(G):
                            for s in range(3):
                                ins = mmul(PS[:, 4, (c % 4) * P:(c % 4) * P + P], h3[:, g, s, c], onehot[:, g],
                                           start=(g == 0 and s == 0), stop=(g == 1 and s == 2))
                    return ins

                def scatter():
                    for c in range(NC_):
                        ins = mmul(PS[:, c // 2, (c % 2) * T:(c % 2) * T + T], yy.rearrange("p (t c) -> p c t", c=NC_)[:, c],
                                   hs[:, 256:512], start=False, stop=False, skip_group_check=True)
                    return ins

                def turn_pair():
                    for j in range(2):
                        turn(PS[:, 6, j * P:j * P + P], hh.rearrange("p (t j) -> p j t", j=2)[:, j])
                    for g in range(G):
                        ins = turn(PS[:, 6, (2 + g) * P:(3 + g) * P], gated[:, g])
                    return ins

                pe.wait_ge(S["pos_ready"], l + 1)
                pe.wait_ge(S["sel_ready"], (PAIRS + 2) * l + 1)
                gather(0).then_inc(S["gathered"], 1)
                pe.wait_ge(S["xg_a"], g0 + 1)
                gather(1).then_inc(S["gathered"], 1)
                with pe.Fori(0, PAIRS // 2) as m:
                    for q in range(2):
                        pe.wait_ge(S["xg_b"], m * 2 + (g0 + q + 1))
                        pe.wait_ge(S["xg_a"], m * 2 + (g0 + q + 1))
                        pe.wait_ge(S["hid_ready"], m * 2 + (PAIRS * l + q + BEFORE))
                        for h in range(2):
                            pe.wait_ge(gu_loaded[gu_slot(l, 2 * q + h)], m * 32 + loaded_at[("expert", l, 2 * q + h)])
                        guv = [gu[:, gu_slot(l, 2 * q + h), :].rearrange("p (u k n) -> p k u n", u=2, k=NC_) for h in range(2)]
                        for k in range(NC_):
                            for h in range(2):
                                ins = mmul(PS[64 * h:64 * h + 64, 5, :], xg[:, k, 64 * h:64 * h + 64], guv[h][:, k],
                                           start=(k == 0), stop=(k == NC_ - 1))
                                if k == NC_ - 1:
                                    ins.then_inc(S["weights_used"], 1)
                        pe.wait_ge(S["sel_ready"], m * 2 + ((PAIRS + 2) * l + q + 2))
                        gather(0).then_inc(S["gathered"], 1)
                        pe.wait_ge(S["y_a"], m * 2 + (PAIRS * l + q + BEFORE))
                        pe.wait_ge(S["y_b"], m * 2 + (PAIRS * l + q + BEFORE))
                        if q == 0:
                            pe.wait_ge(S["zeroed"], l + 2)
                        scatter()
                        pe.wait_ge(S["hid_ready"], m * 2 + (PAIRS * l + q + 1 + BEFORE))
                        pe.wait_ge(S["gated_ready"], m * 2 + (g0 + q + 1))
                        turn_pair().then_inc(S["turned"], 1)
                        pe.wait_ge(S["xg_a"], m * 2 + (g0 + q + 2))
                        gather(1).then_inc(S["gathered"], 1)
                        pe.wait_ge(S["hs_ready"], m * 2 + (PAIRS * l + q + 1))
                        for h in range(2):
                            slot = 2 * q + h
                            pe.wait_ge(dn_loaded[slot], m * 16 + dloaded[("expert", l, slot)])
                        for n in range(2):
                            for j in range(2):
                                for h in range(2):
                                    ins = mmul(PS[64 * h:64 * h + 64, 7 - n, :], hs[:, j * P + 64 * h:j * P + 64 * h + 64],
                                               dn[:, 2 * q + h, j, 512 * n:512 * n + 512], start=(j == 0), stop=(j == 1))
                                    if n == 0 and j == 1 and h == 1:
                                        ins.then_inc(S["down_a"], 1)
                                    if n == 1 and j == 1:
                                        ins.then_inc(S["down_free"], 1)
                pe.wait_ge(S["y_a"], PAIRS * (l + 1) + BEFORE)
                pe.wait_ge(S["y_b"], PAIRS * (l + 1) + BEFORE)
                scatter()
                o = ov[l]
                pe.wait_ge(S["xg_b"], (PAIRS + 1) * (l + 1))
                with pe.If(over_flag(pe, l) > 0):
                    with pe.Fori(0, E) as e:
                        for w in range(OW):
                            pe.wait_ge(o["sel"], e * OW + (w + 1))
                            pe.wait_ge(o["xg"], e * (2 * OW) + (2 * w + BEFORE))
                            gather(0).then_inc(o["gath"], 1)
                            pe.wait_ge(o["xg"], e * (2 * OW) + (2 * w + 1 + BEFORE))
                            gather(1).then_inc(o["gath"], 1)
                            pe.wait_ge(o["xg"], e * (2 * OW) + (2 * w + 2 + BEFORE))
                            pe.wait_ge(o["hid"], e * OW + (w + BEFORE))
                            pe.wait_ge(o["w"], e * 48 + 48)
                            guv = gu[:, 0, :].rearrange("p (u k n) -> p k u n", u=2, k=NC_)
                            for k in range(NC_):
                                ins = mmul(PS[:, 5, :], xg[:, k], guv[:, k], start=(k == 0), stop=(k == NC_ - 1))
                            ins.then_inc(o["up"], 1)
                            pe.wait_ge(o["hid"], e * OW + (w + 1 + BEFORE))
                            pe.wait_ge(o["y"], e * (2 * OW) + (2 * w + BEFORE))
                            turn_pair().then_inc(o["turn"], 1)
                            pe.wait_ge(o["hs"], e * OW + (w + 1))
                            for n in range(2):
                                for j in range(2):
                                    ins = mmul(PS[:, 7 - n, :], hs[:, j * P:j * P + P],
                                               dn[:, 0, j, 512 * n:512 * n + 512], start=(j == 0), stop=(j == 1))
                                ins.then_inc(o["down"], 1)
                            pe.wait_ge(o["y"], e * (2 * OW) + (2 * w + 2 + BEFORE))
                            scatter().then_inc(o["comb"], 1)
                mmul(PS[:, 6, 0:2], ident, col("sel", 2), start=True, stop=True).then_inc(S["combined"], 1)
            for g in range(G):
                for c in range(NC_):
                    if g == 0 and c % 2 == 0:
                        pe.wait_ge(S["x_bank"], x_banks(2 * DEPTH - 1) + c // 2 + 1)
                    ins = turn(PS[:, 4 + 2 * g + c // 4, (c % 4) * P:(c % 4) * P + P], xT[:, c, g * P:g * P + P])
                    if c % 4 == 3:
                        ins.then_inc(S["turned_y"], 1)


_OUTS = [("y_prompt", (1, P, D)), ("y_sample", (1, P, D)), ("diff_k", (1, DEPTH, DIF_H, P, 2 * DIF_D)),
         ("diff_v", (1, DEPTH, DIF_H, P, DIF_V)), ("mla_ckv", (1, DEPTH, P, KV_LORA)),
         ("mla_kpe", (1, DEPTH, P, MLA_R)), ("ret_fwd", (1, DEPTH, RET_H, RET_D, RET_D)),
         ("ret_bwd", (1, DEPTH, RET_H, RET_D, RET_D))]


def kernel(**inputs):
    import concourse.bacc as bacc
    from concourse.bass_utils import run_bass_kernel_spmd

    nc = bacc.Bacc("TRN2", target_bir_lowering=False, num_devices=1)
    arrays, t, out = {}, {}, {}
    for name, value in [*inputs.items(), ("shape_consts", shape_constants())]:
        a = np.ascontiguousarray(value)
        arrays[f"in_{name}"] = a
        t[name] = nc.dram_tensor(f"in_{name}", a.shape, mybir.dt.from_np(a.dtype), kind="ExternalInput").ap()
    for name, shape in _OUTS:
        out[name] = nc.dram_tensor(f"out_{name}", shape, F32, kind="ExternalOutput").ap()
    trunk(nc, t, out)
    r = run_bass_kernel_spmd(nc, [arrays], core_ids=[0])
    return tuple(r.results[0][f"out_{name}"] for name, _ in _OUTS)
```

```python
import math
from contextlib import ExitStack

import numpy as np

import concourse.bass as bass
from concourse import mybir

F32 = mybir.dt.float32
BF16 = mybir.dt.bfloat16
I32 = mybir.dt.int32
U32 = mybir.dt.uint32
ALU = mybir.AluOpType
ACT = mybir.ActivationFunctionType
AX = mybir.AxisListType

P = 128
D = 1024
NC_ = D // P
G = 2
T = G * P
DEPTH = 2
EPS = 1e-6
GRID_W = 64
ROPE_THETA = 10000.0

RET_H, RET_D = 4, 64
DIF_H, DIF_D, DIF_V = 4, 32, 64
MLA_H, MLA_N, MLA_R, MLA_V = 8, 64, 32, 64
MLA_QK = MLA_N + MLA_R
Q_LORA, KV_LORA = 256, 128
IN_W = 2208

E = 64
GROUPS = 8
TOP_G, TOP_K = 4, 6
FF = 256
ROUTED_SCALE = 2.5
CAP = 64
PAIRS = E // 2
EARLY = E - 3

CONSTS = ["ident", "ones", "rot_d", "rot_m", "cos_d", "sin_d", "cos_m", "sin_m", "fwd", "bwd", "before", "iota", "cols"]
CO = {n: P * i for i, n in enumerate(CONSTS)}
COL = {"i+1": 0, "C-i": 1, "C-1-i": 2, "i": 3, "eps": 4, "sel": 5}


def shape_constants():
    a = np.zeros((P, len(CONSTS), P), np.float32)
    i = np.arange(P)
    a[:, 0] = np.eye(P)
    a[:, 1] = 1.0

    def tables(n_heads, lead, dim):
        freqs = ROPE_THETA ** (-np.arange(0, dim // 2, 2, dtype=np.float32) / (dim // 2))
        ar = (i // GRID_W)[:, None] * freqs[None, :].astype(np.float32)
        ac = (i % GRID_W)[:, None] * freqs[None, :].astype(np.float32)
        ang = np.concatenate([ar, ar, ac, ac], axis=-1).astype(np.float32)
        rot = np.zeros((P, P), np.float32)
        cos, sin = np.zeros((P, P), np.float32), np.zeros((P, P), np.float32)
        cos[:lead], q = 1.0, dim // 4
        for h in range(n_heads):
            o = lead + h * dim
            cos[o:o + dim], sin[o:o + dim] = np.cos(ang).T, np.sin(ang).T
            for k in range(q):
                rot[o + q + k, o + k] = -1.0
                rot[o + k, o + q + k] = 1.0
                rot[o + 3 * q + k, o + 2 * q + k] = -1.0
                rot[o + 2 * q + k, o + 3 * q + k] = 1.0
        return rot, cos, sin

    a[:, 2], a[:, 4], a[:, 5] = tables(P // DIF_D, 0, DIF_D)
    a[:, 3], a[:, 6], a[:, 7] = tables(1, MLA_N, MLA_R)
    a[:, 8] = np.maximum(i[None, :] - i[:, None], 0)
    a[:, 9] = np.maximum(i[:, None] - i[None, :], 0)
    a[:, 10] = i[:, None] < i[None, :]
    a[:, 11] = i[None, :]
    a[:, 12, 0], a[:, 12, 1], a[:, 12, 2], a[:, 12, 3], a[:, 12, 4] = i + 1, P - i, P - 1 - i, i, EPS
    a[:, 12, 5], a[:, 12, 6] = i % 32 == 0, i % 32 == 1
    return a.reshape(P, len(CONSTS) * P)


ADA_AT = [[[4], [5], [6], [7], [8], [9], [10, 11], [12], [13], [14, 15]],
          [[], [], [], [], [18], [19], [20, 21], [22], [], [23]]]
ADA_NORM = {1: 16, 2: 17}
ADA_BY = [16, 24]


def stream_items():
    out = []
    for l in range(DEPTH):
        if l == 0:
            out += [("ada", n // 12, n % 12) for n in range(4)]
        if 2 * l in ADA_NORM:
            out.append(("ada", 1, ADA_NORM[2 * l] % 12))
        for k in range(5):
            out.append(("w_in", l, k))
            out += [("ada", n // 12, n % 12) for n in ADA_AT[l][k]]
        out += [("ada", n // 12, n % 12) for n in ADA_AT[l][5]] + [("mla", l, 0)]
        out += [("ada", n // 12, n % 12) for at in ADA_AT[l][6:] for n in at]
        out += [("w_out", l, 0), ("w_out", l, 1)]
        if 2 * l + 1 in ADA_NORM:
            out.append(("ada", 1, ADA_NORM[2 * l + 1] % 12))
        out.append(("shared", l, 0))
        out += [("expert", l, e) for e in range(E)]
    return out


def trunk(nc, t, out):
    ctx = ExitStack()
    with ctx:
        def sb(name, shape, dt=F32):
            return ctx.enter_context(nc.sbuf_tensor(name, shape, dt))

        def sem(name):
            return ctx.enter_context(nc.semaphore(name))

        RING = 4
        gu = sb("gu", [P, RING, 2 * NC_ * FF])
        dn = sb("dn", [P, RING, 2, D])
        cst = sb("cst", [P, len(CONSTS) * P])
        xT = sb("xT", [P, NC_, T])
        hT = sb("hT", [P, NC_, T])
        xn = sb("xn", [P, NC_, T])
        rows = sb("rows", [P, DEPTH, 64 + 64 + KV_LORA + Q_LORA + 128 + 8])
        gains = sb("gains", [P, 4, NC_])
        b_ada = sb("b_ada", [P, DEPTH, 6, NC_])
        cond = sb("cond", [P, G, NC_])
        condw = sb("condw", [P, NC_, 32])
        mod = sb("mod", [P, DEPTH, 6, NC_, G])
        amp = sb("amp", [P, 2, NC_, G])
        rada = sb("rada", [P, 512])
        s0 = sb("s0", [P, DEPTH, 2, 2, RET_D])
        ck = sb("ck", [P, DEPTH, DIF_H, 2 * DIF_D])
        cv = sb("cv", [P, DEPTH, DIF_H, DIF_V])
        cl = sb("cl", [P, DEPTH, KV_LORA])
        cr = sb("cr", [P, DEPTH, MLA_QK])
        w_rt = ck[:, :, :, :].rearrange("p l h d -> p (l h d)")
        ckT = sb("ckT", [P, DEPTH, 2, P])
        clT = sb("clT", [P, DEPTH, P])
        crT = sb("crT", [MLA_QK, DEPTH, P])
        dec = sb("dec", [P, DEPTH, 8])
        decv = sb("decv", [P, 4, 4])
        nlam = sb("nlam", [P, DEPTH])
        small = sb("small", [P, 512])
        arena = sb("arena", [P, 14656])
        flag_i = sb("flag_i", [1, DEPTH], I32)

        at = [0]

        def carve(n, name=None):
            at[0] += n
            assert at[0] <= 14656, at[0]
            return arena[:, at[0] - n:at[0]]

        def split(ap, *sizes):
            o, parts = 0, []
            for n in sizes:
                parts.append(ap[:, o:o + n])
                o += n
            return parts

        keys = carve(MLA_H * 3 * P)
        kmT = keys.rearrange("p (h k t) -> p h k t", h=MLA_H, k=3)
        a_q, a_k, a_s, a_cqn, a_cqT = split(keys, 2 * T, 2 * T, 8 * P, G * Q_LORA, 2 * T)
        qT = a_q.rearrange("p (c t) -> p c t", c=2)
        kT = a_k.rearrange("p (c t) -> p c t", c=2)
        sT = a_s.rearrange("p (b g m t) -> p b g m t", b=2, g=G, m=2)
        cqn = a_cqn.rearrange("p (g n) -> p g n", g=G)
        cqT = a_cqT.rearrange("p (c t) -> p c t", c=2)
        values = carve(3 * 512)
        vm = values.rearrange("p (k n) -> p k n", k=3)
        a_v, a_x, a_kd = split(values, G * 256, 4 * P, 2 * 256)
        v_tok = a_v.rearrange("p (g n) -> p g n", g=G)
        cross = a_x.rearrange("p (h d e) -> p h d e", h=4, d=2)
        kdec = a_kd.rearrange("p (d n) -> p d n", d=2)
        rgate = carve(G * 256).rearrange("p (g n) -> p g n", g=G)
        dqT = carve(2 * T).rearrange("p (c t) -> p c t", c=2)
        dkT = carve(2 * 3 * P).rearrange("p (c k t) -> p c k t", c=2, k=3)
        dv_tok = carve(G * 256).rearrange("p (g n) -> p g n", g=G)
        ckvn = carve(G * KV_LORA).rearrange("p (g n) -> p g n", g=G)
        kpe = carve(G * MLA_QK).rearrange("p (g n) -> p g n", g=G)
        ckvT = carve(3 * P).rearrange("p (k t) -> p k t", k=3)
        kpeT = carve(3 * P).rearrange("p (k t) -> p k t", k=3)
        qmT = carve(MLA_H * T).rearrange("p (h t) -> p h t", h=MLA_H)
        kv_out = carve(2 * 4 * RET_D).rearrange("p (d h e) -> p d h e", d=2, h=4)
        dk_tok = carve(256)
        mix = carve(G * D).rearrange("p (g n) -> p g n", g=G)
        work = carve(512)
        rtmp = carve(2 * 512).rearrange("p (a n) -> p a n", a=2)
        dmat = rtmp[:, 1].rearrange("p (b m t) -> p b m t", b=2, m=2)
        prob = xn[:, :, :].rearrange("p c t -> p (c t)").rearrange("p (m k) -> p m k", m=8)
        probT = hT[:, :, :].rearrange("p c t -> p (c t)").rearrange("p (m k t) -> p m k t", m=8, k=2)
        mixT = xn
        at[0] = 0
        h3 = carve(G * 3 * D // 2).bitcast(BF16).rearrange("p (g s c t) -> p g s c t", g=G, s=3, c=NC_)
        rem = carve(2 * D).rearrange("p (a n) -> p a n", a=2)
        xg = carve(NC_ * P).rearrange("p (c t) -> p c t", c=NC_)
        sact = carve(256)
        hh = carve(256)
        hidT = carve(256)
        selT = carve(G * P // 2).bitcast(BF16)
        slot_gate = carve(2)
        identb = carve(P // 2).bitcast(BF16)
        yy = carve(D)
        ypart = [rem[:, 1, 0:512].bitcast(BF16), rem[:, 1, 512:1024].bitcast(BF16), carve(D // 2).bitcast(BF16)]
        shs = carve(2 * T).rearrange("p (j t) -> p j t", j=2)
        shh = carve(2 * T).rearrange("p (j t) -> p j t", j=2)
        score = carve(G * E).rearrange("p (g e) -> p g e", g=G)
        selv = carve(G * E).rearrange("p (g e) -> p g e", g=G)
        gtop = carve(G * 64).rearrange("p (g a b) -> p g a b", g=G, a=GROUPS)
        gsc = carve(G * 8).rearrange("p (g a) -> p g a", g=G)
        top8 = carve(G * 8).rearrange("p (g a) -> p g a", g=G)
        idx8 = carve(G * 8).bitcast(U32).rearrange("p (g a) -> p g a", g=G)
        idxf = carve(G * 8).rearrange("p (g a) -> p g a", g=G)
        hit = carve(G * E * 8)
        gmask = carve(G * 8).rearrange("p (g a) -> p g a", g=G)
        mask = carve(G * E).rearrange("p (g e) -> p g e", g=G)
        gsum = carve(8)
        pos = carve(G * (E + 4)).rearrange("p (e g) -> p e g", g=G)
        wgt = carve(G * (E + 4)).rearrange("p (e g) -> p e g", g=G)
        onehot = [carve(G * P // 2).bitcast(BF16).rearrange("p (g s) -> p g s", g=G) for _ in range(2)]
        gated = carve(G * P).rearrange("p (g s) -> p g s", g=G)
        fl = carve(8)
        early_gate = xn[:, :, :].rearrange("p c t -> p (c t)")
        early_up = carve(NC_ * FF)
        early_down = hT[:, :, :].rearrange("p c t -> p (c t)")

        PS = ctx.enter_context(nc.psum_tensor("PS", [P, 8, 512], F32))

        def C(name, w=P, parts=P):
            return cst[0:parts, CO[name]:CO[name] + w]

        def col(name, w=1):
            o = CO["cols"] + COL[name]
            return cst[:, o:o + w]

        ident = C("ident")

        def r_bias(l):
            return rows[:, l, 0:64]

        def r_subln(l):
            return rows[:, l, 64:128]

        def r_kvn(l):
            return rows[:, l, 128:128 + KV_LORA]

        def r_qn(l):
            return rows[:, l, 256:256 + Q_LORA]

        def r_lam(l):
            return rows[:, l, 512:640]

        def r_dec(l):
            return rows[:, l, 640:648]

        def bc(ap, axis, n):
            u = ap.unsqueeze(axis)
            s = list(u.shape)
            s[axis] = n
            return u.to_broadcast(s)

        names = """const_in x_in mod_in small_in gain_in router_in router_done early_in weights_used down_free store_done
            cond_ready turned_x xT_a xT_d setup_evict_a setup_evict_d caches_placed
            ada_r ada_sel ada_mod
            sq_ready ss_ready std_ready xn_ready h_a h_d amp_ready
            proj q_ready k_ready rg_exp rv_ready dq_ready dk_ready cq_sq cqn_ready ckv_sq ckvn_ready
            decay_rate decay_args decays_ready lam_arg lam_exp
            t_cq t_ckv t_kpe cqT_ready ckvT_ready kpeT_ready
            ret_s sT_ready ret_x cross_ready t_k ktok_ready d_rot d_roped uq qm_ready
            ret_o ret_sum ret_std kv_p kv_ready kpe_rot kpe_roped q_rot q_roped
            ukv_k km_a km_d ukv_v vm_ready
            s_ready nb_ready exp_done pt_turned pt_even pt_odd pv_done o_done dif_sum dif_std
            t_mix mixT_a mixT_d wo_done x_bank
            sig_exp routed rank_done pos_ready flag_ready t_h part_a part_d sh_gate sh_silu sh_h
            zeroed sel_ready gated_ready gathered xg_a xg_b silu_ready hid_ready turned turn_out down_a parts_act parts_dve
            combined
            turned_y y_sq y_ms y_std y_done act_own dve_own""".split()
        S = {n: sem(n) for n in names}
        gu_loaded = [sem(f"gu_loaded{j}") for j in range(RING)]
        dn_loaded = [sem(f"dn_loaded{j}") for j in range(RING)]
        ov = [{n: sem(f"over{l}_{n}") for n in
               "w sel gath xg up silu hid turn out down parts_act parts_dve comb".split()} for l in range(DEPTH)]

        items = stream_items()
        number = {it: n for n, it in enumerate(items)}
        first_expert = [number[("expert", l, 0)] for l in range(DEPTH)]

        def gu_slot(l, e4):
            return (first_expert[l] + e4) % RING
        loaded_at, cum, dcum, dloaded = {}, [0] * RING, [0] * RING, {}
        for n, it in enumerate(items):
            if it == ("expert", it[1], EARLY):
                continue
            cum[n % RING] += 32 if it[0] in ("shared", "expert", "mla") else 16
            loaded_at[it] = cum[n % RING]
            if it[0] == "shared":
                dcum[RING - 1] += 16
                dloaded[it] = dcum[RING - 1]
            if it[0] == "expert":
                dcum[it[2] % RING] += 16
                dloaded[it] = dcum[it[2] % RING]
        UQ, UKV = 2 * MLA_H * MLA_QK, MLA_H * (MLA_N + MLA_V)
        DN_PER = E + 1
        DN0 = 3

        def w_ada_view(it):
            _, l, q = it
            return t["w_ada"][l].rearrange("(p c) n -> p c n", c=NC_)[:, :, q * 512:(q + 1) * 512]

        items_ada = [("ada", n // 12, n % 12) for n in range(12 * DEPTH)]
        ada_first = (0, 4, 16)
        stores_in_layer = 6
        small_total = 16 * (4 + 4 * DEPTH + DEPTH * 7)
        mod_total = 16 * 3 * DEPTH

        def ada_here(step, l, k):
            for n in ADA_AT[l][k]:
                step(n)

        def projected(eng, l, k, part):
            if part == 0:
                eng.wait_ge(S["proj"], 4 * l + k + 1)
            else:
                eng.wait_ge(S["weights_used"], number[("w_in", l, k)] + 1)

        def x_banks(k):
            return 4 * k

        def k_bank(h):
            return (3, 4, 5, 0, 1, 2, 3, 4)[h]

        def wo_bank(c):
            return (4, 5, 0, 1)[c // 2]

        def pt_before(U):
            return 12 * (U // 4) + (0, 2, 6, 8)[U % 4]

        def half_before(U):
            return pt_before(U) // 2

        def pt_view(b, nk):
            if nk == 2:
                return probT[:, 2 * b:2 * b + 2].rearrange("p m k t -> p (m k) t")
            return probT[:, 4 * b:4 * b + 4, 0, :]

        def chain(eng, own):
            count = [0]

            def link(ins):
                count[0] += 1
                ins.then_inc(own, 1)
                eng.wait_ge(own, count[0])

            told = {}

            def settle(name):
                told[name] = told.get(name, 0) + 1
                eng.wait_ge(S[name], told[name])
            return link, settle

        def over_flag(eng, l):
            eng.wait_ge(S["flag_ready"], l + 1)
            return eng.value_load(flag_i[0:1, l:l + 1], min_val=0, max_val=1)

        BEFORE = 1
        OW = 2

        def over_loads(sp, l):
            o = ov[l]
            with sp.If(over_flag(sp, l) > 0):
                sp.wait_ge(S["weights_used"], first_expert[l] + E)
                sp.wait_ge(S["down_free"], DN0 + DN_PER * (l + 1))
                with sp.Fori(0, E) as e:
                    sp.wait_ge(o["comb"], e * OW + BEFORE)
                    for half, name in enumerate(("gate", "up")):
                        sp.dma_start(gu[:, 0, half * NC_ * FF:(half + 1) * NC_ * FF],
                                     t[f"exp_w_{name}"][l, bass.ds(e, 1)].rearrange("e (p c) n -> (e p) (c n)", c=NC_)
                                     ).then_inc(o["w"], 16)
                    sp.dma_start(dn[:, 0].rearrange("p j n -> p (j n)"),
                                 t["exp_w_down"][l, bass.ds(e, 1)].rearrange("e (p j) n -> (e p) (j n)", j=2)
                                 ).then_inc(o["w"], 16)
                sp.wait_ge(o["comb"], E * OW + BEFORE)

        block = ctx.enter_context(nc.Block())

        @block.sync
        def _(sp):
            def load_expert_gu(slot, l, e, shared=False):
                for half, name in enumerate(("gate", "up")):
                    if shared:
                        src = t[f"sh_w_{name}"][l].rearrange("(p c) n -> p (c n)", c=NC_)
                    else:
                        src = t[f"exp_w_{name}"][l, e].rearrange("e (p c) n -> (e p) (c n)", c=NC_)
                    dst = gu[:, slot, half * NC_ * FF:(half + 1) * NC_ * FF]
                    sp.dma_start(dst, src).then_inc(gu_loaded[slot], 16)

            def load_expert_dn(slot, l, e, shared=False):
                if shared:
                    src = t["sh_w_down"][l].rearrange("(p j) n -> p (j n)", j=2)
                else:
                    src = t["exp_w_down"][l, e].rearrange("e (p j) n -> (e p) (j n)", j=2)
                sp.dma_start(dn[:, slot].rearrange("p j n -> p (j n)"), src).then_inc(dn_loaded[slot], 16)

            def small_loads():
                n_small = [0]

                def load(dst, src):
                    sp.dma_start(dst, src).then_inc(S["small_in"], 16)
                    n_small[0] += 1
                load(ck[:, :, :, :], t["cache_diff_k"][0].rearrange("l h t d -> t l h d"))
                load(cv[:, :, :, :], t["cache_diff_v"][0].rearrange("l h t d -> t l h d"))
                load(cl[:, :, :], t["cache_mla_ckv"][0].rearrange("l t d -> t l d"))
                sp.wait_ge(S["zeroed"], 1)
                load(cr[:, :, MLA_N:], t["cache_mla_kpe"][0].rearrange("l t d -> t l d"))
                for d, name in enumerate(("state_ret_fwd", "state_ret_bwd")):
                    for b in range(2):
                        for l in range(DEPTH):
                            load(s0[64 * b:64 * b + 64, l, :, d, :],
                                 t[name][0, l].rearrange("(m b) d e -> b d m e", b=2)[b])
                for l in range(DEPTH):
                    for dst, src in ((r_bias(l), t["router_bias"][l]), (r_subln(l), t["diff_subln"][l]),
                                     (r_kvn(l), t["mla_kv_norm"][l]), (r_qn(l), t["mla_q_norm"][l]),
                                     (r_lam(l), t["diff_lambda"][l].rearrange("a b -> (a b)")),
                                     (r_dec(l)[:, 0:4], t["ret_decay_fwd"][l]), (r_dec(l)[:, 4:8], t["ret_decay_bwd"][l])):
                        load(dst, src.partition_broadcast(P))
                assert 16 * n_small[0] == small_total

            x_tok = arena[:, 0:G * D].rearrange("p (g n) -> p g n", g=G)
            sp.dma_start(x_tok[:, 0], t["x_prompt"][0]).then_inc(S["const_in"], 16)
            sp.dma_start(x_tok[:, 1], t["x_sample"][0]).then_inc(S["const_in"], 16)
            sp.dma_start(cst[:, :], t["shape_consts"]).then_inc(S["const_in"], 16)

            def load(dst, src, s):
                sp.dma_start(dst, src).then_inc(S[s], 16)
            for g, name in enumerate(("c_ctx", "c")):
                src = t[name] if name == "c_ctx" else t[name].rearrange("a d -> (a d)")
                load(cond[:, g], src.rearrange("(p c) -> p c", c=NC_), "x_in")
            for l in range(DEPTH):
                load(b_ada[:, l], t["b_ada"][l].rearrange("(s p c) -> p s c", p=P, c=NC_), "mod_in")
                load(gains[:, l], t["norm_mix"][l].rearrange("(p c) -> p c", c=NC_), "mod_in")
                load(gains[:, 2 + l], t["norm_ffn"][l].rearrange("(p c) -> p c", c=NC_), "mod_in")
            for l in range(DEPTH):
                for n in range(first_expert[l - 1] + E if l > 0 else 0, first_expert[l]):
                    it = items[n]
                    if n == RING + 1:
                        small_loads()
                    if n >= RING:
                        sp.wait_ge(S["weights_used"], n - RING + 1)
                    slot = n % RING
                    if it[0] == "ada":
                        src = w_ada_view(it)
                        dst = gu[:, slot, :].rearrange("p (c n) -> p c n", c=NC_)
                        sp.dma_start(dst, src).then_inc(gu_loaded[slot], 16)
                    elif it[0] == "w_in":
                        w = min(512, IN_W - 512 * it[2])
                        src = t["w_in"][l].rearrange("(p c) n -> p c n", c=NC_)[:, :, 512 * it[2]:512 * it[2] + w]
                        dst = gu[:, slot, 0:NC_ * w].rearrange("p (c n) -> p c n", c=NC_)
                        sp.dma_start(dst, src).then_inc(gu_loaded[slot], 16)
                    elif it[0] == "w_out":
                        if it[2] == 0:
                            sp.wait_ge(S["turned_x"], 3)
                            if l > 0:
                                sp.wait_ge(S["router_done"], l)
                            sp.dma_start(w_rt, t["router_w"][l].rearrange("(p c) n -> p (c n)", c=NC_)
                                         ).then_inc(S["router_in"], 16)
                        src = t["w_out"][l, 512 * it[2]:512 * it[2] + 512].rearrange("(k p) n -> p k n", p=P)
                        dst = gu[:, slot, :].rearrange("p (k n) -> p k n", k=4)
                        sp.dma_start(dst, src).then_inc(gu_loaded[slot], 16)
                    elif it[0] == "mla":
                        sp.dma_start(gu[:, slot, 0:UQ].rearrange("p (k n) -> p k n", k=2),
                                     t["mla_w_uq"][l].rearrange("(k p) n -> p k n", p=P)).then_inc(gu_loaded[slot], 16)
                        sp.dma_start(gu[:, slot, UQ:UQ + UKV], t["mla_w_ukv"][l]).then_inc(gu_loaded[slot], 16)
                    else:
                        load_expert_gu(slot, l, 0, shared=True)
                        if l > 0:
                            sp.wait_ge(S["down_free"], DN0 + DN_PER * l)
                        load_expert_dn(RING - 1, l, 0, shared=True)

                def ring_gu(m, e4):
                    sp.wait_ge(S["weights_used"], m * RING + (first_expert[l] + e4 - RING + 1))
                    load_expert_gu(gu_slot(l, e4), l, bass.ds(m * RING + e4, 1))

                def ring_dn(m, e4):
                    sp.wait_ge(S["down_free"], m * RING + (DN_PER * l + 1 + e4))
                    load_expert_dn(e4, l, bass.ds(m * RING + e4, 1))

                ring_gu(0, 0)
                ring_gu(0, 1)
                ring_dn(0, 0)
                ring_dn(0, 1)
                ring_gu(0, 2)
                ring_dn(0, 2)
                sp.wait_ge(S["h_a"], NC_ * (2 * l + 2))
                sp.wait_ge(S["h_d"], NC_ * (2 * l + 2))
                for dst, name in ((early_gate, "gate"), (early_up, "up")):
                    sp.dma_start(dst, t[f"exp_w_{name}"][l, EARLY].rearrange("(p c) n -> p (c n)", c=NC_)
                                 ).then_inc(S["early_in"], 16)
                ring_gu(0, 3)
                sp.dma_start(early_down, t["exp_w_down"][l, EARLY].rearrange("(p j) n -> p (j n)", j=2)
                             ).then_inc(S["early_in"], 16)
                ring_dn(0, 3)
                with sp.Fori(1, E // RING - 1) as m:
                    for q in range(2):
                        for h in range(2):
                            ring_gu(m, 2 * q + h)
                        for h in range(2):
                            ring_dn(m, 2 * q + h)
                last = E // RING - 1
                ring_gu(last, 0)
                ring_dn(last, 0)
                ring_gu(last, 2)
                ring_gu(last, 3)
                ring_dn(last, 2)
                ring_dn(last, 3)
                over_loads(sp, l)

        @block.gpsimd
        def _(pool):
            pool.memset(condw[:, :, :], 0.0)
            pool.memset(cr[:, :, :], 0.0).then_inc(S["zeroed"], 1)
            pool.sem_inc(S["down_free"], DN0)
            for name in ("hid_ready", "parts_dve"):
                pool.sem_inc(S[name], BEFORE)
            for o in ov:
                for name in ("comb", "xg", "hid", "parts_dve"):
                    pool.sem_inc(o[name], BEFORE)
            pool.wait_ge(S["const_in"], 48)
            for l in range(DEPTH):
                if l > 0:
                    pool.wait_ge(S["x_bank"], x_banks(2 * l))
                pool.memset(kpe[:, :, 0:MLA_N], 0.0)
                pool.wait_ge(S["setup_evict_d"], 1)
                pool.wait_ge(S["setup_evict_a"], 1)
                pool.tensor_copy(dkT[:, :, 1, :], ckT[:, l])
                pool.tensor_copy(ckvT[:, 1, :], clT[:, l])
                pool.tensor_copy(kpeT[0:MLA_QK, 1, :], crT[:, l]).then_inc(S["caches_placed"], 1)
                pool.wait_ge(S["x_bank"], x_banks(2 * l + 1))
                pool.tensor_copy(identb, ident)
                pool.memset(selT, 0.0)
                pool.wait_ge(S["part_a"], 6 * l + 6)
                for y in ypart:
                    pool.memset(y, 0.0)
                pool.memset(wgt[:, E:E + 4, :], 0.0)
                pool.memset(pos[:, E:E + 4, :], -1.0).then_inc(S["zeroed"], 1)

        @block.scalar
        def _(act):
            link, settle = chain(act, S["act_own"])
            A = nc.scalar.activation
            act.wait_ge(S["x_in"], 32)
            act.wait_ge(S["zeroed"], 1)
            A(condw[:, :, 0:G], cond[:, :, :].rearrange("p g c -> p c g"), ACT.Silu).then_inc(S["cond_ready"], 1)
            settle("cond_ready")
            act.wait_ge(S["turned_x"], 1)
            A(xT[:, :, 0:P], PS[:, 0:2, :].rearrange("p b (c t) -> p (b c) t", c=4), ACT.Copy).then_inc(S["xT_a"], 1)
            settle("xT_a")

            def ada(n):
                act.wait_ge(S["weights_used"], number[items_ada[n]] + 1)
                if n >= 1:
                    act.wait_ge(S["ada_sel"], n)
                A(rada[:, :], PS[:, 7, :], ACT.Copy).then_inc(S["ada_r"], 1)
                settle("ada_r")

            def norm(k):
                for b in range(4):
                    if k == 0:
                        act.wait_ge(S["xT_d"], 1)
                    else:
                        act.wait_ge(S["x_bank"], x_banks(k - 1) + b + 1)
                    A(hT[:, 2 * b:2 * b + 2, :], xT[:, 2 * b:2 * b + 2, :], ACT.Square).then_inc(S["sq_ready"], 1)
                act.wait_ge(S["ss_ready"], k + 1)
                A(small[:, 0:T], PS[:, 6, 0:T], ACT.Sqrt, bias=col("eps"), scale=1.0 / D).then_inc(S["std_ready"], 1)
                if k == 0:
                    for n in range(4):
                        ada(n)
                if k in ADA_NORM:
                    ada(ADA_NORM[k])
                l, w = divmod(k, 2)
                act.wait_ge(S["amp_ready"], k + 1)
                for c in range(NC_):
                    act.wait_ge(S["xn_ready"], NC_ * k + c + 1)
                    A(hT[:, c, 0:P], xn[:, c, 0:P], ACT.Identity, scale=amp[:, w, c, 0:1],
                      bias=mod[:, l, 3 * w, c, 0:1]).then_inc(S["h_a"], 1)

            def prepare(l):
                A(small[:, 260:268], r_dec(l), ACT.Exp).then_inc(S["decay_rate"], 1)
                settle("decay_rate")
                act.wait_ge(S["lam_arg"], l + 1)
                A(small[:, 300:302], small[:, 298:300], ACT.Exp).then_inc(S["lam_exp"], 1)
                settle("lam_exp")
                act.wait_ge(S["decay_args"], l + 1)
                A(decv[:, :, :], decv[:, :, :], ACT.Exp)
                A(dmat, dmat, ACT.Exp).then_inc(S["decays_ready"], 1)
                settle("decays_ready")

            act.wait_ge(S["const_in"], 48)
            for l in range(DEPTH):
                norm(2 * l)
                act.wait_ge(S["small_in"], small_total)
                prepare(l)
                projected(act, l, 0, 0)
                A(qT, PS[:, 0, :].rearrange("p (c t) -> p c t", c=2), ACT.Copy).then_inc(S["q_ready"], 1)
                settle("q_ready")
                projected(act, l, 0, 1)
                A(kT, PS[:, 1, :].rearrange("p (c t) -> p c t", c=2), ACT.Copy,
                  scale=RET_D ** -0.5).then_inc(S["k_ready"], 1)
                settle("k_ready")
                if l == 0:
                    act.wait_ge(S["turned_x"], 4)
                    A(clT[:, :, :], PS[:, 5, 0:2 * P].rearrange("p (l t) -> p l t", l=2), ACT.Copy)
                    A(crT[:, :, :], PS[0:MLA_QK, 5, 2 * P:4 * P].rearrange("p (l t) -> p l t", l=2),
                      ACT.Copy).then_inc(S["setup_evict_a"], 1)
                ada_here(ada, l, 0)
                for g in range(G):
                    projected(act, l, 1, g)
                    A(rgate[:, g], PS[:, 2 + g, 256:512], ACT.Exp, scale=-1.0).then_inc(S["rg_exp"], 1)
                    settle("rg_exp")
                ada_here(ada, l, 1)
                projected(act, l, 2, 0)
                A(dqT, PS[:, 4, :].rearrange("p (c t) -> p c t", c=2), ACT.Copy).then_inc(S["dq_ready"], 1)
                settle("dq_ready")
                ada_here(ada, l, 2)
                for g in range(G):
                    projected(act, l, 3, g)
                    link(A(work[:, 0:256], PS[:, g, 256:512], ACT.Square, accum_out=small[:, 304 + g:305 + g]))
                    A(dv_tok[:, g], PS[:, g, 0:256], ACT.Copy)
                    A(small[:, 306 + g:307 + g], small[:, 304 + g:305 + g], ACT.Sqrt, bias=col("eps"),
                      scale=1.0 / Q_LORA).then_inc(S["cq_sq"], 1)
                    settle("cq_sq")
                ada_here(ada, l, 3)
                act.wait_ge(S["weights_used"], number[("w_in", l, 4)] + 1)
                for g in range(G):
                    link(A(work[:, 0:128], PS[:, 2, 256 * g:256 * g + 128], ACT.Square,
                           accum_out=small[:, 310 + g:311 + g]))
                A(small[:, 312:314], small[:, 310:312], ACT.Sqrt, bias=col("eps"),
                  scale=1.0 / KV_LORA).then_inc(S["ckv_sq"], 1)
                settle("ckv_sq")
                ada_here(ada, l, 4)
                act.wait_ge(S["t_cq"], l + 1)
                A(cqT, PS[:, 3, :].rearrange("p (c t) -> p c t", c=2), ACT.Copy).then_inc(S["cqT_ready"], 1)
                settle("cqT_ready")
                act.wait_ge(S["t_ckv"], l + 1)
                A(ckvT[:, 0:3:2, :], PS[:, 4, 0:2 * P].rearrange("p (k t) -> p k t", k=2),
                  ACT.Copy).then_inc(S["ckvT_ready"], 1)
                settle("ckvT_ready")
                for b in range(4):
                    act.wait_ge(S["uq"], 4 * l + b + 1)
                    A(qmT[0:MLA_QK, 2 * b:2 * b + 2, :], PS[0:MLA_QK, b, :].rearrange("p (h t) -> p h t", h=2),
                      ACT.Copy).then_inc(S["qm_ready"], 1)
                    settle("qm_ready")
                act.wait_ge(S["ret_sum"], l + 1)
                A(small[:, 328:336], small[:, 320:328], ACT.Sqrt, bias=col("eps"),
                  scale=1.0 / RET_D).then_inc(S["ret_std"], 1)
                settle("ret_std")
                act.wait_ge(S["kv_p"], l + 1)
                A(kv_out[0:64], PS[0:64, 5, :].rearrange("p (d h e) -> p d h e", d=2, h=4),
                  ACT.Copy).then_inc(S["kv_ready"], 1)
                settle("kv_ready")
                act.wait_ge(S["kv_ready"], l + 1)
                store_count = [0]

                def store(dst, src):
                    act.dma_start(dst, src).then_inc(S["store_done"], 16)
                    store_count[0] += 1
                for d, name in enumerate(("ret_fwd", "ret_bwd")):
                    store(out[name][0, l].rearrange("h d e -> d h e"), kv_out[0:64, d])
                ada_here(ada, l, 5)
                for h in range(0, MLA_H, 2):
                    act.wait_ge(S["ukv_k"], MLA_H * l + h + 1)
                    A(kmT[0:64, h], PS[0:64, k_bank(h), 0:3 * P].rearrange("p (k t) -> p k t", k=3),
                      ACT.Copy).then_inc(S["km_a"], 1)
                    settle("km_a")
                act.wait_ge(S["ktok_ready"], l + 1)
                act.wait_ge(S["ckvn_ready"], l + 1)
                act.wait_ge(S["cq_sq"], 2 * l + 2)
                store(out["diff_k"][0, l].rearrange("h t d -> t h d"), dk_tok.rearrange("p (h d) -> p h d", h=DIF_H))
                store(out["diff_v"][0, l].rearrange("h t d -> t h d"),
                      dv_tok[:, 0].rearrange("p (h d) -> p h d", h=DIF_H))
                store(out["mla_ckv"][0, l], ckvn[:, 0])
                store(out["mla_kpe"][0, l], kpe[:, 0, MLA_N:])
                assert store_count[0] == stores_in_layer
                for k in range(3):
                    if k < 2:
                        act.wait_ge(S["ukv_v"], 2 * l + k + 1)
                    else:
                        act.wait_ge(S["weights_used"], number[("mla", l, 0)] + 1)
                    A(vm[:, k], PS[:, (5, 0, 1)[k], :], ACT.Copy).then_inc(S["vm_ready"], 1)
                    settle("vm_ready")
                for u in range(4):
                    U = 4 * l + u
                    nk = 1 + u % 2
                    scale = (DIF_D if u < 2 else MLA_QK) ** -0.5
                    act.wait_ge(S["nb_ready"], U + 1)
                    act.wait_ge(S["pt_turned"], pt_before(U))
                    for m in range(8):
                        A(prob[:, m, 0:nk * P], PS[:, m // 2, (m % 2) * 256:(m % 2) * 256 + nk * P], ACT.Exp,
                          bias=small[:, 340 + m:341 + m], scale=scale,
                          accum_out=small[:, 350 + m:351 + m]).then_inc(S["exp_done"], 1)
                        settle("exp_done")
                    ada_here(ada, l, 6 + u)
                    for b in range(1, 2 * nk, 2):
                        act.wait_ge(S["pt_turned"], pt_before(U) + b + 1)
                        A(pt_view(b, nk), PS[:, 5, :].rearrange("p (m t) -> p m t", m=4),
                          ACT.Copy).then_inc(S["pt_odd"], 1)
                        settle("pt_odd")
                    if u in (1, 2):
                        act.wait_ge(S["dif_sum"], 2 * l + u)
                        A(small[:, 472 + 4 * (u - 1):472 + 4 * u], small[:, 464 + 4 * (u - 1):464 + 4 * u], ACT.Sqrt,
                          bias=col("eps"), scale=1.0 / DIF_V).then_inc(S["dif_std"], 1)
                for b in (0, 2):
                    act.wait_ge(S["t_mix"], 4 * l + b + 1)
                    A(mixT[:, 2 * b:2 * b + 2, :], PS[:, b, :].rearrange("p (k t) -> p k t", k=2),
                      ACT.Copy).then_inc(S["mixT_a"], 1)
                    settle("mixT_a")
                norm(2 * l + 1)
                for s in range(3):
                    for g in range(G):
                        if s == 0:
                            act.wait_ge(S["t_h"], 2 * l + g + 1)
                            src = PS[:, 2 * g:2 * g + 2, :].rearrange("p b (c t) -> p (b c) t", c=4)
                        else:
                            act.wait_ge(S["part_d"], 4 * l + 2 * (s - 1) + g + 1)
                            src = rem[:, g].rearrange("p (c t) -> p c t", c=NC_)
                        A(h3[:, g, s], src, ACT.Copy).then_inc(S["part_a"], 1)
                act.wait_ge(S["router_done"], l + 1)
                A(score, PS[:, 4, 0:G * E].rearrange("p (g e) -> p g e", g=G), ACT.Sigmoid).then_inc(S["sig_exp"], 1)
                if l == DEPTH - 1:
                    act.wait_ge(S["part_a"], 6 * l + 6)
                    act.dma_start(rem[:, 0], t["norm_final"].partition_broadcast(P)).then_inc(S["gain_in"], 16)
                act.wait_ge(S["sh_gate"], l + 1)
                A(shs, PS[:, 5, :].rearrange("p (j t) -> p j t", j=2), ACT.Silu).then_inc(S["sh_silu"], 1)
                settle("sh_silu")

                def gated_results(n):
                    half = slice(512 * n, 512 * n + 512)
                    A(yy[:, half], PS[:, 7 - n, :], ACT.Identity, scale=slot_gate[:, 0:1])
                    return A(ypart[0][:, half], PS[:, 7 - n, :], ACT.Identity, scale=slot_gate[:, 0:1])

                def second_part(n):
                    half = slice(512 * n, 512 * n + 512)
                    return A(ypart[1][:, half], yy[:, half], ACT.Copy)
                g0 = (PAIRS + 1) * l
                act.wait_ge(S["gathered"], 2 * g0 + 1)
                A(xg[:, 0:4], PS[:, 4, :].rearrange("p (c t) -> p c t", c=4), ACT.Copy).then_inc(S["xg_a"], 1)
                with act.Fori(0, PAIRS // 2) as m:
                    for q in range(2):
                        act.wait_ge(S["weights_used"], m * 4 + (first_expert[l] + 2 * q + 2))
                        A(sact, PS[:, 5, 0:FF], ACT.Silu).then_inc(S["silu_ready"], 1)
                        act.wait_ge(S["gathered"], m * 4 + (2 * (g0 + q + 1) + 1))
                        A(xg[:, 0:4], PS[:, 4, :].rearrange("p (c t) -> p c t", c=4), ACT.Copy).then_inc(S["xg_a"], 1)
                        for n in range(2):
                            if n == 0:
                                act.wait_ge(S["down_a"], m * 2 + (PAIRS * l + q + 1))
                            else:
                                act.wait_ge(S["down_free"], m * 4 + (DN0 + DN_PER * l + 1 + 2 * q + 2))
                            gated_results(n).then_inc(S["parts_act"], 1)
                        for n in range(2):
                            act.wait_ge(S["parts_dve"], m * 8 + (4 * (PAIRS * l + q) + n + 1 + BEFORE))
                            second_part(n).then_inc(S["parts_act"], 1)
                o = ov[l]
                with act.If(over_flag(act, l) > 0):
                    with act.Fori(0, E) as e:
                        for w in range(OW):
                            act.wait_ge(o["gath"], e * (2 * OW) + (2 * w + 1))
                            A(xg[:, 0:4], PS[:, 4, :].rearrange("p (c t) -> p c t", c=4), ACT.Copy).then_inc(o["xg"], 1)
                            act.wait_ge(o["up"], e * OW + (w + 1))
                            A(sact, PS[:, 5, 0:FF], ACT.Silu).then_inc(o["silu"], 1)
                            for n in range(2):
                                act.wait_ge(o["down"], e * (2 * OW) + (2 * w + n + 1))
                                gated_results(n).then_inc(o["parts_act"], 1)
                            for n in range(2):
                                act.wait_ge(o["parts_dve"], e * (4 * OW) + (4 * w + n + 1 + BEFORE))
                                second_part(n).then_inc(o["parts_act"], 1)
            for b in range(4):
                g, half = divmod(b, 2)
                act.wait_ge(S["turned_y"], b + 1)
                A(hT[:, 2 * b:2 * b + 2, :].rearrange("p c t -> p (c t)"), PS[:, 4 + b, :], ACT.Square,
                  accum_out=small[:, 2 * g + half:2 * g + half + 1]).then_inc(S["y_sq"], 1)
            act.wait_ge(S["y_ms"], 1)
            A(small[:, 6:8], small[:, 4:6], ACT.Sqrt, bias=col("eps"), scale=1.0 / D).then_inc(S["y_std"], 1)
            y_tok = arena[:, 0:G * D].rearrange("p (g n) -> p g n", g=G)
            for g, name in enumerate(("y_prompt", "y_sample")):
                act.wait_ge(S["y_done"], g + 1)
                act.dma_start(out[name][0], y_tok[:, g]).then_inc(S["store_done"], 16)
            act.wait_ge(S["store_done"], 16 * (stores_in_layer * DEPTH + 2))

        @block.vector
        def _(v):
            link, settle = chain(v, S["dve_own"])
            tt, ts, stt = v.tensor_tensor, v.tensor_scalar, v.scalar_tensor_tensor
            v.wait_ge(S["turned_x"], 2)
            v.tensor_copy(xT[:, :, P:T], PS[:, 2:4, :].rearrange("p b (c t) -> p (b c) t", c=4)).then_inc(S["xT_d"], 1)
            settle("xT_d")
            v.wait_ge(S["xT_a"], 1)
            v.wait_ge(S["const_in"], 48)

            def ada(n):
                la, q = divmod(n, 12)
                half = q % 2
                hp = slice(64 * half, 64 * half + 64)
                v.wait_ge(S["ada_sel"], n + 1)
                tt(mod[hp, la, q // 2], PS[hp, 6, 0:16].rearrange("p (c g) -> p c g", g=G),
                   bc(b_ada[hp, la, q // 2], 2, G), ALU.add).then_inc(S["ada_mod"], 1)
                settle("ada_mod")

            def ada_lag(l, k):
                for n in ADA_AT[l][k]:
                    if n not in ada_first:
                        ada(n - 1)

            def amplify(k):
                l, w = divmod(k, 2)
                v.wait_ge(S["ada_mod"], (4, 16, 16, 24)[k])
                if k >= 2:
                    v.wait_ge(S["h_a"], NC_ * (k - 1))
                stt(amp[:, w], mod[:, l, 3 * w + 1], 1.0, bc(gains[:, 2 * w + l], 2, G), ALU.add,
                    ALU.mult).then_inc(S["amp_ready"], 1)
                settle("amp_ready")

            def norm(k):
                v.wait_ge(S["std_ready"], k + 1)
                link(v.reciprocal(small[:, 0:T], small[:, 0:T]))
                l, w = divmod(k, 2)

                def normed(c):
                    tt(xn[:, c], xT[:, c], small[:, 0:T], ALU.mult).then_inc(S["xn_ready"], 1)

                def modulated(c):
                    v.wait_ge(S["xn_ready"], NC_ * k + c + 1)
                    ts(hT[:, c, P:T], xn[:, c, P:T], amp[:, w, c, 1:2], mod[:, l, 3 * w, c, 1:2], ALU.mult,
                       ALU.add).then_inc(S["h_d"], 1)
                if k == 0:
                    for c in range(NC_):
                        normed(c)
                    v.wait_ge(S["mod_in"], mod_total)
                    for n in range(4):
                        ada(n)
                    amplify(0)
                else:
                    normed(0)
                for c in range(NC_):
                    if k > 0 and c + 1 < NC_:
                        normed(c + 1)
                    modulated(c)
                if k in ADA_NORM and ADA_NORM[k] not in ada_first:
                    ada(ADA_NORM[k] - 1)

            def lam_init_of(l):
                return 0.8 - 0.6 * math.exp(-0.3 * l)

            def prepare(l):
                lam_r = r_lam(l).rearrange("p (a b d) -> p a b d", a=2, b=2)
                prod = small[:, 400:464].rearrange("p (a d) -> p a d", a=2)
                link(tt(prod, lam_r[:, :, 0], lam_r[:, :, 1], ALU.mult))
                v.tensor_reduce(small[:, 298:300], prod, AX.X, ALU.add).then_inc(S["lam_arg"], 1)
                settle("lam_arg")
                v.wait_ge(S["decay_rate"], l + 1)
                link(ts(dec[:, l], small[:, 260:268], -1.0, None, ALU.mult))
                for k, (c, o) in enumerate((("i+1", 0), ("C-i", 4), ("C-1-i", 0), ("i", 4))):
                    link(ts(decv[:, k], dec[:, l, o:o + 4], col(c), None, ALU.mult))
                for h in range(RET_H):
                    dst = dmat[:, h % 2, h // 2]
                    link(ts(dst, C("fwd"), dec[:, l, h:h + 1], None, ALU.mult))
                    ins = stt(dst, C("bwd"), dec[:, l, 4 + h:5 + h], dst, ALU.mult, ALU.add)
                    if h < RET_H - 1:
                        link(ins)
                    else:
                        ins.then_inc(S["decay_args"], 1)
                        settle("decay_args")
                v.wait_ge(S["lam_exp"], l + 1)
                link(tt(nlam[:, l:l + 1], small[:, 301:302], small[:, 300:301], ALU.subtract))
                link(ts(nlam[:, l:l + 1], nlam[:, l:l + 1], -lam_init_of(l), None, ALU.add))

            for l in range(DEPTH):
                lam_init = lam_init_of(l)
                if l > 0:
                    amplify(2 * l)
                norm(2 * l)
                v.wait_ge(S["small_in"], small_total)
                prepare(l)
                if l == 0:
                    v.wait_ge(S["turned_x"], 3)
                    v.tensor_copy(ckT[:, :, :, :], PS[:, 4, :].rearrange("p (l c t) -> p l c t", l=2, c=2)
                                  ).then_inc(S["setup_evict_d"], 1)
                    settle("setup_evict_d")
                ada_lag(l, 0)
                for g in range(G):
                    v.wait_ge(S["rg_exp"], 2 * l + g + 1)
                    link(v.tensor_copy(v_tok[:, g], PS[:, 2 + g, 0:256]))
                    link(ts(rgate[:, g], rgate[:, g], 1.0, None, ALU.add))
                    link(v.reciprocal(rgate[:, g], rgate[:, g]))
                    tt(rgate[:, g], rgate[:, g], PS[:, 2 + g, 256:512], ALU.mult).then_inc(S["rv_ready"], 1)
                    settle("rv_ready")
                ada_lag(l, 1)
                projected(v, l, 2, 1)
                v.tensor_copy(dkT[:, :, 0:3:2, :], PS[:, 5, :].rearrange("p (c k t) -> p c k t", c=2, k=2)
                              ).then_inc(S["dk_ready"], 1)
                settle("dk_ready")
                ada_lag(l, 2)
                for g in range(G):
                    v.wait_ge(S["cq_sq"], 2 * l + g + 1)
                    link(v.reciprocal(small[:, 314:315], small[:, 306 + g:307 + g]))
                    stt(cqn[:, g], PS[:, g, 256:512], small[:, 314:315], r_qn(l), ALU.mult,
                        ALU.mult).then_inc(S["cqn_ready"], 1)
                    settle("cqn_ready")
                ada_lag(l, 3)
                v.wait_ge(S["ckv_sq"], l + 1)
                link(v.reciprocal(small[:, 316:318], small[:, 312:314]))
                for g in range(G):
                    link(stt(ckvn[:, g], PS[:, 2, 256 * g:256 * g + 128], small[:, 316 + g:317 + g], r_kvn(l),
                             ALU.mult, ALU.mult))
                v.wait_ge(S["caches_placed"], l + 1)
                v.tensor_copy(kpe[:, :, MLA_N:], PS[:, 2, :].rearrange("p (g n) -> p g n", g=G)[:, :, 128:160]
                              ).then_inc(S["ckvn_ready"], 1)
                settle("ckvn_ready")
                ada_lag(l, 4)
                v.wait_ge(S["t_kpe"], l + 1)
                v.tensor_copy(kpeT[0:MLA_QK, 0:3:2, :],
                              PS[0:MLA_QK, 5, 0:2 * P].rearrange("p (k t) -> p k t", k=2)).then_inc(S["kpeT_ready"], 1)
                settle("kpeT_ready")
                v.wait_ge(S["ret_s"], l + 1)
                v.wait_ge(S["decays_ready"], l + 1)
                for b in range(2):
                    ins = tt(sT[:, b], PS[:, b, :].rearrange("p (g m t) -> p g m t", g=G, m=2), bc(dmat[:, b], 1, G),
                             ALU.mult)
                    if b == 0:
                        link(ins)
                    else:
                        ins.then_inc(S["sT_ready"], 1)
                        settle("sT_ready")
                v.wait_ge(S["ret_x"], l + 1)
                for b in range(2):
                    ins = v.tensor_copy(cross.rearrange("p (m b) d e -> p b m (d e)", b=2)[:, b],
                                        PS[:, 2 + b, 0:256].rearrange("p (m n) -> p m n", m=2))
                    if b == 0:
                        link(ins)
                    else:
                        ins.then_inc(S["cross_ready"], 1)
                        settle("cross_ready")
                v.wait_ge(S["t_k"], l + 1)
                for d in range(2):
                    link(tt(kdec[:, d].rearrange("p (h e) -> p h e", h=4),
                            PS[:, 4, 0:256].rearrange("p (h e) -> p h e", h=4), bc(decv[:, 2 + d], 2, RET_D), ALU.mult))
                v.tensor_copy(dk_tok, PS[:, 4, 256:512]).then_inc(S["ktok_ready"], 1)
                settle("ktok_ready")

                def rope(dst_views, src, cos, sin, tmp, done):
                    link(tt(tmp, src, sin, ALU.mult))
                    link(tt(dst_views, dst_views, cos, ALU.mult))
                    tt(dst_views, dst_views, tmp, ALU.add).then_inc(done, 1)
                v.wait_ge(S["d_rot"], l + 1)
                tmp = rtmp[:, 0].rearrange("p (c t) -> p c t", c=4)
                link(tt(tmp, PS[:, 5, :].rearrange("p (c t) -> p c t", c=4), bc(C("sin_d"), 1, 4), ALU.mult))
                link(tt(dqT[:, :, P:T], dqT[:, :, P:T], bc(C("cos_d"), 1, 2), ALU.mult))
                link(tt(dqT[:, :, P:T], dqT[:, :, P:T], tmp[:, 0:2], ALU.add))
                link(tt(dkT[:, :, 2], dkT[:, :, 2], bc(C("cos_d"), 1, 2), ALU.mult))
                tt(dkT[:, :, 2], dkT[:, :, 2], tmp[:, 2:4], ALU.add).then_inc(S["d_roped"], 1)
                settle("d_roped")
                v.wait_ge(S["ret_o"], l + 1)
                ro = work.rearrange("p (g h e) -> p g h e", g=G, h=4)
                link(v.tensor_copy(ro, PS[:, 4, :].rearrange("p (g h e) -> p g h e", g=G, h=4)))
                for d in range(2):
                    tv = rtmp[:, 1, 0:256].rearrange("p (h e) -> p h e", h=4)
                    link(tt(tv, cross[:, :, d], bc(decv[:, d], 2, RET_D), ALU.mult))
                    link(tt(ro[:, 1], ro[:, 1], tv, ALU.add))
                link(tt(rtmp[:, 0], work, work, ALU.mult))
                v.tensor_reduce(small[:, 320:328], rtmp[:, 0].rearrange("p (a e) -> p a e", e=RET_D), AX.X,
                                ALU.add).then_inc(S["ret_sum"], 1)
                settle("ret_sum")
                v.wait_ge(S["kpe_rot"], l + 1)
                rp = slice(0, MLA_QK)
                tmpk = rtmp[rp, 1, 0:P]
                rope(kpeT[rp, 2], PS[rp, 0, 0:P], C("cos_m", parts=MLA_QK), C("sin_m", parts=MLA_QK), tmpk,
                     S["kpe_roped"])
                for b in range(2):
                    v.wait_ge(S["q_rot"], 2 * l + b + 1)
                    if b == 0:
                        v.wait_ge(S["kpe_roped"], l + 1)
                    else:
                        v.wait_ge(S["q_roped"], 2 * l + 1)
                    rope(qmT[rp, 4 * b:4 * b + 4, P:T], PS[rp, 1 + b, :].rearrange("p (h t) -> p h t", h=4),
                         bc(C("cos_m", parts=MLA_QK), 1, 4), bc(C("sin_m", parts=MLA_QK), 1, 4),
                         rtmp[rp, 1].rearrange("p (h t) -> p h t", h=4), S["q_roped"])
                v.wait_ge(S["ret_std"], l + 1)
                link(v.reciprocal(small[:, 328:336], small[:, 328:336]))
                link(tt(work.rearrange("p (a e) -> p a e", e=RET_D), work.rearrange("p (a e) -> p a e", e=RET_D),
                        bc(small[:, 328:336], 2, RET_D), ALU.mult))
                link(tt(mix[:, :, 0:256], work.rearrange("p (g n) -> p g n", g=G), rgate, ALU.mult))
                ada_lag(l, 5)
                for h in range(1, MLA_H, 2):
                    v.wait_ge(S["ukv_k"], MLA_H * l + h + 1)
                    v.tensor_copy(kmT[0:64, h], PS[0:64, k_bank(h), 0:3 * P].rearrange("p (k t) -> p k t", k=3)
                                  ).then_inc(S["km_d"], 1)
                    settle("km_d")
                v.tensor_copy(kmT[64:96], bc(kpeT[64:96], 1, MLA_H)).then_inc(S["km_d"], 1)
                settle("km_d")
                def negated_max(u):
                    nk = 1 + u % 2
                    scale = (DIF_D if u < 2 else MLA_QK) ** -0.5
                    v.wait_ge(S["s_ready"], 4 * l + u + 1)
                    sv = PS[:, 0:4, :].rearrange("p b (c k) -> p b c k", c=2)[:, :, :, 0:nk * P]
                    link(v.tensor_reduce(small[:, 370:378].rearrange("p (b c) -> p b c", c=2), sv, AX.X, ALU.max))
                    ts(small[:, 340:348], small[:, 370:378], -scale, None, ALU.mult).then_inc(S["nb_ready"], 1)
                    settle("nb_ready")

                def dif_heads(u):
                    return rtmp[:, u, 0:256]

                def dif_normed(u):
                    v.wait_ge(S["dif_std"], 2 * l + u + 1)
                    std = small[:, 472 + 4 * u:476 + 4 * u]
                    link(v.reciprocal(std, std))
                    o3 = dif_heads(u).rearrange("p (h e) -> p h e", h=4)
                    link(tt(o3, o3, bc(std, 2, DIF_V), ALU.mult))
                    link(stt(mix[:, u, 256:512].rearrange("p (h e) -> p h e", h=4), o3, 1.0 - lam_init,
                             bc(r_subln(l), 1, 4), ALU.mult, ALU.mult))

                negated_max(0)
                for u in range(4):
                    U = 4 * l + u
                    g, nk = u % 2, 1 + u % 2
                    ada_lag(l, 6 + u)
                    v.wait_ge(S["exp_done"], 8 * (U + 1))
                    link(v.reciprocal(small[:, 380:388], small[:, 350:358]))
                    for b in range(0, 2 * nk, 2):
                        v.wait_ge(S["pt_turned"], pt_before(U) + b + 1)
                        v.tensor_copy(pt_view(b, nk), PS[:, 4, :].rearrange("p (m t) -> p m t", m=4)
                                      ).then_inc(S["pt_even"], 1)
                        settle("pt_even")
                    if u < 3:
                        negated_max(u + 1)
                    v.wait_ge(S["pv_done"], U + 1)
                    rs = small[:, 380:388].rearrange("p (r c) -> p r c", c=2)
                    o4 = PS[:, 4, :].rearrange("p (r c e) -> p r c e", r=4, c=2)
                    if u < 2:
                        osc = work.rearrange("p (r c e) -> p r c e", r=4, c=2)
                        tt(osc, o4, bc(rs, 3, DIF_V), ALU.mult).then_inc(S["o_done"], 1)
                        settle("o_done")
                        od = dif_heads(u).rearrange("p (c r e) -> p c r e", c=2, r=2)
                        for r1 in range(2):
                            link(stt(od[:, :, r1], osc[:, 2 * r1 + 1], nlam[:, l:l + 1], osc[:, 2 * r1], ALU.mult,
                                     ALU.add))
                        link(tt(rtmp[:, u, 256:512], dif_heads(u), dif_heads(u), ALU.mult))
                        v.tensor_reduce(small[:, 464 + 4 * u:468 + 4 * u],
                                        rtmp[:, u, 256:512].rearrange("p (h e) -> p h e", h=4),
                                        AX.X, ALU.add).then_inc(S["dif_sum"], 1)
                        settle("dif_sum")
                    if u in (1, 2):
                        dif_normed(u - 1)
                    if u >= 2:
                        tt(mix[:, g, 512:1024].rearrange("p (c r e) -> p r c e", c=2, r=4), o4, bc(rs, 3, MLA_V),
                           ALU.mult).then_inc(S["o_done"], 1)
                        settle("o_done")
                for b in (1, 3):
                    v.wait_ge(S["t_mix"], 4 * l + b + 1)
                    v.tensor_copy(mixT[:, 2 * b:2 * b + 2, :], PS[:, b, :].rearrange("p (k t) -> p k t", k=2)
                                  ).then_inc(S["mixT_d"], 1)
                    settle("mixT_d")
                ada(ADA_BY[l] - 1)
                v.wait_ge(S["store_done"], 16 * stores_in_layer * (l + 1))
                v.wait_ge(S["ada_mod"], ADA_BY[l])
                for b in range(4):
                    if b < 3:
                        v.wait_ge(S["wo_done"], 3 * l + b + 1)
                    else:
                        v.wait_ge(S["weights_used"], number[("w_out", l, 1)] + 1)
                    for c in (2 * b, 2 * b + 1):
                        for g in range(G):
                            tk = slice(g * P, g * P + P)
                            ins = stt(xT[:, c, tk], PS[:, wo_bank(c), (c % 2) * T + g * P:(c % 2) * T + g * P + P],
                                      mod[:, l, 2, c, g:g + 1], xT[:, c, tk], ALU.mult, ALU.add)
                    ins.then_inc(S["x_bank"], 1)
                    settle("x_bank")
                amplify(2 * l + 1)
                norm(2 * l + 1)
                for s in range(2):
                    for g in range(G):
                        v.wait_ge(S["part_a"], 6 * l + 2 * s + g + 1)
                        r = rem[:, g].rearrange("p (c t) -> p c t", c=NC_)
                        src = PS[:, 2 * g:2 * g + 2, :].rearrange("p b (c t) -> p (b c) t", c=4) if s == 0 else r
                        if s == 1:
                            v.wait_ge(S["part_d"], 4 * l + g + 1)
                        tt(r, src, h3[:, g, s], ALU.subtract).then_inc(S["part_d"], 1)
                v.wait_ge(S["sig_exp"], l + 1)
                link(tt(selv, score, bc(r_bias(l), 1, G), ALU.add))
                for g in range(G):
                    for a in range(GROUPS):
                        last = v.max(gtop[:, g, a], selv[:, g, 8 * a:8 * a + 8])
                link(last)
                link(tt(gsc, gtop[:, :, :, 0], gtop[:, :, :, 1], ALU.add))

                def topk(src, k, n, dst):
                    for g in range(G):
                        last = v.max(top8[:, g], src[:, g])
                    link(last)
                    for g in range(G):
                        last = v.max_index(idx8[:, g], top8[:, g], src[:, g])
                    link(last)
                    link(v.tensor_copy(idxf, idx8))
                    for g in range(G):
                        hv = hit[:, 0:n * k].rearrange("p (e k) -> p e k", k=k)
                        link(tt(hv, bc(cst[:, CO["iota"]:CO["iota"] + n], 2, k), bc(idxf[:, g, 0:k], 1, n),
                                ALU.is_equal))
                        link(v.tensor_reduce(dst[:, g], hv, AX.X, ALU.max))
                topk(gsc, TOP_G, GROUPS, gmask)
                link(ts(gmask, gmask, 1.0, 1e30, ALU.subtract, ALU.mult))
                link(tt(selv.rearrange("p g (a b) -> p g a b", a=GROUPS), selv.rearrange("p g (a b) -> p g a b", a=GROUPS),
                        bc(gmask, 3, GROUPS), ALU.add))
                topk(selv, TOP_K, E, mask)
                link(tt(score, score, mask, ALU.mult))
                v.tensor_reduce(gsum[:, 0:2], score, AX.X, ALU.add).then_inc(S["routed"], 1)
                settle("routed")
                v.wait_ge(S["routed"], l + 1)
                link(v.reciprocal(gsum[:, 2:4], gsum[:, 0:2]))
                link(ts(gsum[:, 2:4], gsum[:, 2:4], ROUTED_SCALE, None, ALU.mult))
                link(tt(wgt[:, 0:E, :].rearrange("p e g -> p g e"), score, bc(gsum[:, 2:4], 2, E), ALU.mult))
                v.wait_ge(S["sh_silu"], l + 1)
                v.wait_ge(S["weights_used"], number[("shared", l, 0)] + 1)
                tt(shh, shs, PS[:, 6, :].rearrange("p (j t) -> p j t", j=2), ALU.mult).then_inc(S["sh_h"], 1)
                settle("sh_h")
                v.wait_ge(S["rank_done"], l + 1)
                link(v.tensor_reduce(fl[:, 0:1], PS[:, 4, G * E:G * E + E], AX.X, ALU.max))
                link(ts(fl[:, 1:2], fl[:, 0:1], float(CAP), None, ALU.is_gt))
                v.tensor_copy(flag_i[0:1, l:l + 1], fl[0:1, 1:2]).then_inc(S["flag_ready"], 1)
                settle("flag_ready")
                posv = pos[:, 0:E, :].rearrange("p e g -> p g e")
                link(stt(hit[:, 0:G * E].rearrange("p (g e) -> p g e", g=G),
                         PS[:, 4, 0:G * E].rearrange("p (g e) -> p g e", g=G), 1.0, mask, ALU.add, ALU.mult))
                ts(posv, hit[:, 0:G * E].rearrange("p (g e) -> p g e", g=G), -1.0, None, ALU.add
                   ).then_inc(S["pos_ready"], 1)
                settle("pos_ready")
                g0, s0_ = (PAIRS + 1) * l, (PAIRS + 2) * l
                iota2 = bc(bc(cst[:, CO["iota"]:CO["iota"] + CAP], 1, 2), 1, G)

                def pair_of(x, at):
                    return bc(x.rearrange("p e g -> p (e g)")[:, at].rearrange("p (e g) -> p g e", g=G), 3, CAP)

                def one_hot(b, at):
                    return tt(onehot[b].rearrange("p g (e s) -> p g e s", e=2), iota2, pair_of(pos, at), ALU.is_equal)

                def gate_it(b, at):
                    return tt(gated.rearrange("p g (e s) -> p g e s", e=2),
                              onehot[b].rearrange("p g (e s) -> p g e s", e=2), pair_of(wgt, at), ALU.mult)

                def turned_out():
                    v.tensor_copy(slot_gate, PS[:, 5, 0:2])
                    v.tensor_copy(hidT, PS[:, 6, 0:256])
                    return v.tensor_copy(selT, PS[:, 6, 256:512])

                def remainder(n):
                    half = slice(512 * n, 512 * n + 512)
                    return tt(yy[:, half], yy[:, half], ypart[0][:, half], ALU.subtract)

                def third_part(n):
                    half = slice(512 * n, 512 * n + 512)
                    return tt(ypart[2][:, half], yy[:, half], ypart[1][:, half], ALU.subtract)
                v.wait_ge(S["pos_ready"], l + 1)
                v.wait_ge(S["zeroed"], l + 2)
                one_hot(0, slice(0, 4)).then_inc(S["sel_ready"], 1)
                v.wait_ge(S["sel_ready"], s0_ + 1)
                gate_it(0, slice(0, 4)).then_inc(S["gated_ready"], 1)
                one_hot(1, slice(4, 8)).then_inc(S["sel_ready"], 1)
                v.wait_ge(S["gathered"], 2 * g0 + 2)
                v.tensor_copy(xg[:, 4:8], PS[:, 4, :].rearrange("p (c t) -> p c t", c=4)).then_inc(S["xg_b"], 1)
                with v.Fori(0, PAIRS // 2) as m:
                    for q in range(2):
                        v.wait_ge(S["silu_ready"], m * 2 + (PAIRS * l + q + 1))
                        tt(hh, sact, PS[:, 5, FF:2 * FF], ALU.mult).then_inc(S["hid_ready"], 1)
                        v.wait_ge(S["turned"], m * 2 + (PAIRS * l + q + 1))
                        turned_out().then_inc(S["turn_out"], 1)
                        v.wait_ge(S["sel_ready"], m * 2 + (s0_ + q + 2))
                        gate_it(1 - q, bass.ds(m * 8 + 4 * (q + 1), 4)).then_inc(S["gated_ready"], 1)
                        one_hot(q, bass.ds(m * 8 + 4 * (q + 2), 4)).then_inc(S["sel_ready"], 1)
                        v.wait_ge(S["gathered"], m * 4 + (2 * (g0 + q + 1) + 2))
                        v.tensor_copy(xg[:, 4:8], PS[:, 4, :].rearrange("p (c t) -> p c t", c=4)).then_inc(S["xg_b"], 1)
                        for n in range(2):
                            v.wait_ge(S["parts_act"], m * 8 + (4 * (PAIRS * l + q) + n + 1))
                            remainder(n).then_inc(S["parts_dve"], 1)
                        for n in range(2):
                            v.wait_ge(S["parts_act"], m * 8 + (4 * (PAIRS * l + q) + n + 3))
                            third_part(n).then_inc(S["parts_dve"], 1)
                o = ov[l]
                with v.If(over_flag(v, l) > 0):
                    with v.Fori(0, E) as e:
                        for w in range(OW):
                            v.wait_ge(o["comb"], e * OW + (w + BEFORE))
                            p_ap = pos.rearrange("p e g -> p (e g)")[:, bass.ds(e * 2, 2)]
                            w_ap = wgt.rearrange("p e g -> p (e g)")[:, bass.ds(e * 2, 2)]
                            ts(fl[:, 0:2], p_ap, float(-(CAP + P * w)), None, ALU.add).then_inc(o["sel"], 1)
                            v.wait_ge(o["sel"], e * (3 * OW) + (3 * w + 1))
                            tt(onehot[0], bc(C("iota"), 1, G), bc(fl[:, 0:2], 2, P), ALU.is_equal).then_inc(o["sel"], 1)
                            v.wait_ge(o["sel"], e * (3 * OW) + (3 * w + 2))
                            tt(gated, onehot[0], bc(w_ap, 2, P), ALU.mult).then_inc(o["sel"], 1)
                            v.wait_ge(o["gath"], e * (2 * OW) + (2 * w + 2))
                            v.tensor_copy(xg[:, 4:8], PS[:, 4, :].rearrange("p (c t) -> p c t", c=4)).then_inc(o["xg"], 1)
                            v.wait_ge(o["silu"], e * OW + (w + 1))
                            tt(hh, sact, PS[:, 5, FF:2 * FF], ALU.mult).then_inc(o["hid"], 1)
                            v.wait_ge(o["turn"], e * OW + (w + 1))
                            turned_out().then_inc(o["out"], 1)
                            for n in range(2):
                                v.wait_ge(o["parts_act"], e * (4 * OW) + (4 * w + n + 1))
                                remainder(n).then_inc(o["parts_dve"], 1)
                            for n in range(2):
                                v.wait_ge(o["parts_act"], e * (4 * OW) + (4 * w + n + 3))
                                third_part(n).then_inc(o["parts_dve"], 1)
                v.wait_ge(S["combined"], l + 1)
                for c in range(NC_):
                    for g in range(G):
                        tk = slice(g * P, g * P + P)
                        ins = stt(xT[:, c, tk], PS[:, c // 2, (c % 2) * T + g * P:(c % 2) * T + g * P + P],
                                  mod[:, l, 5, c, g:g + 1], xT[:, c, tk], ALU.mult, ALU.add)
                    if c % 2:
                        ins.then_inc(S["x_bank"], 1)
                        settle("x_bank")
            v.wait_ge(S["y_sq"], 4)
            tt(small[:, 4:6], small[:, 0:4:2], small[:, 1:4:2], ALU.add).then_inc(S["y_ms"], 1)
            v.wait_ge(S["y_std"], 1)
            link(v.reciprocal(small[:, 6:8], small[:, 6:8]))
            v.wait_ge(S["gain_in"], 16)
            y_tok = arena[:, 0:G * D].rearrange("p (g n) -> p g n", g=G)
            for g in range(G):
                stt(y_tok[:, g].rearrange("p (t c) -> p c t", c=NC_),
                    PS[:, 4 + 2 * g:6 + 2 * g, :].rearrange("p b (c t) -> p (b c) t", c=4), small[:, 6 + g:7 + g],
                    rem[:, 0].rearrange("p (t c) -> p c t", c=NC_), ALU.mult, ALU.mult).then_inc(S["y_done"], 1)

        @block.tensor
        def _(pe):
            mmul = pe.matmul

            def turn(dst, src, parts=P):
                return pe.transpose(dst, src, ident[0:parts, 0:parts])

            pe.wait_ge(S["const_in"], 48)
            x_tok = arena[:, 0:G * D].rearrange("p (g n) -> p g n", g=G)
            for g in range(G):
                for c in range(NC_):
                    ins = turn(PS[:, 2 * g + c // 4, (c % 4) * P:(c % 4) * P + P],
                               x_tok[:, g].rearrange("p (t c) -> p c t", c=NC_)[:, c])
                ins.then_inc(S["turned_x"], 1)

            def turn_caches():
                pe.wait_ge(S["small_in"], small_total)
                for l in range(DEPTH):
                    for c in range(2):
                        ins = turn(PS[:, 4, (2 * l + c) * P:(2 * l + c + 1) * P],
                                   ck[:, l, 2 * c:2 * c + 2].rearrange("p h d -> p (h d)"))
                ins.then_inc(S["turned_x"], 1)
                for l in range(DEPTH):
                    turn(PS[:, 5, l * P:l * P + P], cl[:, l])
                for l in range(DEPTH):
                    ins = turn(PS[0:MLA_QK, 5, (2 + l) * P:(3 + l) * P], cr[:, l])
                ins.then_inc(S["turned_x"], 1)

            def piece(it):
                n = number[it]
                pe.wait_ge(gu_loaded[n % RING], loaded_at[it])
                return gu[:, n % RING, :]

            def ada_select(n):
                half = (n % 12) % 2
                pe.wait_ge(S["ada_r"], n + 1)
                if n >= 1:
                    pe.wait_ge(S["ada_mod"], n)
                for c in range(NC_):
                    ins = mmul(PS[64 * half:64 * half + 64, 6, 2 * c:2 * c + 2],
                               rada[:, :].rearrange("p (t c) -> p c t", c=NC_)[:, c], col("sel", 2), start=True, stop=True)
                ins.then_inc(S["ada_sel"], 1)

            def ada(n, flush=False, norm=None):
                w = piece(items_ada[n])
                if n >= 1:
                    pe.wait_ge(S["ada_r"], n)
                wv = w.rearrange("p (c n) -> p c n", c=NC_)
                for kk in range(2):
                    for j in range(4):
                        k = 2 * j + kk
                        ins = mmul(PS[32 * j:32 * j + 32, 7, :], condw[:, k, :], wv[:, k], start=(kk == 0), stop=(kk == 1))
                ins.then_inc(S["weights_used"], 1)
                if n not in ada_first:
                    if norm is not None:
                        pe.wait_ge(S["std_ready"], norm + 1)
                    ada_select(n - 1)
                if flush:
                    ada_select(n)

            def norm(k):
                for c in range(NC_):
                    if c % 2 == 0:
                        pe.wait_ge(S["sq_ready"], 4 * k + c // 2 + 1)
                    ins = mmul(PS[:, 6, 0:T], C("ones"), hT[:, c], start=(c == 0), stop=(c == NC_ - 1))
                ins.then_inc(S["ss_ready"], 1)
                if k in ADA_NORM:
                    ada(ADA_NORM[k], norm=k)

            def project(bank, o, lhs, rhs, fresh=None):
                for k in range(NC_):
                    if fresh is not None:
                        pe.wait_ge(S["h_a"], NC_ * fresh + k + 1)
                        pe.wait_ge(S["h_d"], NC_ * fresh + k + 1)
                    ins = mmul(PS[0:lhs(k).shape[-1], bank, o:o + rhs(k).shape[-1]], lhs(k), rhs(k), start=(k == 0),
                               stop=(k == NC_ - 1))
                return ins

            for l in range(DEPTH):
                norm(2 * l)
                if l == 0:
                    pe.wait_ge(S["cond_ready"], 1)
                    pe.wait_ge(S["std_ready"], 1)
                    for n in range(4):
                        ada(n, flush=(n == 3))

                def tok(g):
                    return lambda k: hT[:, k, g * P:g * P + P]

                def wcol(w, a, n, width=512):
                    wv = w[:, 0:NC_ * width].rearrange("p (c n) -> p c n", c=NC_)
                    return lambda k: wv[:, k, a:a + n]

                def all_tok(k):
                    return hT[:, k, :]
                w = piece(("w_in", l, 0))
                for b in range(2):
                    for c in range(2):
                        ins = project(b, c * T, wcol(w, 256 * b + 128 * c, 128), all_tok,
                                      fresh=2 * l if b + c == 0 else None)
                    if b == 0:
                        ins.then_inc(S["proj"], 1)
                    else:
                        ins.then_inc(S["weights_used"], 1)
                if l == 0:
                    turn_caches()
                ada_here(ada, l, 0)
                w = piece(("w_in", l, 1))
                for g in range(G):
                    ins = project(2 + g, 0, tok(g), wcol(w, 0, 512))
                    if g == 0:
                        ins.then_inc(S["proj"], 1)
                    else:
                        ins.then_inc(S["weights_used"], 1)
                ada_here(ada, l, 1)
                w = piece(("w_in", l, 2))
                if l == 0:
                    pe.wait_ge(S["setup_evict_a"], 1)
                    pe.wait_ge(S["setup_evict_d"], 1)
                for b in range(2):
                    for c in range(2):
                        ins = project(4 + b, c * T, wcol(w, 256 * b + 128 * c, 128), all_tok)
                    if b == 0:
                        ins.then_inc(S["proj"], 1)
                    else:
                        ins.then_inc(S["weights_used"], 1)
                ada_here(ada, l, 2)
                w = piece(("w_in", l, 3))
                pe.wait_ge(S["q_ready"], l + 1)
                pe.wait_ge(S["k_ready"], l + 1)
                for g in range(G):
                    ins = project(g, 0, tok(g), wcol(w, 0, 512))
                    if g == 0:
                        ins.then_inc(S["proj"], 1)
                    else:
                        ins.then_inc(S["weights_used"], 1)
                ada_here(ada, l, 3)
                w = piece(("w_in", l, 4))
                pe.wait_ge(S["rv_ready"], 2 * l + 1)
                for g in range(G):
                    ins = project(2, 256 * g, tok(g), wcol(w, 0, 160, 160))
                ins.then_inc(S["weights_used"], 1)
                ada_here(ada, l, 4)
                pe.wait_ge(S["cqn_ready"], 2 * l + 2)
                pe.wait_ge(S["rv_ready"], 2 * l + 2)
                for k in range(2):
                    for g in range(G):
                        ins = turn(PS[:, 3, (2 * k + g) * P:(2 * k + g + 1) * P], cqn[:, g, k * P:k * P + P])
                ins.then_inc(S["t_cq"], 1)
                pe.wait_ge(S["ckvn_ready"], l + 1)
                pe.wait_ge(S["dq_ready"], l + 1)
                for g in range(G):
                    ins = turn(PS[:, 4, g * P:g * P + P], ckvn[:, g])
                ins.then_inc(S["t_ckv"], 1)
                pe.wait_ge(S["dk_ready"], l + 1)
                for g in range(G):
                    ins = turn(PS[0:MLA_QK, 5, g * P:g * P + P], kpe[:, g])
                ins.then_inc(S["t_kpe"], 1)
                for g in range(G):
                    for m in range(2):
                        for b in range(2):
                            hp = slice(64 * b, 64 * b + 64)
                            ins = mmul(PS[:, b, (2 * g + m) * P:(2 * g + m + 1) * P], kT[hp, m, g * P:g * P + P],
                                       qT[hp, m, g * P:g * P + P], start=True, stop=True)
                ins.then_inc(S["ret_s"], 1)
                pe.wait_ge(S["cqT_ready"], l + 1)
                for m in range(2):
                    for b in range(2):
                        hp = slice(64 * b, 64 * b + 64)
                        ins = mmul(PS[:, 2 + b, m * P:m * P + P], qT[hp, m, P:T],
                                   s0[hp, l, m].rearrange("p d e -> p (d e)"), start=True, stop=True)
                ins.then_inc(S["ret_x"], 1)
                pe.wait_ge(S["ckvT_ready"], l + 1)
                for c in range(2):
                    turn(PS[:, 4, c * P:c * P + P], kT[:, c, 0:P])
                for c in range(2):
                    ins = turn(PS[:, 4, (2 + c) * P:(3 + c) * P], dkT[:, c, 0])
                ins.then_inc(S["t_k"], 1)
                pe.wait_ge(S["kpeT_ready"], l + 1)
                mmul(PS[:, 5, 0:256], C("rot_d"), dqT[:, :, P:T], start=True, stop=True)
                mmul(PS[:, 5, 256:512], C("rot_d"), dkT[:, :, 2], start=True, stop=True).then_inc(S["d_rot"], 1)
                w = piece(("mla", l, 0))
                w_uq = w[:, 0:UQ].rearrange("p (k n) -> p k n", k=2)
                w_ukv = w[:, UQ:UQ + UKV]
                for h in range(MLA_H):
                    if h == 0:
                        pe.wait_ge(S["sT_ready"], l + 1)
                    if h == 4:
                        pe.wait_ge(S["cross_ready"], l + 1)
                    for k in range(2):
                        ins = mmul(PS[0:MLA_QK, h // 2, (h % 2) * T:(h % 2) * T + T],
                                   w_uq[:, k, MLA_QK * h:MLA_QK * h + MLA_QK], cqT[:, k], start=(k == 0), stop=(k == 1))
                    if h % 2:
                        ins.then_inc(S["uq"], 1)
                pe.wait_ge(S["ktok_ready"], l + 1)
                for g in range(G):
                    for h in range(RET_H):
                        ins = mmul(PS[:, 4, (4 * g + h) * 64:(4 * g + h + 1) * 64], sT[:, h % 2, g, h // 2],
                                   v_tok[:, g, 64 * h:64 * h + 64], start=True, stop=True)
                ins.then_inc(S["ret_o"], 1)
                pe.wait_ge(S["d_roped"], l + 1)
                for d in range(2):
                    for h in range(RET_H):
                        ins = mmul(PS[0:64, 5, (4 * d + h) * 64:(4 * d + h + 1) * 64], kdec[:, d, 64 * h:64 * h + 64],
                                   v_tok[:, 0, 64 * h:64 * h + 64], start=True, stop=True)
                ins.then_inc(S["kv_p"], 1)
                pe.wait_ge(S["qm_ready"], 4 * l + 4)
                rm = cst[0:MLA_QK, CO["rot_m"]:CO["rot_m"] + MLA_QK]
                mmul(PS[0:MLA_QK, 0, 0:P], rm, kpeT[0:MLA_QK, 2], start=True, stop=True).then_inc(S["kpe_rot"], 1)
                for b in range(2):
                    mmul(PS[0:MLA_QK, 1 + b, :], rm, qmT[0:MLA_QK, 4 * b:4 * b + 4, P:T], start=True,
                         stop=True).then_inc(S["q_rot"], 1)
                ada_here(ada, l, 5)
                for h in range(MLA_H):
                    if h == 1:
                        pe.wait_ge(S["ret_sum"], l + 1)
                    if h == 2:
                        pe.wait_ge(S["kv_ready"], l + 1)
                    if h == 3:
                        pe.wait_ge(S["kpe_roped"], l + 1)
                    if h in (4, 5):
                        pe.wait_ge(S["q_roped"], 2 * l + h - 3)
                    if h == 6:
                        pe.wait_ge(S["km_a"], 4 * l + 1)
                    if h == 7:
                        pe.wait_ge(S["km_d"], 5 * l + 1)
                    mmul(PS[0:64, k_bank(h), 0:3 * P], w_ukv[:, 128 * h:128 * h + 64],
                         ckvT.rearrange("p k t -> p (k t)"), start=True, stop=True).then_inc(S["ukv_k"], 1)
                wv = w_ukv.rearrange("p (h n) -> p h n", h=MLA_H)[:, :, MLA_N:]
                for k in range(3):
                    if k == 0:
                        pe.wait_ge(S["km_a"], 4 * l + 2)
                    if k == 1:
                        pe.wait_ge(S["km_d"], 5 * l + 2)
                    if k == 2:
                        pe.wait_ge(S["km_a"], 4 * l + 3)
                    mmul(PS[:, (5, 0, 1)[k], :], ckvT[:, k], wv, start=True, stop=True
                         ).then_inc(S["weights_used"] if k == 2 else S["ukv_v"], 1)
                pe.wait_ge(S["vm_ready"], 3 * l + 3)
                pe.wait_ge(S["km_a"], 4 * l + 4)
                pe.wait_ge(S["km_d"], 5 * l + 5)
                def scores(u):
                    U = 4 * l + u
                    g, nk = u % 2, 1 + u % 2
                    ks = slice(0, 1) if g == 0 else slice(1, 3)
                    if u > 0:
                        pe.wait_ge(S["exp_done"], 8 * U)
                    for c in range(2):
                        for r in range(4):
                            dst = PS[:, r, c * 256:c * 256 + nk * P]
                            if u < 2:
                                rp = slice(32 * r, 32 * r + 32)
                                ins = mmul(dst, dqT[rp, c, g * P:g * P + P],
                                           dkT[rp, c, ks].rearrange("p k t -> p (k t)"), start=True, stop=True)
                            else:
                                h = 4 * c + r
                                ins = mmul(dst, qmT[0:MLA_QK, h, g * P:g * P + P],
                                           kmT[0:MLA_QK, h, ks].rearrange("p k t -> p (k t)"), start=True, stop=True)
                    ins.then_inc(S["s_ready"], 1)

                scores(0)
                for u in range(4):
                    U = 4 * l + u
                    g, nk = u % 2, 1 + u % 2
                    ada_here(ada, l, 6 + u)
                    if u > 0:
                        pe.wait_ge(S["o_done"], U)
                    for b in range(2 * nk):
                        if b >= 2:
                            pe.wait_ge(S["pt_even" if b % 2 == 0 else "pt_odd"], half_before(U) + b // 2)
                        for j in range(4):
                            m, k = divmod(4 * b + j, nk)
                            if j == 0:
                                pe.wait_ge(S["exp_done"], 8 * U + (4 * b + 3) // nk + 1)
                            ins = turn(PS[:, 4 + b % 2, j * P:j * P + P], prob[:, m, k * P:k * P + P])
                        ins.then_inc(S["pt_turned"], 1)
                    if u < 3:
                        scores(u + 1)
                    pe.wait_ge(S["pt_even"], half_before(U) + nk)
                    pe.wait_ge(S["pt_odd"], half_before(U) + nk)
                    for m in range(8):
                        r, c = divmod(m, 2)
                        for k in range(nk):
                            if u < 2:
                                h = 2 * c + r // 2
                                vv = (dv_tok[:, 0, 64 * h:64 * h + 64] if g == 0 else
                                      cv[:, l, h] if k == 0 else dv_tok[:, 1, 64 * h:64 * h + 64])
                            else:
                                h = 4 * c + r
                                vv = vm[:, k + g, 64 * h:64 * h + 64]
                            ins = mmul(PS[:, 4, m * 64:m * 64 + 64], probT[:, m, k, :], vv, start=(k == 0),
                                       stop=(k == nk - 1))
                    ins.then_inc(S["pv_done"], 1)
                pe.wait_ge(S["o_done"], 4 * l + 4)
                for k in range(NC_):
                    for g in range(G):
                        ins = turn(PS[:, k // 2, ((k % 2) * 2 + g) * P:((k % 2) * 2 + g + 1) * P],
                                   mix[:, g, k * P:k * P + P])
                    if k % 2:
                        ins.then_inc(S["t_mix"], 1)
                ada_select(ADA_BY[l] - 1)
                pe.wait_ge(S["mixT_a"], 2 * l + 2)
                pe.wait_ge(S["mixT_d"], 2 * l + 2)
                wo = [piece(("w_out", l, i)).rearrange("p (k t c) -> p k c t", k=4, c=NC_) for i in range(2)]
                for c in range(NC_):
                    for k in range(NC_):
                        ins = mmul(PS[:, wo_bank(c), (c % 2) * T:(c % 2) * T + T], wo[k // 4][:, k % 4, c], mixT[:, k],
                                   start=(k == 0), stop=(k == NC_ - 1))
                        if c == NC_ - 1 and k == 3:
                            ins.then_inc(S["weights_used"], 1)
                    if c == NC_ - 1:
                        ins.then_inc(S["weights_used"], 1)
                    elif c % 2:
                        ins.then_inc(S["wo_done"], 1)
                norm(2 * l + 1)
                for g in range(G):
                    for c in range(NC_):
                        if g == 0:
                            pe.wait_ge(S["h_a"], NC_ * (2 * l + 1) + c + 1)
                        else:
                            pe.wait_ge(S["h_d"], NC_ * (2 * l + 1) + c + 1)
                        ins = turn(PS[:, 2 * g + c // 4, (c % 4) * P:(c % 4) * P + P], hT[:, c, g * P:g * P + P])
                    ins.then_inc(S["t_h"], 1)
                pe.wait_ge(S["router_in"], 16 * (l + 1))
                for g in range(G):
                    ins = project(4, g * E, tok(g), lambda k: w_rt[:, k * E:k * E + E])
                ins.then_inc(S["router_done"], 1)
                w = piece(("shared", l, 0)).rearrange("p (u k t j) -> p u k j t", u=2, k=NC_, j=2)
                pe.wait_ge(S["std_ready"], 2 * l + 2)
                for u in range(2):
                    for j in range(2):
                        ins = project(5 + u, j * T, lambda k: w[:, u, k, j], all_tok)
                    ins.then_inc(S["sh_gate"] if u == 0 else S["weights_used"], 1)
                pe.wait_ge(S["routed"], l + 1)
                mmul(PS[:, 4, 0:E], C("before"), mask[:, 0], start=True, stop=True)
                mmul(PS[:, 4, E:2 * E], C("ones"), mask[:, 0], start=True, stop=False)
                mmul(PS[:, 4, E:2 * E], C("before"), mask[:, 1], start=False, stop=True)
                mmul(PS[:, 4, 2 * E:3 * E], C("ones"), mask[:, 0], start=True, stop=False)
                mmul(PS[:, 4, 2 * E:3 * E], C("ones"), mask[:, 1], start=False, stop=True).then_inc(S["rank_done"], 1)
                pe.wait_ge(dn_loaded[RING - 1], dloaded[("shared", l, 0)])
                pe.wait_ge(S["sh_h"], l + 1)
                pe.wait_ge(S["part_a"], 6 * l + 6)
                wd = dn[:, RING - 1].rearrange("p j (t c) -> p j c t", c=NC_)

                def shared_down(half):
                    for c in range(4 * half, 4 * half + 4):
                        for j in range(2):
                            ins = mmul(PS[:, c // 2, (c % 2) * T:(c % 2) * T + T], wd[:, j, c], shh[:, j],
                                       start=(j == 0 and c % 2 == 0), stop=False, skip_group_check=True)
                    return ins
                shared_down(0)

                g0 = (PAIRS + 1) * l

                def gather(b, half):
                    for c in range(4 * half, 4 * half + 4):
                        for g in range(G):
                            for s in range(3):
                                ins = mmul(PS[:, 4, (c % 4) * P:(c % 4) * P + P], h3[:, g, s, c], onehot[b][:, g],
                                           start=(g == 0 and s == 0), stop=(g == 1 and s == 2))
                    return ins

                def scatter():
                    for c in range(NC_):
                        for y in ypart:
                            part = y.rearrange("p (t c) -> p c t", c=NC_)[:, c]
                            ins = mmul(PS[:, c // 2, (c % 2) * T:(c % 2) * T + T], part, selT, start=False, stop=False,
                                       skip_group_check=True)
                    return ins

                def turn_pair(b):
                    for j in range(2):
                        turn(PS[:, 6, j * P:j * P + P], hh.rearrange("p (t j) -> p j t", j=2)[:, j])
                    for g in range(G):
                        mmul(PS[:, 6, (2 + g) * P:(3 + g) * P], onehot[b][:, g], identb, start=True, stop=True)
                    for g in range(G):
                        ins = mmul(PS[:, 5, 0:2], gated[:, g], C("ones", 2), start=(g == 0), stop=(g == 1))
                    return ins

                pe.wait_ge(S["pos_ready"], l + 1)
                pe.wait_ge(S["sel_ready"], (PAIRS + 2) * l + 1)
                gather(0, 0).then_inc(S["gathered"], 1)
                shared_down(1).then_inc(S["down_free"], 1)
                pe.wait_ge(S["xg_a"], g0 + 1)
                gather(0, 1).then_inc(S["gathered"], 1)

                def pair(m, q, early=False):
                    pe.wait_ge(S["xg_b"], m * 2 + (g0 + q + 1))
                    pe.wait_ge(S["xg_a"], m * 2 + (g0 + q + 1))
                    pe.wait_ge(S["hid_ready"], m * 2 + (PAIRS * l + q + BEFORE))
                    for h in range(1 if early else 2):
                        pe.wait_ge(gu_loaded[gu_slot(l, 2 * q + h)], m * 32 + loaded_at[("expert", l, 2 * q + h)])
                    if early:
                        pe.wait_ge(S["early_in"], 48 * l + 32)
                    guv = [gu[:, gu_slot(l, 2 * q + h), :].rearrange("p (u k n) -> p k u n", u=2, k=NC_) for h in range(2)]
                    for k in range(NC_):
                        for h in range(2):
                            lhs, st = xg[:, k, 64 * h:64 * h + 64], dict(start=(k == 0), stop=(k == NC_ - 1))
                            if early and h == 1:
                                for u, half in enumerate((early_gate, early_up)):
                                    ins = mmul(PS[64:128, 5, u * FF:(u + 1) * FF], lhs, half[:, k * FF:(k + 1) * FF],
                                               start=(k == 0 and u == 0), stop=(k == NC_ - 1 and u == 1),
                                               skip_group_check=True)
                            else:
                                ins = mmul(PS[64 * h:64 * h + 64, 5, :], lhs, guv[h][:, k], **st)
                            if k == NC_ - 1:
                                ins.then_inc(S["weights_used"], 1)
                    pe.wait_ge(S["sel_ready"], m * 2 + ((PAIRS + 2) * l + q + 2))
                    gather(1 - q, 0).then_inc(S["gathered"], 1)
                    pe.wait_ge(S["parts_dve"], m * 8 + (4 * (PAIRS * l + q) + BEFORE))
                    if q == 0:
                        pe.wait_ge(S["zeroed"], l + 2)
                    scatter()
                    pe.wait_ge(S["hid_ready"], m * 2 + (PAIRS * l + q + 1 + BEFORE))
                    pe.wait_ge(S["gated_ready"], m * 2 + (g0 + q + 1))
                    turn_pair(q).then_inc(S["turned"], 1)
                    pe.wait_ge(S["xg_a"], m * 2 + (g0 + q + 2))
                    gather(1 - q, 1).then_inc(S["gathered"], 1)
                    pe.wait_ge(S["turn_out"], m * 2 + (PAIRS * l + q + 1))
                    for h in range(1 if early else 2):
                        slot = 2 * q + h
                        pe.wait_ge(dn_loaded[slot], m * 16 + dloaded[("expert", l, slot)])
                    if early:
                        pe.wait_ge(S["early_in"], 48 * (l + 1))
                    dnv = [dn[:, 2 * q], early_down.rearrange("p (j n) -> p j n", j=2) if early else dn[:, 2 * q + 1]]
                    for n in range(2):
                        for j in range(2):
                            for h in range(2):
                                ins = mmul(PS[64 * h:64 * h + 64, 7 - n, :], hidT[:, j * P + 64 * h:j * P + 64 * h + 64],
                                           dnv[h][:, j, 512 * n:512 * n + 512], start=(j == 0), stop=(j == 1))
                                if n == 0 and j == 1 and h == 1:
                                    ins.then_inc(S["down_a"], 1)
                                if n == 1 and j == 1:
                                    ins.then_inc(S["down_free"], 1)

                last = E // RING - 1
                with pe.Fori(0, last) as m:
                    for q in range(2):
                        pair(m, q)
                pair(last, 0, early=True)
                pair(last, 1)
                pe.wait_ge(S["parts_dve"], 4 * PAIRS * (l + 1) + BEFORE)
                scatter()
                o = ov[l]
                pe.wait_ge(S["xg_b"], (PAIRS + 1) * (l + 1))
                with pe.If(over_flag(pe, l) > 0):
                    with pe.Fori(0, E) as e:
                        for w in range(OW):
                            pe.wait_ge(o["sel"], e * (3 * OW) + (3 * w + 3))
                            pe.wait_ge(o["xg"], e * (2 * OW) + (2 * w + BEFORE))
                            gather(0, 0).then_inc(o["gath"], 1)
                            pe.wait_ge(o["xg"], e * (2 * OW) + (2 * w + 1 + BEFORE))
                            gather(0, 1).then_inc(o["gath"], 1)
                            pe.wait_ge(o["xg"], e * (2 * OW) + (2 * w + 2 + BEFORE))
                            pe.wait_ge(o["hid"], e * OW + (w + BEFORE))
                            pe.wait_ge(o["w"], e * 48 + 48)
                            guv = gu[:, 0, :].rearrange("p (u k n) -> p k u n", u=2, k=NC_)
                            for k in range(NC_):
                                ins = mmul(PS[:, 5, :], xg[:, k], guv[:, k], start=(k == 0), stop=(k == NC_ - 1))
                            ins.then_inc(o["up"], 1)
                            pe.wait_ge(o["hid"], e * OW + (w + 1 + BEFORE))
                            pe.wait_ge(o["parts_dve"], e * (4 * OW) + (4 * w + BEFORE))
                            turn_pair(0).then_inc(o["turn"], 1)
                            pe.wait_ge(o["out"], e * OW + (w + 1))
                            for n in range(2):
                                for j in range(2):
                                    ins = mmul(PS[:, 7 - n, :], hidT[:, j * P:j * P + P],
                                               dn[:, 0, j, 512 * n:512 * n + 512], start=(j == 0), stop=(j == 1))
                                ins.then_inc(o["down"], 1)
                            pe.wait_ge(o["parts_dve"], e * (4 * OW) + (4 * w + 4 + BEFORE))
                            scatter().then_inc(o["comb"], 1)
                mmul(PS[:, 6, 0:2], ident, col("sel", 2), start=True, stop=True).then_inc(S["combined"], 1)
            for g in range(G):
                for c in range(NC_):
                    if g == 0 and c % 2 == 0:
                        pe.wait_ge(S["x_bank"], x_banks(2 * DEPTH - 1) + c // 2 + 1)
                    ins = turn(PS[:, 4 + 2 * g + c // 4, (c % 4) * P:(c % 4) * P + P], xT[:, c, g * P:g * P + P])
                    if c % 4 == 3:
                        ins.then_inc(S["turned_y"], 1)


_OUTS = [("y_prompt", (1, P, D)), ("y_sample", (1, P, D)), ("diff_k", (1, DEPTH, DIF_H, P, 2 * DIF_D)),
         ("diff_v", (1, DEPTH, DIF_H, P, DIF_V)), ("mla_ckv", (1, DEPTH, P, KV_LORA)),
         ("mla_kpe", (1, DEPTH, P, MLA_R)), ("ret_fwd", (1, DEPTH, RET_H, RET_D, RET_D)),
         ("ret_bwd", (1, DEPTH, RET_H, RET_D, RET_D))]


def kernel(**inputs):
    import concourse.bacc as bacc
    from concourse.bass_utils import run_bass_kernel_spmd

    nc = bacc.Bacc("TRN2", target_bir_lowering=False, num_devices=1)
    arrays, t, out = {}, {}, {}
    for name, value in [*inputs.items(), ("shape_consts", shape_constants())]:
        a = np.ascontiguousarray(value)
        arrays[f"in_{name}"] = a
        t[name] = nc.dram_tensor(f"in_{name}", a.shape, mybir.dt.from_np(a.dtype), kind="ExternalInput").ap()
    for name, shape in _OUTS:
        out[name] = nc.dram_tensor(f"out_{name}", shape, F32, kind="ExternalOutput").ap()
    trunk(nc, t, out)
    r = run_bass_kernel_spmd(nc, [arrays], core_ids=[0])
    return tuple(r.results[0][f"out_{name}"] for name, _ in _OUTS)
```
